# Optimizing a Trainium2 kernel written in Bass

```python
import math
import jax
import jax.numpy as jnp
from jax import lax
import numpy as np

D_MODEL = 1024
BATCH = 1
SEQ = 2048
DEPTH = 2

GRID_W = 64
CTX_LEN = 256
HEAD_DIM = 64
ROPE_BASE = 10000.0
LN_EPS = 1e-5

A_HEADS = D_MODEL // 256
A_KV_HEADS = A_HEADS // 2
A_GROUP = A_HEADS // A_KV_HEADS
A_WIDTH = A_HEADS * HEAD_DIM
A_KV_WIDTH = A_KV_HEADS * HEAD_DIM
WINDOW = 128

B_HEADS = 3 * D_MODEL // 512
B_QK_DIM = 32
B_V_DIM = 2 * B_QK_DIM
B_QK_WIDTH = B_HEADS * 2 * B_QK_DIM
B_WIDTH = B_HEADS * B_V_DIM
Q_BLOCK = 128

C_HEADS = 3 * D_MODEL // 512
C_WIDTH = C_HEADS * HEAD_DIM
C_GATE_WIDTH = 2 * 2 * C_HEADS
CHUNK = 64

D_MIX = A_WIDTH + B_WIDTH + C_WIDTH
D_IN = 2 * A_WIDTH + 2 * A_KV_WIDTH + 2 * B_QK_WIDTH + 2 * B_WIDTH + 5 * C_WIDTH + C_GATE_WIDTH

ALPHA = (2 * DEPTH) ** 0.25
BETA = (8 * DEPTH) ** -0.25

kernel_name = "hymba_style_diffusion_hybrid_block"

def layer_norm(x, g, b):
    xf = x.astype(jnp.float32)
    mu = xf.mean(-1, keepdims=True)
    var = jnp.mean(jnp.square(xf - mu), -1, keepdims=True)
    y = (xf - mu) * lax.rsqrt(var + LN_EPS)
    return (y * g.astype(jnp.float32) + b.astype(jnp.float32)).astype(x.dtype)

def rms_norm(x, g):
    xf = x.astype(jnp.float32)
    y = xf * lax.rsqrt(jnp.mean(jnp.square(xf), -1, keepdims=True) + LN_EPS)
    return (y * g.astype(jnp.float32)).astype(x.dtype)

def axial_rope_tables(n_tokens, dim):
    rows = n_tokens // GRID_W
    row = jnp.broadcast_to(jnp.arange(rows, dtype=jnp.float32)[:, None], (rows, GRID_W)).reshape(-1)
    col = jnp.broadcast_to(jnp.arange(GRID_W, dtype=jnp.float32)[None, :], (rows, GRID_W)).reshape(-1)
    n_freq = dim // 4
    inv = ROPE_BASE ** (-jnp.arange(n_freq, dtype=jnp.float32) / n_freq)
    ar = row[:, None] * inv
    ac = col[:, None] * inv
    ang = jnp.concatenate([ar, ar, ac, ac], -1)
    return jnp.cos(ang), jnp.sin(ang)

def apply_rope(x, tables):
    cos, sin = tables
    shp = (cos.shape[0],) + (1,) * (x.ndim - 3) + (cos.shape[1],)
    cos = cos.reshape(shp)
    sin = sin.reshape(shp)
    x1, x2, x3, x4 = jnp.split(x, 4, axis=-1)
    rot = jnp.concatenate([-x2, x1, -x4, x3], -1)
    return (x * cos + rot * sin).astype(x.dtype)

def sink_softmax(s, sink):
    m = jnp.maximum(s.max(-1, keepdims=True), sink)
    p = jnp.exp(s - m)
    return p / (p.sum(-1, keepdims=True) + jnp.exp(sink - m))

def window_attention(q, k, v, qc, kc, vc, sink, with_ctx):
    B, T = q.shape[:2]
    nb = T // WINDOW
    scale = HEAD_DIM ** -0.5
    sink = sink.astype(jnp.float32).reshape(A_KV_HEADS, A_GROUP)[:, :, None, None]
    qb = q.reshape(B, nb, WINDOW, A_KV_HEADS, A_GROUP, HEAD_DIM)
    pad = ((0, 0), (WINDOW, WINDOW), (0, 0), (0, 0))
    kp = jnp.pad(k, pad).reshape(B, nb + 2, WINDOW, A_KV_HEADS, HEAD_DIM)
    vp = jnp.pad(v, pad).reshape(B, nb + 2, WINDOW, A_KV_HEADS, HEAD_DIM)
    kb = jnp.concatenate([kp[:, :-2], kp[:, 1:-1], kp[:, 2:]], axis=2)
    vb = jnp.concatenate([vp[:, :-2], vp[:, 1:-1], vp[:, 2:]], axis=2)
    s_loc = jnp.einsum('bnqgrd,bnkgd->bngrqk', qb, kb, preferred_element_type=jnp.float32) * scale
    r = jnp.arange(WINDOW)[:, None]
    j = jnp.arange(3 * WINDOW)[None, :]
    rel = j - WINDOW - r
    kpos = jnp.arange(nb)[:, None, None] * WINDOW - WINDOW + j[None]
    mask = (jnp.abs(rel) <= WINDOW)[None] & (kpos >= 0) & (kpos < T)
    s_loc = jnp.where(mask[None, :, None, None], s_loc, -jnp.inf)
    s_ctx = jnp.einsum('bnqgrd,bkgd->bngrqk', qb, kc, preferred_element_type=jnp.float32) * scale
    p = sink_softmax(jnp.concatenate([s_loc, s_ctx], -1), sink)
    n_loc = 3 * WINDOW
    o = (jnp.einsum('bngrqk,bnkgd->bnqgrd', p[..., :n_loc].astype(v.dtype), vb)
         + jnp.einsum('bngrqk,bkgd->bnqgrd', p[..., n_loc:].astype(v.dtype), vc))
    y = o.reshape(B, T, A_WIDTH)
    yc = None
    if with_ctx:
        Cn = qc.shape[1]
        qcb = qc.reshape(B, Cn, A_KV_HEADS, A_GROUP, HEAD_DIM)
        sc = jnp.einsum('bqgrd,bkgd->bgrqk', qcb, kc, preferred_element_type=jnp.float32) * scale
        pc = sink_softmax(sc, sink)
        yc = jnp.einsum('bgrqk,bkgd->bqgrd', pc.astype(vc.dtype), vc).reshape(B, Cn, A_WIDTH)
    return y, yc

def diff_attention(q, k, v, qc, kc, vc, lam, lam_init, norm_g, with_ctx):
    B, T = q.shape[:2]
    scale = B_QK_DIM ** -0.5

    def attend(qblk, keys, vals):
        s = jnp.einsum('bqhmd,bkhmd->bhmqk', qblk, keys, preferred_element_type=jnp.float32) * scale
        p = jax.nn.softmax(s, axis=-1)
        pd = p[:, :, 0] - lam * p[:, :, 1]
        return jnp.einsum('bhqk,bkhv->bqhv', pd.astype(vals.dtype), vals)

    k_all = jnp.concatenate([k, kc], axis=1)
    v_all = jnp.concatenate([v, vc], axis=1)
    nb = T // Q_BLOCK
    q_blocks = jnp.moveaxis(q.reshape(B, nb, Q_BLOCK, B_HEADS, 2, B_QK_DIM), 1, 0)
    o = lax.map(lambda qb: attend(qb, k_all, v_all), q_blocks)
    o = jnp.moveaxis(o, 0, 1).reshape(B, T, B_HEADS, B_V_DIM)
    y = (rms_norm(o, norm_g) * (1.0 - lam_init)).reshape(B, T, B_WIDTH)
    yc = None
    if with_ctx:
        oc = attend(qc, kc, vc)
        yc = (rms_norm(oc, norm_g) * (1.0 - lam_init)).reshape(B, qc.shape[1], B_WIDTH)
    return y, yc

def mlstm_scan(q, k, v, i_pre, logf, state):
    B, H, T, d = q.shape
    nc = T // CHUNK

    def to_chunks(a):
        return jnp.moveaxis(a.reshape(a.shape[:2] + (nc, CHUNK) + a.shape[3:]), 2, 0)

    xs = (to_chunks(q), to_chunks(k), to_chunks(v), to_chunks(i_pre), to_chunks(logf))
    lower = jnp.tril(jnp.ones((CHUNK, CHUNK), dtype=bool))

    def step(carry, inp):
        Cm, n, m = carry
        qc, kc, vc, ic, fc = inp
        b = jnp.cumsum(fc, axis=-1)
        log_d = jnp.where(lower, b[..., :, None] - b[..., None, :] + ic[..., None, :], -jnp.inf)
        m_inter = b + m[..., None]
        m_t = jnp.maximum(m_inter, log_d.max(-1))
        dmat = jnp.exp(log_d - m_t[..., None])
        s = jnp.einsum('bhtd,bhsd->bhts', qc, kc) * dmat
        w_inter = jnp.exp(m_inter - m_t)
        num = w_inter[..., None] * jnp.einsum('bhvd,bhtd->bhtv', Cm, qc) + jnp.einsum('bhts,bhsv->bhtv', s, vc)
        den = w_inter * jnp.einsum('bhd,bhtd->bht', n, qc) + s.sum(-1)
        h = num / jnp.maximum(jnp.abs(den), jnp.exp(-m_t))[..., None]
        b_last = b[..., -1]
        log_w = b_last[..., None] - b + ic
        m_new = jnp.maximum(b_last + m, log_w.max(-1))
        w = jnp.exp(log_w - m_new[..., None])
        decay = jnp.exp(b_last + m - m_new)
        C_new = decay[..., None, None] * Cm + jnp.einsum('bhs,bhsv,bhsd->bhvd', w, vc, kc)
        n_new = decay[..., None] * n + jnp.einsum('bhs,bhsd->bhd', w, kc)
        return (C_new, n_new, m_new), h

    state, hs = lax.scan(step, state, xs)
    return jnp.moveaxis(hs, 0, 2).reshape(B, H, T, d), state

def mlstm_branch(q, k, v, o, gates, qc, kc, vc, oc, gates_c, i_bias, f_bias, norm_g):
    def prep(q, k, v, gates):
        bht = lambda a: jnp.transpose(a, (0, 2, 1, 3)).astype(jnp.float32)
        g = jnp.transpose(gates.astype(jnp.float32), (2, 3, 0, 4, 1))
        return bht(q), bht(k) * HEAD_DIM ** -0.5, bht(v), g

    ql, kl, vl, gl = prep(q, k, v, gates)
    qx, kx, vx, gx = prep(qc, kc, vc, gates_c)
    B, H, _, d = ql.shape
    zero = (jnp.zeros((B, H, d, d), jnp.float32), jnp.zeros((B, H, d), jnp.float32), jnp.zeros((B, H), jnp.float32))
    flip = lambda a: jnp.flip(a, axis=2)
    h_lat_dirs = []
    h_ctx_dirs = []
    for direction in range(2):
        ib = i_bias[direction].astype(jnp.float32)[:, None]
        fb = f_bias[direction].astype(jnp.float32)[:, None]
        lat = (ql, kl, vl, gl[direction, 0] + ib, jax.nn.log_sigmoid(gl[direction, 1] + fb))
        cx = (qx, kx, vx, gx[direction, 0] + ib, jax.nn.log_sigmoid(gx[direction, 1] + fb))
        if direction == 1:
            lat = tuple(flip(a) for a in lat)
            cx = tuple(flip(a) for a in cx)
        hx, st = mlstm_scan(*cx, zero)
        hl, _ = mlstm_scan(*lat, st)
        if direction == 1:
            hx, hl = flip(hx), flip(hl)
        h_lat_dirs.append(hl)
        h_ctx_dirs.append(hx)
    g = norm_g.reshape(C_HEADS, HEAD_DIM)

    def finish(h, o_gate):
        h = rms_norm(jnp.transpose(h, (0, 2, 1, 3)), g)
        return (h.reshape(h.shape[0], h.shape[1], C_WIDTH) * jax.nn.sigmoid(o_gate.astype(jnp.float32))).astype(q.dtype)

    return (finish(h_lat_dirs[0] + h_lat_dirs[1], o), finish(h_ctx_dirs[0] + h_ctx_dirs[1], oc))

def split_proj(p):
    sizes = (A_WIDTH, A_KV_WIDTH, A_KV_WIDTH, A_WIDTH,
             B_QK_WIDTH, B_QK_WIDTH, B_WIDTH, B_WIDTH,
             C_WIDTH, C_WIDTH, C_WIDTH, C_WIDTH, C_WIDTH, C_GATE_WIDTH)
    return jnp.split(p, np.cumsum(sizes)[:-1].tolist(), axis=-1)

def heads(t, *shape):
    return t.reshape(t.shape[:2] + shape)

def hybrid_layer(x, ctx, c, c_ctx, w_mod, b_mod, w_in, sink, lam_vec, lam_init, diff_g,
                 i_bias, f_bias, mlstm_g, w_out, ln_g, ln_b, rope_a, rope_b, with_ctx):
    mod = jax.nn.silu(c) @ w_mod + b_mod
    mod_c = jax.nn.silu(c_ctx) @ w_mod + b_mod
    shift, scale, gate = jnp.split(mod, 3, axis=-1)
    shift_c, scale_c, gate_c = jnp.split(mod_c, 3, axis=-1)
    h = x * (1.0 + scale[:, None]) + shift[:, None]
    hc = ctx * (1.0 + scale_c) + shift_c
    qa, ka, va, za, qb, kb, vb, zb, qm, km, vm, om, zm, gm = split_proj(h @ w_in)
    qa_c, ka_c, va_c, za_c, qb_c, kb_c, vb_c, zb_c, qm_c, km_c, vm_c, om_c, zm_c, gm_c = split_proj(hc @ w_in)

    ya, ya_c = window_attention(
        apply_rope(heads(qa, A_HEADS, HEAD_DIM), rope_a), apply_rope(heads(ka, A_KV_HEADS, HEAD_DIM), rope_a),
        heads(va, A_KV_HEADS, HEAD_DIM),
        heads(qa_c, A_HEADS, HEAD_DIM), heads(ka_c, A_KV_HEADS, HEAD_DIM), heads(va_c, A_KV_HEADS, HEAD_DIM),
        sink, with_ctx)

    lv = lam_vec.astype(jnp.float32)
    lam = jnp.exp(jnp.sum(lv[0] * lv[1])) - jnp.exp(jnp.sum(lv[2] * lv[3])) + lam_init
    yb, yb_c = diff_attention(
        apply_rope(heads(qb, B_HEADS, 2, B_QK_DIM), rope_b), apply_rope(heads(kb, B_HEADS, 2, B_QK_DIM), rope_b),
        heads(vb, B_HEADS, B_V_DIM),
        heads(qb_c, B_HEADS, 2, B_QK_DIM), heads(kb_c, B_HEADS, 2, B_QK_DIM), heads(vb_c, B_HEADS, B_V_DIM),
        lam, lam_init, diff_g, with_ctx)

    ym, ym_c = mlstm_branch(
        heads(qm, C_HEADS, HEAD_DIM), heads(km, C_HEADS, HEAD_DIM), heads(vm, C_HEADS, HEAD_DIM), om,
        heads(gm, 2, 2, C_HEADS),
        heads(qm_c, C_HEADS, HEAD_DIM), heads(km_c, C_HEADS, HEAD_DIM), heads(vm_c, C_HEADS, HEAD_DIM), om_c,
        heads(gm_c, 2, 2, C_HEADS),
        i_bias, f_bias, mlstm_g)

    y = jnp.concatenate([ya * jax.nn.silu(za), yb * jax.nn.silu(zb), ym * jax.nn.silu(zm)], -1) @ w_out
    x_new = layer_norm(ALPHA * x + gate[:, None] * y, ln_g, ln_b)
    ctx_new = None
    if with_ctx:
        yc = jnp.concatenate([ya_c * jax.nn.silu(za_c), yb_c * jax.nn.silu(zb_c), ym_c * jax.nn.silu(zm_c)], -1) @ w_out
        ctx_new = layer_norm(ALPHA * ctx + gate_c * yc, ln_g, ln_b)
    return x_new, ctx_new

def setup_inputs(seed: int = 0) -> dict:
    key = jax.random.key(seed)
    ks = jax.random.split(key, 16)

    def nrm(k, shape, s):
        return jax.random.normal(k, shape, jnp.float32) * s

    return {
        "x": nrm(ks[0], (BATCH, SEQ, D_MODEL), 1.0),
        "c": nrm(ks[1], (BATCH, D_MODEL), 1.0),
        "ctx": nrm(ks[2], (BATCH, CTX_LEN, D_MODEL), 1.0),
        "c_ctx": nrm(ks[3], (D_MODEL,), 1.0),
        "w_mod": nrm(ks[4], (DEPTH, D_MODEL, 3 * D_MODEL), 0.5 * D_MODEL ** -0.5),
        "b_mod": nrm(ks[5], (DEPTH, 3 * D_MODEL), 0.02),
        "w_in": nrm(ks[6], (DEPTH, D_MODEL, D_IN), D_MODEL ** -0.5),
        "attn_sink": nrm(ks[7], (DEPTH, A_HEADS), 0.5),
        "diff_lambda": nrm(ks[8], (DEPTH, 4, B_QK_DIM), 0.1),
        "diff_norm_g": 1.0 + nrm(ks[9], (DEPTH, B_V_DIM), 0.02),
        "mlstm_i_bias": nrm(ks[10], (DEPTH, 2, C_HEADS), 0.1),
        "mlstm_f_bias": jnp.linspace(3.0, 6.0, C_HEADS, dtype=jnp.float32) + nrm(ks[11], (DEPTH, 2, C_HEADS), 0.1),
        "mlstm_norm_g": 1.0 + nrm(ks[12], (DEPTH, C_WIDTH), 0.02),
        "w_out": nrm(ks[13], (DEPTH, D_MIX, D_MODEL), BETA * D_MIX ** -0.5),
        "ln_g": 1.0 + nrm(ks[14], (DEPTH, D_MODEL), 0.02),
        "ln_b": nrm(ks[15], (DEPTH, D_MODEL), 0.02),
    }

def reference(x, c, ctx, c_ctx, w_mod, b_mod, w_in, attn_sink, diff_lambda, diff_norm_g,
              mlstm_i_bias, mlstm_f_bias, mlstm_norm_g, w_out, ln_g, ln_b):
    T = x.shape[1]
    rope_a = axial_rope_tables(T, HEAD_DIM)
    rope_b = axial_rope_tables(T, B_QK_DIM)
    for l in range(DEPTH):
        lam_init = 0.8 - 0.6 * math.exp(-0.3 * l)
        x, ctx = hybrid_layer(x, ctx, c, c_ctx, w_mod[l], b_mod[l], w_in[l], attn_sink[l], diff_lambda[l],
                              lam_init, diff_norm_g[l], mlstm_i_bias[l], mlstm_f_bias[l], mlstm_norm_g[l],
                              w_out[l], ln_g[l], ln_b[l], rope_a, rope_b, with_ctx=(l < DEPTH - 1))
    return x


_drawn_inputs = setup_inputs


def setup_inputs(seed=0):
    import zlib

    import numpy as np

    out = dict(_drawn_inputs(seed))
    spreads = {}
    factors = {'ctx': 8.0,
     'c_ctx': 5.493,
     'b_mod': 8.0,
     'attn_sink': 64.0,
     'diff_lambda': 8.0,
     'diff_norm_g': 49.661,
     'mlstm_i_bias': 64.0,
     'mlstm_f_bias': 2.951,
     'mlstm_norm_g': 64.0}
    for name, (base, spread) in spreads.items():
        noise = np.random.default_rng([zlib.crc32(name.encode()), seed]).standard_normal(out[name].shape)
        drawn = base * np.exp(spread * noise) if base else spread * noise
        out[name] = jnp.asarray(drawn.astype(out[name].dtype))
    for name, factor in factors.items():
        out[name] = (out[name] * factor).astype(out[name].dtype)
    return out
```

```python
from contextlib import ExitStack

import numpy as np

import concourse.bass as bass
from concourse import mybir

F32 = mybir.dt.float32
BF16 = mybir.dt.bfloat16
ALU = mybir.AluOpType
ACT = mybir.ActivationFunctionType
AX = mybir.AxisListType

P = 128
DM = 1024
KT = DM // P
DEPTH = 2
SEQ, CTX = 2048, 256
TOK = SEQ + CTX
NT = TOK // P
NTL = SEQ // P
HD = 64
A_HEADS, A_KV = 4, 2
B_HEADS, B_QK = 6, 32
C_HEADS = 6
GRID_W = 64
EPS = 1e-5
ALPHA = (2 * DEPTH) ** 0.25
WIN = 128
NEG = -1.0e30
CW, NCH = 384, 6
VA, SA, VB, SB, VM, SC, NW = 0, 128, 384, 768, 1152, 1536, 1920
TILES = 16
PADTOK = TOK + 2 * WIN
LAT0, CTX0 = WIN, SEQ + 2 * WIN
TB = [(512 * b, 512) for b in range(4)] + [(SEQ, CTX)]


class Chain:

    def __init__(self, eng, sem):
        self.eng, self.sem, self.base, self.n = eng, sem, 0, 0

    def turn(self, base):
        self.base, self.n = base, 0

    def __call__(self, instruction):
        self.n += 1
        instruction.then_inc(self.sem, 1)
        self.eng.wait_ge(self.sem, self.base + self.n)


class Core:

    def __init__(self, nc, stack, io, d):
        self.nc, self.stack, self.io, self.d = nc, stack, io, d
        self.stage = 0

    def semaphores(self, stack, prefix, single, several=()):
        self.stage += 1
        made = {n: stack.enter_context(self.nc.semaphore(f"{prefix}_{n}_{self.stage}")) for n in single}
        made.update({n: [stack.enter_context(self.nc.semaphore(f"{prefix}_{n}{u}_{self.stage}")) for u in range(count)]
                     for n, count in dict(several).items()})
        for s in made.values():
            for one in s if isinstance(s, list) else [s]:
                self.nc.sync.sem_clear(one)
        self.nc.all_engine_barrier()
        return made

    def buffers(self, stack):
        self.stage += 1
        stage = self.stage
        return lambda name, shape, dtype=F32: stack.enter_context(self.nc.sbuf_tensor(f"{name}_{stage}", shape, dtype))


def modulation(k, l, names):
    nc, io, d, ps = k.nc, k.io, k.d, k.ps
    with ExitStack() as st:
        sb = k.buffers(st)
        NC2, W = 6, 512
        wm = sb("mod_w", [P, 3, KT, W])
        brow = sb("mod_bias", [2, 3 * DM])
        mod = sb("mod_rows", [2, 3 * DM])
        w_ld, b_ld, done, added, stored, cols_ld = names["w_ld"], names["b_ld"], names["done"], names["added"], names["stored"], names["cols_ld"]
        block = st.enter_context(nc.Block())
        wv = io["w_mod"].rearrange("l (k p) n -> l p k n", p=P)
        modv = d["mod"].rearrange("r (j k p) -> p j r k", j=3, p=P)

        @block.sync
        def _(sp):
            sp.dma_start(brow[:], io["b_mod"][l, :].partition_broadcast(2)).then_inc(b_ld, 16)
            for c in range(NC2):
                if c >= 3:
                    sp.wait_ge(done, c - 2)
                sp.dma_start(wm[:, c % 3, :, :], wv[l, :, :, c * W:(c + 1) * W]).then_inc(w_ld[c % 3], 16)
            sp.wait_ge(added, NC2)
            sp.dma_start(d["mod"], mod[:]).then_inc(stored, 16)
            sp.wait_ge(stored, 16)
            for j in range(2):
                for r in range(2):
                    sp.dma_start(k.modc[:, j, r, :], modv[:, j, r, :], allow_slow_non_contiguous=True).then_inc(cols_ld, 16)
            sp.wait_ge(cols_ld, 64)

        @block.tensor
        def _(pe):
            for c in range(NC2):
                pe.wait_ge(w_ld[c % 3], 16 * (c // 3 + 1))
                for j in range(KT):
                    mm = nc.tensor.matmul(ps[0:2, c, 0:W], k.silu_c[:, j, :], wm[:, c % 3, j, :],
                                          start=(j == 0), stop=(j == KT - 1))
                mm.then_inc(done, 1)

        @block.vector
        def _(dve):
            dve.wait_ge(b_ld, 16)
            for c in range(NC2):
                dve.wait_ge(done, c + 1)
                nc.vector.tensor_tensor(mod[:, c * W:(c + 1) * W], ps[0:2, c, 0:W],
                                        brow[:, c * W:(c + 1) * W], ALU.add).then_inc(added, 1)
            dve.wait_ge(cols_ld, 64)
            nc.vector.tensor_scalar(k.modc[:, 1, :, :], k.modc[:, 1, :, :], 1.0, None, ALU.add).then_inc(added, 1)
            dve.wait_ge(added, NC2 + 1)


def natural_project(k, l, hT, s):
    nc, io, d, ps = k.nc, k.io, k.d, k.ps
    with ExitStack() as st:
        sb = k.buffers(st)
        wn = sb("wn", [P, NCH, KT, CW])
        xt = sb("xt", [P, 2, DM])
        hs = sb("hs", [P, 2, KT, P])
        nt = sb("nt", [P, 2, NW])
        sz = sb("sz", [P, 2, CW])
        block = st.enter_context(nc.Block())
        w_ld, x_ld, n_st = s["w_ld"], s["x_ld"], s["n_st"]
        turned, h_ready, kept = s["turned"], s["h_ready"], s["kept"]
        prod, evac, v_free, z_free, n_ready = s["prod"], s["evac"], s["v_free"], s["z_free"], s["n_ready"]
        PAIRS = NT // 2
        HEAD = 2 * NCH

        @block.sync
        def _(sp):
            for u in range(2):
                sp.sem_inc(n_st[u], 16)
                sp.dma_start(xt[:, u, :], d["x"][u * P:(u + 1) * P, :]).then_inc(x_ld[u], 16)
            for c in range(NCH):
                sp.dma_start(wn[:, c, :, :], io["w_nat"][l, c, :, :, :]).then_inc(w_ld[c], 16)

            def store(i, u):
                sp.wait_ge(n_ready, 2 * i + (u + 1))
                sp.dma_start(d["nat"][bass.ds(i * (2 * P) + u * P, P), :], nt[:, u, :]).then_inc(n_st[u], 16)

            def store_va(i, u, row):
                sp.dma_start(d["va"][bass.ds(row, P), :], nt[:, u, 0:P]).then_inc(n_st[u], 16)

            with sp.Fori(0, PAIRS - 1) as i:
                for u in range(2):
                    sp.wait_ge(turned, 2 * i + (u + 1))
                    sp.dma_start(xt[:, u, :], d["x"][bass.ds(i * (2 * P) + (u + 2) * P, P), :]).then_inc(x_ld[u], 16)
                    store(i, u)
                    store_va(i, u, i * (2 * P) + u * P + LAT0)
            for u in range(2):
                store(PAIRS - 1, u)
                store_va(PAIRS - 1, u, CTX0 + u * P)
            for u in range(2):
                sp.wait_ge(n_st[u], 16 + 32 * PAIRS)

        @block.tensor
        def _(pe):
            pe.sem_inc(prod, HEAD)

            def turn(i, u, t):
                for j in range(KT):
                    tr = nc.tensor.transpose(ps[:, j // 4, (j % 4) * P:(j % 4 + 1) * P],
                                             xt[:, u, j * P:(j + 1) * P], k.ident[:])
                tr.then_inc(turned, 1)

            def product(i, u):
                pe.wait_ge(h_ready, 2 * i + (u + 1))
                for c in range(NCH):
                    free = v_free if c in (1, 3, 4) else z_free
                    n = {1: 0, 3: 1, 4: 2, 0: 0, 2: 1, 5: 2}[c]
                    pe.wait_ge(free, 6 * i + (3 * u + n + 1))
                    for j in range(KT):
                        mm = nc.tensor.matmul(ps[:, 2 + c, 0:CW], hs[:, u, j, :], wn[:, c, j, :],
                                              start=(j == 0), stop=(j == KT - 1))
                    mm.then_inc(prod, 1)

            pe.wait_ge(x_ld[0], 16)
            turn(0, 0, 0)
            for c in range(NCH):
                pe.wait_ge(w_ld[c], 16)
            with pe.Fori(0, PAIRS - 1) as i:
                pe.wait_ge(x_ld[1], 16 * i + 16)
                pe.wait_ge(h_ready, 2 * i + 1)
                turn(i, 1, None)
                product(i, 0)
                pe.wait_ge(x_ld[0], 16 * i + 32)
                pe.wait_ge(h_ready, 2 * i + 2)
                turn(i, 0, None)
                product(i, 1)
            i = PAIRS - 1
            pe.wait_ge(x_ld[1], 16 * i + 16)
            pe.wait_ge(h_ready, 2 * i + 1)
            turn(i, 1, None)
            product(i, 0)
            product(i, 1)

        @block.vector
        def _(dve):
            dve.sem_inc(z_free, 3)

            def modulate(t, u, r):
                dve.wait_ge(turned, t + 1)
                dve.wait_ge(prod, 6 * t + 6)
                dve.wait_ge(kept, t + 1)
                for j in range(KT):
                    op = nc.vector.tensor_scalar(hs[:, u, j, :], ps[:, j // 4, (j % 4) * P:(j % 4 + 1) * P],
                                                 k.modc[:, 1, r, j:j + 1], k.modc[:, 0, r, j:j + 1],
                                                 ALU.mult, ALU.add)
                op.then_inc(h_ready, 1)

            def gates(i, u):
                base = 6 * i + 3 * u
                zb = 6 * i + (3 * u + 3)
                dve.wait_ge(evac, base + 1)
                nc.vector.tensor_tensor(nt[:, u, SA:VB], nt[:, u, SA:VB], ps[:, 2, P:CW], ALU.mult).then_inc(z_free, 1)
                dve.wait_ge(evac, base + 2)
                nc.vector.tensor_tensor(nt[:, u, SB:VM], nt[:, u, SB:VM], ps[:, 4, 0:CW], ALU.mult).then_inc(z_free, 1)
                dve.wait_ge(evac, base + 3)
                nc.vector.tensor_tensor(sz[:, u, :], sz[:, u, :], ps[:, 7, 0:CW], ALU.mult).then_inc(z_free, 1)
                dve.wait_ge(z_free, zb + 3)
                nc.vector.tensor_tensor(nt[:, u, SC:NW], nt[:, u, SC:NW], sz[:, u, :], ALU.mult).then_inc(n_ready, 1)

            modulate(0, 0, 0)
            with dve.Fori(0, PAIRS - 2) as i:
                modulate(2 * i + 1, 1, 0)
                gates(i, 0)
                modulate(2 * i + 2, 0, 0)
                gates(i, 1)
            i = PAIRS - 2
            modulate(2 * i + 1, 1, 0)
            gates(i, 0)
            modulate(2 * i + 2, 0, 1)
            gates(i, 1)
            i = PAIRS - 1
            modulate(2 * i + 1, 1, 1)
            gates(i, 0)
            gates(i, 1)

        @block.scalar
        def _(act):
            act.sem_inc(v_free, 3)

            def body(i, u):
                base = 12 * i + (6 * u + HEAD)
                act.wait_ge(n_st[u], 32 * i + 16)

                def chunk(c):
                    act.wait_ge(prod, base + (c + 1))
                chunk(0)
                nc.scalar.copy(nt[:, u, VA:SA], ps[:, 2, 0:P])
                nc.scalar.activation(nt[:, u, SA:VB], ps[:, 2, P:CW], ACT.Sigmoid).then_inc(evac, 1)
                chunk(1)
                nc.scalar.copy(nt[:, u, VB:SB], ps[:, 3, 0:CW]).then_inc(v_free, 1)
                chunk(2)
                nc.scalar.activation(nt[:, u, SB:VM], ps[:, 4, 0:CW], ACT.Sigmoid).then_inc(evac, 1)
                chunk(3)
                nc.scalar.copy(nt[:, u, VM:SC], ps[:, 5, 0:CW]).then_inc(v_free, 1)
                chunk(4)
                nc.scalar.activation(nt[:, u, SC:NW], ps[:, 6, 0:CW], ACT.Sigmoid).then_inc(v_free, 1)
                chunk(5)
                nc.scalar.activation(sz[:, u, :], ps[:, 7, 0:CW], ACT.Sigmoid).then_inc(evac, 1)

            with act.Fori(0, PAIRS) as i:
                for u in range(2):
                    body(i, u)

        @block.gpsimd
        def _(pool):
            pool.sem_inc(kept, 2)
            with pool.Fori(0, PAIRS) as i:
                for u in range(2):
                    pool.wait_ge(h_ready, 2 * i + (u + 1))
                    nc.gpsimd.tensor_copy(hT[:, :, bass.ds(i * (2 * P) + u * P, P)], hs[:, u, :, :]).then_inc(kept, 1)


def transposed_project(k, l, hT, s, kinds, first, pairs, out):
    nc, io, d, ps = k.nc, k.io, k.d, k.ps
    rope = [isinstance(kind, str) for kind in kinds]
    split = kinds[0] == "rope_b"
    parts = 3 if split else 1
    NB = len(TB)
    R = sum(rope) * 4
    with ExitStack() as st:
        sb = k.buffers(st)
        wt = sb("wt", [P, 2, KT, P])
        qs = sb("qs", [P, 2, 512])
        tab = sb("tab", [P, 2, SEQ])
        perm = sb("perm", [P, P])
        t1 = sb("t1", [P, 2, 512])
        t2 = sb("t2", [P, 2, 512])
        ob = sb("ob", [P, 2, 3, 512], BF16) if split else sb("ob", [P, 2, 1, 512])
        block = st.enter_context(nc.Block())
        w_ld, tab_ld, o_st, prod, evac, rot, rot_free, done, chain = (
            s["w_ld"], s["tab_ld"], s["o_st"], s["prod"], s["evac"], s["rot"], s["rot_free"], s["done"], s["chain"])
        which = 1 if split else 0
        blocks = [(u, b) for u in range(2) for b in range(NB)]

        @block.sync
        def _(sp):
            for u in range(2):
                sp.sem_inc(o_st[u], 16 * parts)
                sp.dma_start(wt[:, u, :, :], io["w_tr"][l, first + u, :, :, :]).then_inc(w_ld[u], 16)
            if R:
                sp.dma_start(tab[:], io["rope"][which, :, :, :]).then_inc(tab_ld, 16)
                sp.dma_start(perm[:], io["perm"][which, :, :]).then_inc(tab_ld, 16)

            def store(i, n, u, b):
                sp.wait_ge(done, 2 * NB * i + (n + 3))
                t0, w = TB[b]
                for dst, src in out(i, u, b, t0, w, ob[:, n % 2, :, 0:w]):
                    sp.dma_start(dst, src).then_inc(o_st[n % 2], 16)

            def turn(i, more):
                for n, (u, b) in enumerate(blocks):
                    store(i, n, u, b)
                    if b == NB - 1 and more:
                        sp.wait_ge(prod, 2 * NB * i + NB * (u + 1))
                        sp.dma_start(wt[:, u, :, :], io["w_tr"][l, bass.ds(2 * i + (first + 2 + u), 1), :, :, :]
                                     .rearrange("o p k n -> p (o k) n")).then_inc(w_ld[u], 16)

            if pairs > 1:
                with sp.Fori(0, pairs - 1) as i:
                    turn(i, True)
            turn(pairs - 1, False)
            for u in range(2):
                sp.wait_ge(o_st[u], 16 * parts * (1 + NB * pairs))

        def loop(eng, body):
            if pairs > 1:
                with eng.Fori(0, pairs) as i:
                    body(i)
            else:
                body(0)

        @block.tensor
        def _(pe):
            if R:
                pe.wait_ge(tab_ld, 32)

            def body(i):
                r = 0
                for n, (u, b) in enumerate(blocks):
                    if b == 0:
                        pe.wait_ge(w_ld[u], 16 * i + 16)
                    t0, w = TB[b]
                    pe.wait_ge(evac, 2 * NB * i + (n + 1))
                    for j in range(KT):
                        mm = nc.tensor.matmul(ps[:, b, 0:w], wt[:, u, j, :], hT[:, j, t0:t0 + w],
                                              start=(j == 0), stop=(j == KT - 1))
                    mm.then_inc(prod, 1)
                    if rope[u] and b >= 1:
                        pe.wait_ge(evac, 2 * NB * i + (n + NB))
                        pe.wait_ge(rot_free, R * i + (r + 1))
                        nc.tensor.matmul(ps[:, 5 + r % 2, 0:512], perm[:], qs[:, (n - 1) % 2, 0:512],
                                         start=True, stop=True).then_inc(rot, 1)
                        r += 1
            loop(pe, body)

        @block.scalar
        def _(act):
            act.sem_inc(evac, NB)

            def body(i):
                for n, (u, b) in enumerate(blocks):
                    w = TB[b][1]
                    act.wait_ge(prod, 2 * NB * i + (n + 1))
                    act.wait_ge(done, 2 * NB * i + (n + 1))
                    nc.scalar.copy(qs[:, n % 2, 0:w], ps[:, b, 0:w]).then_inc(evac, 1)
            loop(act, body)

        @block.vector
        def _(dve):
            link = Chain(dve, chain)
            steps = 3 * 2 * NB + R
            dve.sem_inc(rot_free, 2)
            dve.sem_inc(done, 2)
            if R:
                dve.wait_ge(tab_ld, 32)

            def body(i):
                link.turn(steps * i)
                r = 0
                for n, (u, b) in enumerate(blocks):
                    t0, w = TB[b]
                    v = n % 2
                    src = qs[:, v, 0:w]
                    dve.wait_ge(evac, 2 * NB * i + (n + 1 + NB))
                    dve.wait_ge(o_st[v], 16 * parts * NB * i + 16 * parts * (n // 2 + 1))
                    if rope[u] and b < 4:
                        nc.vector.tensor_tensor(t1[:, v, 0:w], src, tab[:, 0, t0:t0 + w], ALU.mult)
                        dve.wait_ge(rot, R * i + (r + 1))
                        nc.vector.tensor_tensor(t2[:, v, 0:w], ps[:, 5 + r % 2, 0:w], tab[:, 1, t0:t0 + w],
                                                ALU.mult).then_inc(rot_free, 1)
                        r += 1
                        dve.wait_ge(rot_free, R * i + (r + 2))
                        if split:
                            link(nc.vector.tensor_tensor(t1[:, v, 0:w], t1[:, v, 0:w], t2[:, v, 0:w], ALU.add))
                            src = t1[:, v, 0:w]
                        else:
                            last = nc.vector.tensor_tensor(ob[:, v, 0, 0:w], t1[:, v, 0:w], t2[:, v, 0:w], ALU.add)
                    elif not split:
                        factor = 1.0 if rope[u] else kinds[u]
                        last = nc.vector.tensor_scalar(ob[:, v, 0, 0:w], src, factor, None, ALU.mult)
                    if split:
                        link(nc.vector.tensor_copy(ob[:, v, 0, 0:w], src))
                        link(nc.vector.tensor_tensor(t2[:, v, 0:w], src, ob[:, v, 0, 0:w], ALU.subtract))
                        link(nc.vector.tensor_copy(ob[:, v, 1, 0:w], t2[:, v, 0:w]))
                        last = nc.vector.tensor_tensor(ob[:, v, 2, 0:w], t2[:, v, 0:w], ob[:, v, 1, 0:w], ALU.subtract)
                    last.then_inc(done, 1)
                assert not split or link.n == steps
            loop(dve, body)


UNITS = 2 * C_HEADS
PAIRS_C = C_HEADS // 2
SV = HD + 1
PV = 2 * SV
KEY, INTER, UPDATE, FLOOR = range(4)
DIRS = ((0, 32), (32, 64))


def mlstm_gates(k, l, s, cols, knat, v1):
    nc, io, d, ps = k.nc, k.io, k.d, k.ps
    with ExitStack() as st:
        sb = k.buffers(st)
        gi, gf, keep, tmp, logf, b, m = (sb(n, [64, TOK]) for n in ("gi", "gf", "keep", "tmp", "logf", "b", "m"))
        stat = sb("stat", [64, 4, TOK])
        turn = sb("turn", [64, 2, 4, P])
        ib, fb = sb("ib", [64, 1]), sb("fb", [64, 1])
        mprev, delta, decay = (sb(n, [64, NT]) for n in ("mprev", "delta", "decay"))
        kc = sb("kc", [P, 2, PAIRS_C, P])
        block = st.enter_context(nc.Block())
        cleared, g_ld, v_ld, k_ld, dve_s, act_s, row_st = (
            s[n] for n in ("cleared", "g_ld", "v_ld", "k_ld", "gate_steps", "gate_exps", "row_st"))
        staged, turned, kept = s["staged"], s["turned"], s["kept"]

        @block.sync
        def _(sp):
            for u in range(2):
                sp.dma_start(kc[:, u, :, :], d["qkc"][1, :, u * P:(u + 1) * P].rearrange("(c p) t -> p c t", p=P)
                             ).then_inc(k_ld[u], 16)
            sp.dma_start(keep[:], io["keep"]).then_inc(g_ld, 16)
            sp.wait_ge(dve_s, 1)
            for way, (lo, _) in enumerate(DIRS):
                sp.dma_start(gi[lo:lo + 6, :], d["gates"][12 * way:12 * way + 6, :]).then_inc(g_ld, 16)
                sp.dma_start(gf[lo:lo + 6, :], d["gates"][12 * way + 6:12 * way + 12, :]).then_inc(g_ld, 16)
                sp.dma_start(ib[lo:lo + 6, :], io["i_bias"][l, way, :].unsqueeze(1)).then_inc(g_ld, 16)
                sp.dma_start(fb[lo:lo + 6, :], io["f_bias"][l, way, :].unsqueeze(1)).then_inc(g_ld, 16)
            sp.wait_ge(cleared, 1)
            for h in range(C_HEADS):
                sp.dma_start(v1[:, :, h, 0:HD], d["nat"][:, VM + h * HD:VM + (h + 1) * HD].rearrange("(c p) v -> p c v", p=P)
                             ).then_inc(v_ld, 16)
            with sp.Fori(0, NT // 2 - 1) as i:
                for u in range(2):
                    sp.wait_ge(turned, 2 * i + (u + 3))
                    sp.dma_start(kc[:, u, :, :], d["qkc"][1, :, bass.ds(i * (2 * P) + (2 + u) * P, P)].rearrange("(c p) t -> p c t", p=P)
                                 ).then_inc(k_ld[u], 16)
            sp.wait_ge(act_s, 6)
            for way, (lo, _) in enumerate(DIRS):
                sp.dma_start(d["u"][6 * way:6 * way + 6, :], tmp[lo:lo + 6, :]).then_inc(row_st, 16)
                sp.dma_start(d["decay"][6 * way:6 * way + 6, :], decay[lo:lo + 6, :]).then_inc(row_st, 16)
            sp.wait_ge(row_st, 64)
            sp.wait_ge(v_ld, 16 * C_HEADS)

        @block.gpsimd
        def _(pool):
            nc.gpsimd.memset(v1[:], 1.0).then_inc(cleared, 1)
            pool.wait_ge(cleared, 1)

        @block.vector
        def _(dve):
            link = Chain(dve, dve_s)
            for t in (gi, gf, ib, fb):
                last = nc.vector.memset(t[:], 0.0)
            link(last)
            dve.wait_ge(g_ld, 16 * 9)
            link(nc.vector.tensor_scalar(gi[:], gi[:], ib[:], None, ALU.add))
            link(nc.vector.tensor_scalar(gf[:], gf[:], fb[:], None, ALU.add))
            link(nc.vector.scalar_tensor_tensor(out=tmp[:], in0=gf[:], scalar=-1.0, in1=gf[:],
                                                op0=ALU.mult, op1=ALU.max))
            dve.wait_ge(act_s, 2)
            link(nc.vector.scalar_tensor_tensor(out=logf[:], in0=gf[:], scalar=0.0, in1=tmp[:],
                                                op0=ALU.min, op1=ALU.subtract))
            scan = nc.vector.tensor_tensor_scan
            scan(out=b[0:32, :], data0=keep[0:32, :], data1=logf[0:32, :], initial=0.0, op0=ALU.mult, op1=ALU.add)
            scan(out=b[32:64, ::-1], data0=keep[32:64, ::-1], data1=logf[32:64, ::-1], initial=0.0, op0=ALU.mult, op1=ALU.add)
            scan(out=m[32:64, ::-1], data0=logf[32:64, ::-1], data1=gi[32:64, ::-1], initial=0.0, op0=ALU.add, op1=ALU.max)
            link(scan(out=m[0:32, SEQ:TOK], data0=logf[0:32, SEQ:TOK], data1=gi[0:32, SEQ:TOK], initial=0.0,
                      op0=ALU.add, op1=ALU.max))
            link(scan(out=m[0:32, 0:SEQ], data0=logf[0:32, 0:SEQ], data1=gi[0:32, 0:SEQ],
                      initial=m[0:32, TOK - 1:TOK], op0=ALU.add, op1=ALU.max))
            chunks = lambda t: t.rearrange("r (c t) -> r c t", t=P)
            mc, bc = chunks(m[:]), chunks(b[:])
            nc.vector.tensor_tensor(tmp[:], b[:], m[:], ALU.subtract)
            nc.vector.tensor_tensor(stat[:, KEY, :], gi[:], b[:], ALU.subtract)
            nc.vector.memset(mprev[:], 0.0)
            nc.vector.tensor_tensor(delta[0:32, :], bc[0:32, :, P - 1], mc[0:32, :, P - 1], ALU.subtract)
            link(nc.vector.tensor_tensor(delta[32:64, :], bc[32:64, :, 0], mc[32:64, :, 0], ALU.subtract))
            nc.vector.tensor_copy(mprev[0:32, 1:NTL], mc[0:32, 0:NTL - 1, P - 1])
            nc.vector.tensor_copy(mprev[0:32, 0:1], mc[0:32, NT - 1, P - 1:P])
            nc.vector.tensor_copy(mprev[0:32, NTL + 1:NT], mc[0:32, NTL:NT - 1, P - 1])
            link(nc.vector.tensor_copy(mprev[32:64, 0:NT - 1], mc[32:64, 1:NT, 0]))
            wide = lambda t: t[:].unsqueeze(2).to_broadcast([64, NT, P])
            nc.vector.tensor_tensor(chunks(stat[:, INTER, :]), chunks(tmp[:]), wide(mprev), ALU.add)
            nc.vector.tensor_tensor(chunks(stat[:, UPDATE, :]), chunks(stat[:, KEY, :]), wide(delta), ALU.add)
            link(nc.vector.tensor_tensor(decay[:], delta[:], mprev[:], ALU.add))
            dve.wait_ge(act_s, 6)
            with dve.Fori(0, NT // 2) as i:
                for u in range(2):
                    dve.wait_ge(turned, 2 * i + (u + 1))
                    nc.vector.tensor_copy(turn[:, u, :, :], stat[:, :, bass.ds(i * (2 * P) + u * P, P)]).then_inc(staged, 1)

        @block.scalar
        def _(act):
            link = Chain(act, act_s)
            act.wait_ge(dve_s, 4)
            link(nc.scalar.activation(tmp[:], tmp[:], ACT.Exp, scale=-1.0))
            link(nc.scalar.activation(tmp[:], tmp[:], ACT.Ln, bias=1.0))
            act.wait_ge(dve_s, 10)
            link(nc.scalar.activation(stat[:, INTER, :], stat[:, INTER, :], ACT.Exp))
            link(nc.scalar.activation(stat[:, UPDATE, :], stat[:, UPDATE, :], ACT.Exp))
            link(nc.scalar.activation(stat[:, FLOOR, :], m[:], ACT.Exp, scale=-1.0))
            link(nc.scalar.activation(decay[:], decay[:], ACT.Exp))
            act.sem_inc(kept, 2)
            with act.Fori(0, NT // 2) as i:
                for u in range(2):
                    act.wait_ge(turned, 2 * i + (u + 3))
                    nc.scalar.copy(cols[:, bass.ds(2 * i + u, 1), :, :].rearrange("p o f (w h) -> p (o f) w h", w=2),
                                   ps[:, u, 0:256].rearrange("p (f w h) -> p f w h", f=4, w=2)[:, :, :, 0:C_HEADS])
                    nc.scalar.copy(knat[:, bass.ds(2 * i + u, 1), :].rearrange("p o c -> p (o c)"),
                                   ps[:, 2 + u, 0:PAIRS_C * P]).then_inc(kept, 1)

        @block.tensor
        def _(pe):
            pe.sem_inc(turned, 2)
            with pe.Fori(0, NT // 2) as i:
                for u in range(2):
                    pe.wait_ge(k_ld[u], 16 * i + 16)
                    pe.wait_ge(kept, 2 * i + (u + 1))
                    pe.wait_ge(staged, 2 * i + (u + 1))
                    for p in range(PAIRS_C):
                        nc.tensor.transpose(ps[:, 2 + u, p * P:(p + 1) * P], kc[:, u, p, :], k.ident[:])
                    for f in range(4):
                        tr = nc.tensor.transpose(ps[:, u, f * 64:(f + 1) * 64], turn[:, u, f, :], k.ident[0:64, 0:64])
                    tr.then_inc(turned, 1)


def mlstm_states(k, l, s, cols, knat, v1, states):
    nc, io, d, ps = k.nc, k.io, k.d, k.ps
    with ExitStack() as st:
        sb = k.buffers(st)
        kw = sb("kw", [P, 2, 2, C_HEADS, HD])
        dec = sb("dec", [P, 2, PAIRS_C, NT])
        block = st.enter_context(nc.Block())
        d_ld, weighed, prod, stepped = s["d_ld"], s["weighed"], s["prod"], s["stepped"]
        head = [(NT - 2, NT - 1, NT - 1, NT - 2), (NT - 1, NT - 2, 0, NTL - 1)]

        def steps(eng, body):
            for n, c in enumerate(head):
                body(n, n % 2, *c)
            with eng.Fori(0, (NTL - 2) // 2) as i:
                for u in range(2):
                    body(2 * i + (2 + u), u, 2 * i + u, (NTL - 1 - u) - 2 * i, 2 * i + (u + 1), (NTL - 2 - u) - 2 * i)
            body(NTL, 0, NTL - 2, 1, NTL - 1, 0)

        @block.sync
        def _(sp):
            by_half = d["decay"].rearrange("(w p h) c -> h w p c", w=2, h=2)
            for h in range(2):
                sp.dma_start(dec[64 * h:64 * h + 64, :, :, :], by_half[h, :, :, :].partition_broadcast(64)).then_inc(d_ld, 16)
            sp.wait_ge(d_ld, 32)

        @block.gpsimd
        def _(pool):
            nc.gpsimd.memset(states[:, NT // 2:NTL, :, :, :], 0.0).then_inc(s["cleared3"], 1)

            def body(n, u, f, b, fn, bn):
                pool.wait_ge(prod, n + 1)
                for way, c in ((0, f), (1, b)):
                    op = nc.gpsimd.tensor_tensor(
                        kw[:, u, way, :, :], knat[:, bass.ds(c, 1), :].rearrange("p o (h e) -> p (o h) e", e=HD),
                        cols[:, bass.ds(c, 1), UPDATE, way * C_HEADS:(way + 1) * C_HEADS].rearrange("p o h -> p (o h)")
                        .unsqueeze(2).to_broadcast([P, C_HEADS, HD]), ALU.mult)
                op.then_inc(weighed, 1)
            steps(pool, body)

        @block.tensor
        def _(pe):
            pe.sem_inc(prod, 2)

            def body(n, u, f, b, fn, bn):
                pe.wait_ge(weighed, n + 1)
                pe.wait_ge(stepped, n + 1)
                for way, c in ((0, f), (1, b)):
                    for p in range(PAIRS_C):
                        mm = nc.tensor.matmul(ps[:, 2 * u + way, p * PV:(p + 1) * PV],
                                              kw[:, u, way, 2 * p:2 * p + 2, :].rearrange("p h e -> p (h e)"),
                                              v1[:, bass.ds(c, 1), 2 * p:2 * p + 2, :].rearrange("p o h e -> p (o h e)"),
                                              start=True, stop=True)
                mm.then_inc(prod, 1)
            steps(pe, body)

        @block.vector
        def _(dve):
            dve.sem_inc(stepped, 1)
            nc.vector.memset(states[:, 0:NT // 2, :, :, :], 0.0)
            nc.vector.memset(states[:, NTL:, :, :, :], 0.0).then_inc(stepped, 1)
            dve.wait_ge(d_ld, 32)
            dve.wait_ge(s["cleared3"], 1)

            def body(n, u, f, b, fn, bn):
                dve.wait_ge(prod, n + 3)
                dve.wait_ge(stepped, n + 2)
                for way, c, cn in ((0, f, fn), (1, b, bn)):
                    for p in range(PAIRS_C):
                        for h in range(2):
                            half, at = slice(64 * h, 64 * h + 64), slice(h * SV, (h + 1) * SV)
                            state = lambda c: states[half, bass.ds(c, 1), way, p, at].rearrange("p o e -> p (o e)")
                            op = nc.vector.scalar_tensor_tensor(
                                out=state(cn), in0=state(c), scalar=dec[half, way, p, bass.ds(c, 1)],
                                in1=ps[half, 2 * u + way, p * PV + h * SV:p * PV + (h + 1) * SV],
                                op0=ALU.mult, op1=ALU.add)
                op.then_inc(stepped, 1)
            steps(dve, body)


def mlstm_outputs(k, l, s, cols, v1, states):
    nc, io, d, ps = k.nc, k.io, k.d, k.ps
    with ExitStack() as st:
        sb = k.buffers(st)
        mask = sb("mask", [P, 2, P])
        kt = sb("kt", [P, 2, PAIRS_C, P])
        qt = sb("qt", [P, 2, PAIRS_C, P])
        qd = sb("qd", [P, 2, PAIRS_C, 2, P])
        ur = sb("ur", [P, 2, UNITS, P])
        gate = sb("gate", [P, 2, UNITS, P])
        mt = sb("mt", [P, UNITS, P])
        num = sb("num", [P, 2, UNITS, SV])
        den = sb("den", [P, 2, UNITS])
        both = sb("both", [P, 2, UNITS, HD])
        yt = sb("yt", [P, 2, C_HEADS * HD])
        block = st.enter_context(nc.Block())
        (m_ld, c_ld, y_st, cleared, logits, gated, scored, mixed, intra, inter, inter_free, chain, ready, y_done) = (
            s[n] for n in ("m_ld", "c_ld", "y_st", "cleared2", "logits", "gated", "scored", "mixed", "intra", "inter",
                           "inter_free", "den_steps", "ready", "y_done"))
        LOADS = 5

        @block.sync
        def _(sp):
            sp.dma_start(mask[:], io["causal"]).then_inc(m_ld, 16)
            sp.wait_ge(cleared, 1)

            def load(c, u):
                span = bass.ds(c * P, P)
                pairs = lambda j: d["qkc"][j, :, span].rearrange("(c p) t -> p c t", p=P)
                sp.dma_start(kt[:, u, :, :], pairs(1)).then_inc(c_ld[u], 16)
                sp.dma_start(qt[:, u, :, :], pairs(0)).then_inc(c_ld[u], 16)
                for h in range(2):
                    half = slice(64 * h, 64 * h + 64)
                    sp.dma_start(qd[half, u, :, h, :], pairs(0)[half, :, :]).then_inc(c_ld[u], 16)
                sp.dma_start(ur[:, u, :, :], d["u"][:, span].partition_broadcast(P)).then_inc(c_ld[u], 16)

            def store(c, u):
                sp.wait_ge(y_done, c + (1 + 2))
                sp.dma_start(d["y"][bass.ds(c * P, P), 640:DM], yt[:, u, :]).then_inc(y_st[u], 16)
            for u in range(2):
                sp.sem_inc(y_st[u], 16)
                load(u, u)
            with sp.Fori(0, NT // 2 - 1) as i:
                for u in range(2):
                    sp.wait_ge(inter, 2 * i + (u + 1))
                    sp.wait_ge(logits, 2 * i + (u + 1))
                    load(2 * i + (u + 2), u)
                    store(2 * i + u, u)
            for u in range(2):
                store(NT - 2 + u, u)
            for u in range(2):
                sp.wait_ge(y_st[u], 16 + 16 * (NT // 2))

        def over_chunks(eng, first, body):
            first()
            with eng.Fori(0, NT // 2 - 1) as i:
                for u in range(2):
                    body(2 * i + u, u, i, True)
            body(NT - 2, 0, NT // 2 - 1, True)
            body(NT - 1, 1, NT // 2 - 1, False)

        @block.tensor
        def _(pe):
            def score(c, u, turn):
                pe.wait_ge(c_ld[u], 16 * LOADS * turn + 16 * LOADS)
                for p in range(PAIRS_C):
                    mm = nc.tensor.matmul(ps[:, p // 2, (p % 2) * 256:(p % 2) * 256 + 256], kt[:, u, p, :],
                                          qd[:, u, p, :, :].rearrange("p h t -> p (h t)"), start=True, stop=True)
                mm.then_inc(scored, 1)

            def incoming(c, u):
                for p in range(PAIRS_C):
                    mm = nc.tensor.matmul(ps[:, 4 + p, 0:2 * PV], qt[:, u, p, :],
                                          states[:, bass.ds(c, 1), :, p, :].rearrange("p o w e -> p (o w) e"),
                                          start=True, stop=True)
                mm.then_inc(inter, 1)

            def within(c, u):
                for way in range(2):
                    pe.wait_ge(mixed, 2 * c + (way + 1))
                    for h in range(C_HEADS):
                        mm = nc.tensor.matmul(ps[:, 2 + way, h * SV:(h + 1) * SV], mt[:, way * C_HEADS + h, :],
                                              v1[:, bass.ds(c, 1), h, :].rearrange("p o e -> p (o e)"), start=True, stop=True)
                mm.then_inc(intra, 1)

            def first():
                score(0, 0, 0)
                incoming(0, 0)
                within(0, 0)

            def body(c, u, i, more):
                if more:
                    score(c + 1, 1 - u, i + u)
                    pe.wait_ge(inter_free, 2 * c + 2)
                    incoming(c + 1, 1 - u)
                    within(c + 1, 1 - u)
            over_chunks(pe, first, body)

        @block.scalar
        def _(act):
            def one(c, u):
                act.wait_ge(logits, c + 1)
                nc.scalar.activation(gate[:, u, :, :], gate[:, u, :, :], ACT.Exp).then_inc(gated, 1)
            with act.Fori(0, NT // 2) as i:
                for u in range(2):
                    one(2 * i + u, u)

        @block.vector
        def _(dve):
            link = Chain(dve, chain)
            nc.vector.memset(qd[:], 0.0).then_inc(cleared, 1)
            dve.wait_ge(m_ld, 16)

            def logit(c, u, turn):
                dve.wait_ge(c_ld[u], 16 * LOADS * turn + 16 * LOADS)
                for n in range(UNITS):
                    op = nc.vector.scalar_tensor_tensor(
                        out=gate[:, u, n, :], in0=ur[:, u, n, :],
                        scalar=cols[:, bass.ds(c, 1), KEY, n], in1=mask[:, n // C_HEADS, :],
                        op0=ALU.add, op1=ALU.add)
                op.then_inc(logits, 1)

            def mix(c, u):
                dve.wait_ge(scored, c + 1)
                dve.wait_ge(gated, c + 1)
                for way in range(2):
                    span = slice(way * C_HEADS, (way + 1) * C_HEADS)
                    nc.vector.tensor_tensor(mt[:, span, :].rearrange("p n t -> p (n t)"),
                                            ps[:, 0:2, :].rearrange("p b t -> p (b t)")[:, 0:C_HEADS * P],
                                            gate[:, u, span, :].rearrange("p n t -> p (n t)"), ALU.mult).then_inc(mixed, 1)

            def finish(c, u):
                stat = lambda f, lo, hi: cols[:, bass.ds(c, 1), f, lo:hi].rearrange("p o n -> p (o n)")
                link.turn(5 * c)
                dve.wait_ge(inter, c + 1)
                dve.wait_ge(y_done, c + 1)
                for way in range(2):
                    lo = way * C_HEADS
                    nc.vector.tensor_tensor(
                        num[:, u, lo:lo + C_HEADS, :].rearrange("p (q h) e -> p q h e", h=2),
                        ps[:, 4:7, way * PV:(way + 1) * PV].rearrange("p q (h e) -> p q h e", h=2),
                        stat(INTER, lo, lo + C_HEADS).rearrange("p (q h) -> p q h", h=2).unsqueeze(3)
                        .to_broadcast([P, PAIRS_C, 2, SV]), ALU.mult).then_inc(inter_free, 1)
                dve.wait_ge(inter_free, 2 * c + 2)
                dve.wait_ge(intra, c + 1)
                link(nc.vector.tensor_tensor(num[:, u, :, :].rearrange("p (w h) e -> p w (h e)", w=2),
                                             num[:, u, :, :].rearrange("p (w h) e -> p w (h e)", w=2),
                                             ps[:, 2:4, 0:C_HEADS * SV], ALU.add))
                norm = num[:, u, :, HD:SV].rearrange("p n o -> p (n o)")
                link(nc.vector.scalar_tensor_tensor(out=den[:, u, :], in0=norm, scalar=-1.0, in1=norm,
                                                    op0=ALU.mult, op1=ALU.max))
                link(nc.vector.tensor_tensor(den[:, u, :], den[:, u, :], stat(FLOOR, 0, UNITS), ALU.max))
                link(nc.vector.reciprocal(den[:, u, :], den[:, u, :]))
                link(nc.vector.tensor_tensor(both[:, u, :, :], num[:, u, :, 0:HD],
                                             den[:, u, :].unsqueeze(2).to_broadcast([P, UNITS, HD]), ALU.mult))

            def first():
                logit(0, 0, 0)
                mix(0, 0)

            def body(c, u, i, more):
                if more:
                    logit(c + 1, 1 - u, i + u)
                finish(c, u)
                if more:
                    mix(c + 1, 1 - u)
            over_chunks(dve, first, body)

        @block.gpsimd
        def _(pool):
            pool.sem_inc(y_done, 2)
            with pool.Fori(0, NT // 2) as i:
                for u in range(2):
                    c = 2 * i + u
                    pool.wait_ge(chain, 5 * c + 5)
                    pool.wait_ge(y_st[u], 16 * i + 16)
                    nc.gpsimd.tensor_tensor(yt[:, u, :].rearrange("p (h e) -> p h e", e=HD), both[:, u, 0:C_HEADS, :],
                                            both[:, u, C_HEADS:, :], ALU.add).then_inc(y_done, 1)


def mlstm(k, l, s):
    with ExitStack() as st:
        sb = k.buffers(st)
        cols = sb("cols", [P, NT, 4, UNITS])
        v1 = sb("v1", [P, NT, C_HEADS, SV])
        knat = sb("knat", [P, NT, C_HEADS * HD])
        mlstm_gates(k, l, s, cols, knat, v1)
        states = sb("states", [P, NT, 2, PAIRS_C, PV])
        mlstm_states(k, l, s, cols, knat, v1, states)
        mlstm_outputs(k, l, s, cols, v1, states)


def window(k, l, s):
    nc, io, d, ps = k.nc, k.io, k.d, k.ps
    SCALE = HD ** -0.5
    NK = CTX + 3 * WIN
    with ExitStack() as st:
        sb = k.buffers(st)
        masks = sb("masks", [P, 3, 3 * WIN])
        maskb = sb("maskb", [P, 3, 3 * WIN], BF16)
        identb = sb("identb", [P, P], BF16)
        kx, vx = sb("kx", [P, CTX]), sb("vx", [P, 2, P])
        sink, nsink = sb("sink", [P, A_HEADS]), sb("nsink", [P, A_HEADS])
        qt = sb("qt", [P, 2, A_HEADS, P])
        kw = sb("kw", [P, 2, 3 * WIN])
        vw = sb("vw", [P, 2, 3, P])
        pr = sb("pr", [P, A_HEADS, NK])
        pt = sb("pt", [P, 2, 5, 2 * P])
        mx, nm, sums, es, rs = (sb(n, [P, 2, A_HEADS]) for n in ("mx", "nm", "sums", "es", "rs"))
        ot = sb("ot", [P, 2 * P])
        yt = sb("yt", [P, 2, A_HEADS * HD])
        block = st.enter_context(nc.Block())
        c_ld, ld, y_st, cleared, scored, maxed, chain, weighed, turned, ev_a, ev_d, summed, o_out, back, y_done = (
            s[n] for n in ("c_ld", "ld", "y_st", "cleared", "scored", "maxed", "chain", "weighed", "turned", "ev_a",
                           "ev_d", "summed", "o_out", "back", "y_done"))
        banks = lambda nk: {t: (4 + t // 2, (t % 2) * 256) for t in range(5)} if nk == 5 else {0: (4, 0), 1: (5, 0)}

        def blocks(eng, body, last):
            for u in range(2):
                body(u, u, 0, 5, 1 - (u == 0), u > 0)
            with eng.Fori(1, NTL // 2 - 1) as i:
                for u in range(2):
                    body(2 * i + u, u, i, 5, 1, True)
            for u in range(2):
                body(NTL - 2 + u, u, NTL // 2 - 1, 5, 1 + u, True)
            for u in range(2):
                body(NTL + u, u, NTL // 2, 2, None, True)
            last(NT, 2)

        @block.sync
        def _(sp):
            sp.dma_start(masks[:], io["window"]).then_inc(c_ld, 16)
            sp.dma_start(kx[:], d["ka"][:, CTX0:CTX0 + CTX]).then_inc(c_ld, 16)
            sp.dma_start(vx[:], d["va"][CTX0:CTX0 + CTX, :].rearrange("(c p) v -> p c v", p=P)).then_inc(c_ld, 16)
            sp.dma_start(sink[:], io["attn_sink"][l, :].partition_broadcast(P)).then_inc(c_ld, 16)
            sp.wait_ge(cleared, 1)

            def load(n, u, local):
                for g in range(A_KV):
                    sp.dma_start(qt[64 * g:64 * g + 64, u, 2 * g:2 * g + 2, :],
                                 d["qa"][g, :, bass.ds(n * P, P)].rearrange("(h e) t -> e h t", e=HD)).then_inc(ld[u], 16)
                if local:
                    sp.dma_start(kw[:, u, :], d["ka"][:, bass.ds(n * P, 3 * WIN)]).then_inc(ld[u], 16)
                    sp.dma_start(vw[:, u, :, :], d["va"][bass.ds(n * P, 3 * WIN), :].rearrange("(c p) v -> p c v", p=P)
                                 ).then_inc(ld[u], 16)

            def store(n, u):
                sp.wait_ge(y_done, n + 1)
                sp.dma_start(d["y"][bass.ds(n * P, P), 0:A_HEADS * HD], yt[:, u, :]).then_inc(y_st[u], 16)
            for u in range(2):
                sp.sem_inc(y_st[u], 16)
                load(u, u, True)

            def turn(i, local):
                for u in range(2):
                    sp.wait_ge(summed, 4 * i + (2 * u + 4))
                    load(2 * i + (u + 2), u, local)
                    store(2 * i + u, u)
            with sp.Fori(0, NTL // 2 - 1) as i:
                turn(i, True)
            turn(NTL // 2 - 1, False)
            for u in range(2):
                store(NTL + u, u)
            for u in range(2):
                sp.wait_ge(y_st[u], 16 + 16 * (NT // 2))

        @block.tensor
        def _(pe):
            pe.sem_inc(summed, 2)
            pe.sem_inc(turned, 2)
            pe.wait_ge(maxed, 1)
            pe.wait_ge(c_ld, 64)

            def score(n, u, g, nk, mask):
                for h in (2 * g, 2 * g + 1):
                    q = qt[:, u, h, :]
                    b = 2 * (h % 2)
                    pe.wait_ge(weighed, 4 * n + (h + 1))
                    mm = nc.tensor.matmul(ps[:, b, 0:CTX], q, kx[:], start=True, stop=True)
                    if nk == 5:
                        for dst, w in ((ps[:, b, CTX:512], slice(0, 256)), (ps[:, b + 1, 0:P], slice(256, 384))):
                            nc.tensor.matmul(dst, q, kw[:, u, w], start=True, stop=False)
                            mm = nc.tensor.matmul(dst, identb[:], maskb[:, mask, w], start=False, stop=True)
                    mm.then_inc(scored, 1)

            def turn(n, g, nk, more=None):
                pe.wait_ge(weighed, 4 * n + (2 * g + 4))
                pe.wait_ge(ev_a, 2 * n + (g + 1))
                pe.wait_ge(ev_d, 2 * n + (g + 1))
                for t in range(nk):
                    bank, at = banks(nk)[t]
                    if t == 4 and more is not None:
                        pe.wait_ge(y_done, more)
                    for h in range(2):
                        tr = nc.tensor.transpose(ps[:, bank, at + h * P:at + (h + 1) * P],
                                                 pr[:, 2 * g + h, t * P:(t + 1) * P], k.ident[:])
                tr.then_inc(turned, 1)

            def values(n, u, g, nk):
                pe.wait_ge(ev_a, 2 * n + (g + 2))
                pe.wait_ge(ev_d, 2 * n + (g + 2))
                if g == 0:
                    pe.wait_ge(o_out, n + 1)
                for t in range(nk):
                    v = vx[:, t, 64 * g:64 * g + 64] if t < 2 else vw[:, u, t - 2, 64 * g:64 * g + 64]
                    mm = nc.tensor.matmul(ps[64 * g:64 * g + 64, 7, 0:2 * P], v, pt[:, g, t, :],
                                          start=(t == 0), stop=(t == nk - 1))
                mm.then_inc(summed, 1)

            def turn_back(n):
                pe.wait_ge(o_out, n + 2)
                for h in range(2):
                    tr = nc.tensor.transpose(ps[:, 6, 256 + h * P:256 + (h + 1) * P], ot[:, h * P:(h + 1) * P], k.ident[:])
                tr.then_inc(back, 1)

            def body(n, u, i, nk, mask, before):
                pe.wait_ge(ld[u], 64 * i + (64 if nk == 5 else 32))
                score(n, u, 0, nk, mask)
                if before:
                    pnk = 2 if (nk == 2 and u == 1) else 5
                    turn(n - 1, 1, pnk)
                    values(n - 1, 1 - u, 1, pnk)
                score(n, u, 1, nk, mask)
                if before:
                    turn_back(n - 1)
                turn(n, 0, nk, n if before else None)
                values(n, u, 0, nk)

            def last(n, nk):
                turn(n - 1, 1, nk)
                values(n - 1, 1, 1, nk)
                turn_back(n - 1)
            blocks(pe, body, last)

        @block.scalar
        def _(act):
            act.sem_inc(ev_a, 1)
            act.sem_inc(weighed, 2)

            def weigh(n, u, h, nk):
                act.wait_ge(maxed, 4 * n + (h + 2))
                act.wait_ge(turned, 2 * n + (h // 2 + 1))
                width = NK if nk == 5 else CTX
                nc.scalar.activation(es[:, u, h:h + 1], sink[:, h:h + 1], ACT.Exp, bias=nm[:, u, h:h + 1])
                nc.scalar.activation(pr[:, h, 0:width], ps[:, 2 * (h % 2):2 * (h % 2) + 2, :].rearrange("p b t -> p (b t)")[:, 0:width],
                                     ACT.Exp, bias=nm[:, u, h:h + 1], scale=SCALE,
                                     accum_out=sums[:, u, h:h + 1]).then_inc(weighed, 1)

            def move(n, g, nk):
                act.wait_ge(turned, 2 * n + (g + 3))
                act.wait_ge(summed, 2 * n + (g + 1))
                if nk == 5:
                    nc.scalar.copy(pt[:, g, 4, :], ps[:, 6, 0:256])
                    nc.scalar.copy(pt[:, g, 0:2, :].rearrange("p t q -> p (t q)"), ps[:, 4, :]).then_inc(ev_a, 1)
                else:
                    nc.scalar.copy(pt[:, g, 0, :], ps[:, 4, 0:256]).then_inc(ev_a, 1)

            def body(n, u, i, nk, mask, before):
                weigh(n, u, 0, nk)
                weigh(n, u, 1, nk)
                if before:
                    move(n - 1, 1, 2 if (nk == 2 and u == 1) else 5)
                weigh(n, u, 2, nk)
                weigh(n, u, 3, nk)
                move(n, 0, nk)
            blocks(act, body, lambda n, nk: move(n - 1, 1, nk))

        @block.vector
        def _(dve):
            link = Chain(dve, chain)
            nc.vector.memset(qt[:], 0.0).then_inc(cleared, 1)
            dve.wait_ge(c_ld, 64)
            nc.vector.tensor_copy(maskb[:], masks[:])
            nc.vector.tensor_copy(identb[:], k.ident[:])
            nc.vector.tensor_scalar(nsink[:], sink[:], -1.0, None, ALU.mult).then_inc(maxed, 1)
            dve.wait_ge(maxed, 1)
            dve.sem_inc(ev_d, 1)
            dve.sem_inc(o_out, 1)

            def most(n, u, h, nk):
                dve.wait_ge(scored, 4 * n + (h + 1))
                width = NK if nk == 5 else CTX
                link(nc.vector.reduce_max(mx[:, u, h:h + 1], ps[:, 2 * (h % 2):2 * (h % 2) + 2, :].rearrange("p b t -> p (b t)")[:, 0:width], AX.X))
                nc.vector.tensor_scalar(nm[:, u, h:h + 1], mx[:, u, h:h + 1], -SCALE, nsink[:, h:h + 1],
                                        ALU.mult, ALU.min).then_inc(maxed, 1)

            def move(n, g, nk):
                dve.wait_ge(turned, 2 * n + (g + 3))
                dve.wait_ge(summed, 2 * n + (g + 1))
                if nk == 5:
                    nc.vector.tensor_copy(pt[:, g, 2:4, :].rearrange("p t q -> p (t q)"), ps[:, 5, :]).then_inc(ev_d, 1)
                else:
                    nc.vector.tensor_copy(pt[:, g, 1, :], ps[:, 5, 0:256]).then_inc(ev_d, 1)

            def take_sums(n):
                dve.wait_ge(summed, 2 * n + 4)
                dve.wait_ge(back, n) if not isinstance(n, int) or n > 0 else None
                nc.vector.tensor_copy(ot[:], ps[:, 7, 0:2 * P]).then_inc(o_out, 1)

            def finish(n, u, turn_of):
                dve.wait_ge(weighed, 4 * n + 6)
                link(nc.vector.tensor_tensor(rs[:, u, :], sums[:, u, :], es[:, u, :], ALU.add))
                link(nc.vector.reciprocal(rs[:, u, :], rs[:, u, :]))
                dve.wait_ge(back, n + 1)
                dve.wait_ge(y_st[u], turn_of)
                nc.vector.tensor_tensor(
                    yt[:, u, :].rearrange("p (g h e) -> p h g e", g=2, h=2),
                    ps[:, 6, 256:512].rearrange("p (h g e) -> p h g e", h=2, g=2),
                    rs[:, u, :].rearrange("p (g h) -> p h g", g=2).unsqueeze(3).to_broadcast([P, 2, 2, HD]),
                    ALU.mult).then_inc(y_done, 1)

            def body(n, u, i, nk, mask, before):
                link.turn(6 * n - 2 if before else 0)
                most(n, u, 0, nk)
                most(n, u, 1, nk)
                if before:
                    move(n - 1, 1, 2 if (nk == 2 and u == 1) else 5)
                    take_sums(n - 1)
                most(n, u, 2, nk)
                most(n, u, 3, nk)
                if before:
                    finish(n - 1, 1 - u, 16 * i + 16 * u)
                move(n, 0, nk)

            def last(n, nk):
                link.turn(6 * n - 2)
                move(n - 1, 1, nk)
                take_sums(n - 1)
                finish(n - 1, 1, 16 * (NT // 2))
            blocks(dve, body, last)


GQ = 512
GB = GQ // P
NG = SEQ // GQ
PIECES = ((0, 4), (4, 4), (8, 4), (12, 4), (16, 2))
HALVES = ((0, 1024, (0, 1)), (1024, TOK, (2, 3, 4)))


def stack_loads(sp, sem, d, dst_q, dst_k, h, m, q_span, k_span):
    rows = bass.ds(h * (2 * B_QK) + m * B_QK, B_QK)
    q = lambda part: d["qkb"][0, part, rows, q_span]
    kk = lambda part: d["qkb"][1, part, rows, k_span]
    for dst, part, order in ((dst_q, q, ((0, 0, 1, 1), (0, 1, 2, 2))), (dst_k, kk, ((0, 1, 0, 1), (2, 2, 0, 1)))):
        for a in range(2):
            for n in range(4):
                sp.dma_start(dst(m, a)[B_QK * n:B_QK * n + B_QK], part(order[a][n])).then_inc(sem, 16)


STACK_LOADS = 32


def lambdas(k, l, s, nlam):
    nc, io = k.nc, k.io
    with ExitStack() as st:
        sb = k.buffers(st)
        lv, pv, e, li = sb("lv", [P, 4, B_QK]), sb("pv", [P, 2, B_QK]), sb("e", [P, 2]), sb("li", [P, 1])
        ld, steps, exps = s["lam_ld"], s["lam_steps"], s["lam_exps"]
        block = st.enter_context(nc.Block())

        @block.sync
        def _(sp):
            sp.dma_start(lv[:], io["diff_lambda"][l, :, :].partition_broadcast(P)).then_inc(ld, 16)
            sp.dma_start(li[:], io["lam_init"][l, 0:1].partition_broadcast(P)).then_inc(ld, 16)

        @block.vector
        def _(dve):
            link = Chain(dve, steps)
            dve.wait_ge(ld, 32)
            pairs = lv[:].rearrange("p (a b) e -> p a b e", b=2)
            link(nc.vector.tensor_tensor(pv[:], pairs[:, :, 0, :], pairs[:, :, 1, :], ALU.mult))
            link(nc.vector.reduce_sum(e[:], pv[:], AX.X))
            dve.wait_ge(exps, 1)
            link(nc.vector.tensor_tensor(e[:, 1:2], e[:, 1:2], e[:, 0:1], ALU.subtract))
            link(nc.vector.tensor_tensor(nlam[:], e[:, 1:2], li[:], ALU.subtract))

        @block.scalar
        def _(act):
            act.wait_ge(steps, 2)
            nc.scalar.activation(e[:], e[:], ACT.Exp).then_inc(exps, 1)


def differential(k, l, s, nlam):
    nc, io, d, ps = k.nc, k.io, k.d, k.ps
    SCALE = B_QK ** -0.5
    with ExitStack() as st:
        sb = k.buffers(st)
        kst = sb("kst", [P, 2, 2, 2, TOK], BF16)
        qst = sb("qst", [P, 2, 2, 2, SEQ], BF16)
        vt = sb("vt", [P, NT, HD])
        pr = sb("pr", [P, 2, 2, TOK])
        pt = sb("pt", [P, NT, GQ])
        mx = sb("mx", [P, 2, 2, 2])
        nm, rl, ls = (sb(n, [P, 2, 2]) for n in ("nm", "rl", "ls"))
        sums = sb("sums", [P, 2, 2, 2])
        cc = sb("cc", [P, 2, 1])
        r0, r_old = sb("r0", [P, GB]), sb("r_old", [P, GB])
        ot = sb("ot", [P, GQ])
        yt = sb("yt", [P, GB, HD])
        block = st.enter_context(nc.Block())
        v_ready, s_ld, v_ld, y_st, cleared, scored, maxed, chain, weighed, mixed, turned, ev_a, ev_d, summed, o_out, back, y_done = (
            s[n] for n in ("v_ready", "s_ld", "v_ld", "y_st", "cleared", "scored", "maxed", "chain", "weighed", "mixed", "turned",
                           "ev_a", "ev_d", "summed", "o_out", "back", "y_done"))
        STEPS = 5 * GB + 1

        def groups(eng, body):
            body(0, 0, 0, 0, False)
            with eng.Fori(1, NG) as g:
                body(0, 0, g, g, True)
            with eng.Fori(0, NG) as g:
                body(1, 1, g, NG + g, True)
            with eng.Fori(1, B_HEADS // 2) as i:
                for u in range(2):
                    with eng.Fori(0, NG) as g:
                        body(2 * i + u, u, g, i * (2 * NG) + g + u * NG, True)

        @block.sync
        def _(sp):
            def stacks(h, hs):
                for m in range(2):
                    stack_loads(sp, s_ld, d, lambda m, a: qst[:, hs, m, a, :], lambda m, a: kst[:, hs, m, a, :],
                                h, m, slice(0, SEQ), slice(0, TOK))

            def values(h):
                sp.dma_start(vt[:], d["nat"][:, bass.ds(h * HD + VB, HD)].rearrange("(c p) v -> p c v", p=P)).then_inc(v_ld, 16)

            def store(h, g, w):
                sp.wait_ge(y_done, w + 2)
                sp.dma_start(d["y"][bass.ds(g * GQ, GQ), bass.ds(h * HD + 256, HD)].rearrange("(b p) e -> p b e", p=P),
                             yt[:]).then_inc(y_st, 16)

            sp.sem_inc(y_st, 16)
            values(0)
            stacks(0, 0)
            sp.wait_ge(v_ld, 16)
            sp.sem_inc(v_ready, NG)
            sp.wait_ge(s_ld, 16 * STACK_LOADS)
            stacks(1, 1)

            def head(h, hs, w0, values_next, stacks_next):
                with sp.Fori(0, NG - 1) as g:
                    store(h, g, w0 + g)
                if values_next:
                    sp.wait_ge(summed, w0 + NG)
                    values(h + 1)
                    if stacks_next:
                        sp.wait_ge(s_ld, 16 * STACK_LOADS * (h + 2))
                        stacks(h + 2, hs)
                    sp.wait_ge(v_ld, 16 * (h + 2))
                    sp.sem_inc(v_ready, NG)
                store(h, NG - 1, w0 + (NG - 1))
            head(0, 0, 0, True, True)
            head(1, 1, NG, True, True)
            head(2, 0, 2 * NG, True, True)
            head(3, 1, 3 * NG, True, True)
            head(4, 0, 4 * NG, True, False)
            head(5, 1, 5 * NG, False, False)
            sp.wait_ge(y_st, 16 + 16 * NG * B_HEADS)

        @block.tensor
        def _(pe):
            pe.wait_ge(cleared, 1)

            def score(n, hs, g, b, m):
                unit = 4 * n + 2 * m
                for half, (lo, hi, banks) in enumerate(HALVES):
                    pe.wait_ge(weighed, unit + (half + 1))
                    for bank in banks:
                        w = min(512, TOK - 512 * bank)
                        for a in range(2):
                            mm = nc.tensor.matmul(ps[:, bank, 0:w], qst[:, hs, m, a, bass.ds(g * GQ + b * P, P)],
                                                  kst[:, hs, m, a, 512 * bank:512 * bank + w],
                                                  start=(a == 0), stop=(a == 1))
                    mm.then_inc(scored, 1)

            def turn(n, b, pieces):
                for j in pieces:
                    t0, nt = PIECES[j]
                    if j == 0:
                        pe.wait_ge(mixed, 2 * n + 1)
                    if j == 2:
                        pe.wait_ge(mixed, 2 * n + 2)
                    if j < 4:
                        pe.wait_ge(ev_a, 4 * n + {0: 4, 1: 3, 2: 5, 3: 6}[j])
                    else:
                        pe.wait_ge(ev_d, n + 1)
                    for t in range(nt):
                        tr = nc.tensor.transpose(ps[:, 5 + j % 2, t * P:(t + 1) * P],
                                                 pr[:, b % 2, 0, (t0 + t) * P:(t0 + t + 1) * P], k.ident[:])
                    tr.then_inc(turned, 1)

            def values(w):
                pe.wait_ge(v_ready, w + 1)
                pe.wait_ge(ev_a, 16 * w + 20)
                pe.wait_ge(ev_d, 4 * w + 4)
                pe.wait_ge(y_done, w + 1)
                for t in range(NT):
                    mm = nc.tensor.matmul(ps[0:HD, 7, 0:GQ], vt[:, t, :], pt[:, t, :], start=(t == 0), stop=(t == NT - 1))
                mm.then_inc(summed, 1)

            def turn_back(w):
                pe.wait_ge(o_out, w + 1)
                for b in range(GB):
                    tr = nc.tensor.transpose(ps[:, 7, b * P:(b + 1) * P], ot[:, b * P:(b + 1) * P], k.ident[:])
                tr.then_inc(back, 1)

            def body(h, hs, g, w, before):
                pe.wait_ge(s_ld, 16 * STACK_LOADS * h + 16 * STACK_LOADS)
                for b in range(GB):
                    n = 4 * w + b
                    prev = b > 0 or before
                    score(n, hs, g, b, 0)
                    if b == 1 and before:
                        turn_back(w - 1)
                    if prev:
                        turn(n - 1, b - 1, (0, 1, 2))
                    score(n, hs, g, b, 1)
                    if prev:
                        turn(n - 1, b - 1, (3, 4))
                    if b == 0 and before:
                        values(w - 1)

            groups(pe, body)
            w = NG * B_HEADS
            turn(4 * w - 1, GB - 1, range(5))
            values(w - 1)
            turn_back(w - 1)

        @block.scalar
        def _(act):
            act.sem_inc(weighed, 2)
            act.sem_inc(ev_a, 4)

            def weigh(n, b, m):
                act.wait_ge(maxed, 2 * n + (m + 1))
                for half, (lo, hi, banks) in enumerate(HALVES):
                    nc.scalar.activation(pr[:, b % 2, m, lo:hi], ps[:, 0:5, :].rearrange("p b t -> p (b t)")[:, lo:hi],
                                         ACT.Exp, bias=nm[:, b % 2, m:m + 1], scale=SCALE,
                                         accum_out=sums[:, b % 2, m, half:half + 1]).then_inc(weighed, 1)

            def move(n, b, pieces):
                for j in pieces:
                    t0, nt = PIECES[j]
                    act.wait_ge(turned, 5 * n + (j + 1))
                    nc.scalar.copy(pt[:, t0:t0 + nt, b * P:(b + 1) * P],
                                   ps[:, 5 + j % 2, 0:nt * P].rearrange("p (t q) -> p t q", q=P)).then_inc(ev_a, 1)

            def body(h, hs, g, w, before):
                for b in range(GB):
                    n = 4 * w + b
                    prev = b > 0 or before
                    weigh(n, b, 0)
                    if prev:
                        if b == 1 and before:
                            act.wait_ge(summed, w)
                        move(n - 1, (b - 1) % GB, (0, 1))
                    weigh(n, b, 1)
                    if prev:
                        move(n - 1, (b - 1) % GB, (3, 4))
            groups(act, body)
            move(4 * NG * B_HEADS - 1, GB - 1, (0, 1, 3, 4))

        @block.vector
        def _(dve):
            link = Chain(dve, chain)
            nc.vector.memset(ot[:], 0.0).then_inc(cleared, 1)
            nc.vector.memset(r0[:], 1.0).then_inc(cleared, 1)
            dve.wait_ge(cleared, 2)
            dve.sem_inc(y_done, 1)

            def most(n, b, m):
                for half, (lo, hi, banks) in enumerate(HALVES):
                    dve.wait_ge(scored, 4 * n + (2 * m + half + 1))
                    op = nc.vector.reduce_max(mx[:, b % 2, m, half:half + 1],
                                              ps[:, 0:5, :].rearrange("p b t -> p (b t)")[:, lo:hi], AX.X)
                link(op)
                nc.vector.tensor_scalar(nm[:, b % 2, m:m + 1], mx[:, b % 2, m, 0:1], mx[:, b % 2, m, 1:2], -SCALE,
                                        ALU.max, ALU.mult).then_inc(maxed, 1)

            def mix(n, b):
                v = b % 2
                dve.wait_ge(weighed, 4 * n + 6)
                link(nc.vector.tensor_tensor(ls[:, v, :], sums[:, v, :, 0], sums[:, v, :, 1], ALU.add))
                link(nc.vector.reciprocal(rl[:, v, :], ls[:, v, :]))
                nc.vector.tensor_copy(r0[:, b:b + 1], rl[:, v, 0:1])
                link(nc.vector.scalar_tensor_tensor(out=cc[:, v, :], in0=ls[:, v, 0:1], scalar=nlam[:], in1=rl[:, v, 1:2],
                                                    op0=ALU.mult, op1=ALU.mult))
                for lo, hi, _ in HALVES:
                    nc.vector.scalar_tensor_tensor(out=pr[:, v, 0, lo:hi], in0=pr[:, v, 1, lo:hi], scalar=cc[:, v, :],
                                                   in1=pr[:, v, 0, lo:hi], op0=ALU.mult, op1=ALU.add).then_inc(mixed, 1)

            def move(n, b):
                t0, nt = PIECES[2]
                dve.wait_ge(turned, 5 * n + 3)
                nc.vector.tensor_copy(pt[:, t0:t0 + nt, b * P:(b + 1) * P],
                                      ps[:, 5, 0:nt * P].rearrange("p (t q) -> p t q", q=P)).then_inc(ev_d, 1)

            def take_sums(w):
                dve.wait_ge(summed, w + 1)
                nc.vector.tensor_copy(ot[0:HD, :], ps[0:HD, 7, :]).then_inc(o_out, 1)

            def finish(w):
                dve.wait_ge(back, w + 1)
                dve.wait_ge(y_st, 16 * w + 16)
                nc.vector.tensor_tensor(yt[:], ps[:, 7, :].rearrange("p (b t) -> p b t", b=GB)[:, :, 0:HD],
                                        r_old[:].unsqueeze(2).to_broadcast([P, GB, HD]), ALU.mult).then_inc(y_done, 1)

            def body(h, hs, g, w, before):
                link.turn(w * STEPS)
                for b in range(GB):
                    n = 4 * w + b
                    prev = b > 0 or before
                    most(n, b, 0)
                    if b == 0:
                        link(nc.vector.tensor_copy(r_old[:], r0[:]))
                    if b == 1 and before:
                        take_sums(w - 1)
                    if prev:
                        if b == 1 and before:
                            dve.wait_ge(summed, w)
                        move(n - 1, (b - 1) % GB)
                    if b == 2 and before:
                        finish(w - 1)
                    most(n, b, 1)
                    mix(n, b)
                assert link.n == STEPS
            groups(dve, body)
            w = NG * B_HEADS
            link.turn(w * STEPS)
            link(nc.vector.tensor_copy(r_old[:], r0[:]))
            move(4 * w - 1, GB - 1)
            take_sums(w - 1)
            finish(w - 1)


def differential_context(k, l, s, nlam):
    nc, io, d, ps = k.nc, k.io, k.d, k.ps
    SCALE = B_QK ** -0.5
    QB = CTX // P
    with ExitStack() as st:
        sb = k.buffers(st)
        kst = sb("kst", [P, 2, 2, 2, CTX], BF16)
        qst = sb("qst", [P, 2, 2, 2, CTX], BF16)
        vt = sb("vt", [P, 2, QB, HD])
        pr = sb("pr", [P, QB, 2, CTX])
        pt = sb("pt", [P, QB, CTX])
        mx, nm, sums, rl = (sb(n, [P, QB, 2]) for n in ("mx", "nm", "sums", "rl"))
        cc = sb("cc", [P, QB, 1])
        ot = sb("ot", [P, CTX])
        yt = sb("yt", [P, QB, B_HEADS, HD])
        block = st.enter_context(nc.Block())
        s_ld, y_st, cleared, scored, chain, weighed, turned, summed, back = (
            s[n] for n in ("xs_ld", "xy_st", "x_cleared", "x_scored", "x_chain", "x_weighed", "x_turned", "x_summed", "x_back"))
        LOADS = STACK_LOADS + 1
        STEPS = 9
        ctx = slice(SEQ, TOK)

        def heads(eng, body):
            with eng.Fori(0, B_HEADS // 2) as i:
                for u in range(2):
                    body(2 * i + u, u, i)

        @block.sync
        def _(sp):
            def load(h, u):
                for m in range(2):
                    stack_loads(sp, s_ld[u], d, lambda m, a: qst[:, u, m, a, :], lambda m, a: kst[:, u, m, a, :], h, m, ctx, ctx)
                sp.dma_start(vt[:, u, :, :], d["nat"][SEQ:TOK, bass.ds(h * HD + VB, HD)].rearrange("(c p) v -> p c v", p=P)
                             ).then_inc(s_ld[u], 16)
            for u in range(2):
                load(u, u)
            with sp.Fori(0, B_HEADS // 2 - 1) as i:
                for u in range(2):
                    sp.wait_ge(summed, 2 * i + (u + 1))
                    load(2 * i + (u + 2), u)
            sp.wait_ge(chain, STEPS * B_HEADS)
            sp.dma_start(d["y"][ctx, 256:640].rearrange("(b p) e -> p b e", p=P),
                         yt[:].rearrange("p b h e -> p b (h e)")).then_inc(y_st, 16)
            sp.wait_ge(y_st, 16)

        @block.tensor
        def _(pe):
            pe.wait_ge(cleared, 1)

            def body(h, u, i):
                pe.wait_ge(s_ld[u], 16 * LOADS * i + 16 * LOADS)
                for b in range(QB):
                    for m in range(2):
                        for a in range(2):
                            mm = nc.tensor.matmul(ps[:, b, m * CTX:(m + 1) * CTX], qst[:, u, m, a, b * P:(b + 1) * P],
                                                  kst[:, u, m, a, :], start=(a == 0), stop=(a == 1))
                mm.then_inc(scored, 1)
                pe.wait_ge(chain, STEPS * h + 6)
                for t in range(QB):
                    for b in range(QB):
                        tr = nc.tensor.transpose(ps[:, 2, (2 * t + b) * P:(2 * t + b + 1) * P],
                                                 pr[:, b, 0, t * P:(t + 1) * P], k.ident[:])
                tr.then_inc(turned, 1)
                pe.wait_ge(chain, STEPS * h + 7)
                for t in range(QB):
                    mm = nc.tensor.matmul(ps[0:HD, 3, 0:CTX], vt[:, u, t, :], pt[:, t, :], start=(t == 0), stop=(t == QB - 1))
                mm.then_inc(summed, 1)
                pe.wait_ge(chain, STEPS * h + 8)
                for b in range(QB):
                    tr = nc.tensor.transpose(ps[:, 4, b * P:(b + 1) * P], ot[:, b * P:(b + 1) * P], k.ident[:])
                tr.then_inc(back, 1)
            heads(pe, body)

        @block.scalar
        def _(act):
            def body(h, u, i):
                act.wait_ge(chain, STEPS * h + 2)
                for b in range(QB):
                    for m in range(2):
                        nc.scalar.activation(pr[:, b, m, :], ps[:, b, m * CTX:(m + 1) * CTX], ACT.Exp,
                                             bias=nm[:, b, m:m + 1], scale=SCALE,
                                             accum_out=sums[:, b, m:m + 1]).then_inc(weighed, 1)
            heads(act, body)

        @block.vector
        def _(dve):
            link = Chain(dve, chain)
            nc.vector.memset(ot[:], 0.0).then_inc(cleared, 1)

            def body(h, u, i):
                link.turn(STEPS * h)
                dve.wait_ge(scored, h + 1)
                link(nc.vector.reduce_max(mx[:], ps[:, 0:QB, :].rearrange("p b (m t) -> p b m t", m=2), AX.X))
                link(nc.vector.tensor_scalar(nm[:], mx[:], -SCALE, None, ALU.mult))
                dve.wait_ge(weighed, 4 * h + 4)
                link(nc.vector.reciprocal(rl[:], sums[:]))
                for b in range(QB):
                    op = nc.vector.scalar_tensor_tensor(out=cc[:, b, :], in0=sums[:, b, 0:1], scalar=nlam[:],
                                                        in1=rl[:, b, 1:2], op0=ALU.mult, op1=ALU.mult)
                link(op)
                for b in range(QB):
                    link(nc.vector.scalar_tensor_tensor(out=pr[:, b, 0, :], in0=pr[:, b, 1, :], scalar=cc[:, b, :],
                                                        in1=pr[:, b, 0, :], op0=ALU.mult, op1=ALU.add))
                dve.wait_ge(turned, h + 1)
                link(nc.vector.tensor_copy(pt[:].rearrange("p t q -> p (t q)"), ps[:, 2, :]))
                dve.wait_ge(summed, h + 1)
                link(nc.vector.tensor_copy(ot[0:HD, :], ps[0:HD, 3, 0:CTX]))
                dve.wait_ge(back, h + 1)
                link(nc.vector.tensor_tensor(yt[:, :, bass.ds(h, 1), :].rearrange("p b o e -> p b (o e)"),
                                             ps[:, 4, 0:CTX].rearrange("p (b t) -> p b t", b=QB)[:, :, 0:HD],
                                             rl[:, :, 0:1].to_broadcast([P, QB, HD]), ALU.mult))
                assert link.n == STEPS
            heads(dve, body)


def output(k, l, s):
    nc, io, d, ps = k.nc, k.io, k.d, k.ps
    NH = B_HEADS + C_HEADS
    A = A_HEADS * HD
    W = 512
    with ExitStack() as st:
        sb = k.buffers(st)
        wo = sb("wo", [P, KT, DM])
        gn = sb("gn", [P, NH, HD])
        keep = sb("keep", [P, 1])
        gate = sb("gate", [P, 2, DM])
        lng, lnb = sb("lng", [P, DM]), sb("lnb", [P, DM])
        xt, yt, gt = (sb(n, [P, 2, DM]) for n in ("xt", "yt", "gt"))
        sq = sb("sq", [P, 2, NH, HD])
        ss, sr, rr = (sb(n, [P, 2, NH]) for n in ("ss", "sr", "rr"))
        yT = sb("yT", [P, 2, KT, P])
        res = sb("res", [P, 2, DM])
        ot = sb("ot", [P, 2, DM])
        bn = sb("bn", [P, 2, 2, 6])
        mv, sd = sb("mv", [P, 2, 2]), sb("sd", [P, 2, 2])
        block = st.enter_context(nc.Block())
        w_ld, ld, o_st, squared, steps, roots, gains, ready, turned, moved, prod, taken, centred, done = (
            s[n] for n in ("w_ld", "ld", "o_st", "squared", "steps", "roots", "gains", "ready", "turned", "moved",
                           "prod", "taken", "centred", "done"))
        PAIRS = NT // 2
        PRE, POST = 3, 5

        def tiles(eng, first, body):
            first()
            with eng.Fori(0, NTL // 2 - 1) as i:
                for u in range(2):
                    body(2 * i + u, u, i, 0, True)
            for u in range(2):
                body(NTL - 2 + u, u, PAIRS - 2, 0, True)
            for u in range(2):
                body(NTL + u, u, PAIRS - 1, 1, u == 0)

        @block.sync
        def _(sp):
            def load(t, u):
                rows = bass.ds(t * P, P)
                sp.dma_start(xt[:, u, :], d["x"][rows, :]).then_inc(ld[u], 16)
                sp.dma_start(yt[:, u, :], d["y"][rows, :]).then_inc(ld[u], 16)
                for lo, hi, src in ((0, A, SA), (A, A + 384, SB), (A + 384, DM, SC)):
                    sp.dma_start(gt[:, u, lo:hi], d["nat"][rows, src:src + hi - lo]).then_inc(ld[u], 16)

            def store(t, u, latent):
                sp.wait_ge(done, t + 3)
                sp.dma_start(d["x"][bass.ds(t * P, P), :], ot[:, u, :]).then_inc(o_st[u], 16)
                if latent:
                    sp.dma_start(k.out[bass.ds(t * P, P), :], ot[:, u, :]).then_inc(o_st[u], 16)
            for u in range(2):
                sp.sem_inc(o_st[u], 32)
                load(u, u)
            for h in range(B_HEADS):
                sp.dma_start(gn[:, h, :], io["diff_norm_g"][l, :].partition_broadcast(P)).then_inc(w_ld, 16)
            sp.dma_start(gn[:, B_HEADS:, :].rearrange("p h e -> p (h e)"), io["mlstm_norm_g"][l, :].partition_broadcast(P)).then_inc(w_ld, 16)
            sp.dma_start(keep[:], io["lam_keep"][l, 0:1].partition_broadcast(P)).then_inc(w_ld, 16)
            for r in range(2):
                sp.dma_start(gate[:, r, :], d["mod"][r, 2 * DM:].partition_broadcast(P)).then_inc(w_ld, 16)
            sp.dma_start(lng[:], io["ln_g"][l, :].partition_broadcast(P)).then_inc(w_ld, 16)
            sp.dma_start(lnb[:], io["ln_b"][l, :].partition_broadcast(P)).then_inc(w_ld, 16)
            sp.dma_start(wo[:], io["w_out"][l, :, :, :]).then_inc(w_ld, 16)

            def turn(i, more):
                for u in range(2):
                    store(2 * i + u, u, True)
                    if more:
                        load(2 * i + (u + 2), u)
            with sp.Fori(0, PAIRS - 1) as i:
                turn(i, True)
            for u in range(2):
                store(NTL + u, u, False)
            for u in range(2):
                sp.wait_ge(o_st[u], 32 + 32 * (PAIRS - 1) + 16)

        @block.tensor
        def _(pe):
            pe.sem_inc(turned, 1)

            def turn(t, u):
                pe.wait_ge(ready, t + 1)
                pe.wait_ge(moved, t + 1)
                for j in range(KT):
                    tr = nc.tensor.transpose(ps[:, j // 4, (j % 4) * P:(j % 4 + 1) * P], yt[:, u, j * P:(j + 1) * P], k.ident[:])
                tr.then_inc(turned, 1)

            def product(t, u):
                pe.wait_ge(moved, t + 2)
                pe.wait_ge(taken, t + 1)
                for n in range(DM // W):
                    for j in range(KT):
                        mm = nc.tensor.matmul(ps[:, 2 + 2 * u + n, :], yT[:, u, j, :], wo[:, j, n * W:(n + 1) * W],
                                              start=(j == 0), stop=(j == KT - 1))
                mm.then_inc(prod, 1)

            def first():
                turn(0, 0)
                pe.wait_ge(w_ld, 16 * (B_HEADS + 7))

            def body(t, u, i, r, more):
                if more:
                    turn(t + 1, 1 - u)
                product(t, u)
            tiles(pe, first, body)

        @block.gpsimd
        def _(pool):
            pool.sem_inc(done, 2)

            def before(t, u, i):
                pool.wait_ge(ld[u], 80 * i + 80)
                y = yt[:, u, A:].rearrange("p (h e) -> p h e", e=HD)
                nc.gpsimd.tensor_tensor(sq[:, u, :, :], y, y, ALU.mult).then_inc(squared, 1)
                g = gt[:, u, A:].rearrange("p (h e) -> p h e", e=HD)
                nc.gpsimd.tensor_tensor(g, g, gn[:], ALU.mult).then_inc(gains, 1)

            def after(t, u, i):
                pool.wait_ge(centred, t + 1)
                pool.wait_ge(o_st[u], 32 * i + 32)
                nc.gpsimd.tensor_tensor(ot[:, u, :], res[:, u, :], lng[:], ALU.mult).then_inc(s["scaled"], 1)
                pool.wait_ge(s["scaled"], t + 1)
                nc.gpsimd.tensor_tensor(ot[:, u, :], ot[:, u, :], lnb[:], ALU.add).then_inc(done, 1)

            def first():
                pool.wait_ge(s["gn_ready"], 1)
                before(0, 0, 0)

            def body(t, u, i, r, more):
                if more:
                    before(t + 1, 1 - u, i + u)
                after(t, u, i)
            tiles(pool, first, body)

        @block.scalar
        def _(act):
            act.sem_inc(moved, 1)

            def before(t, u):
                act.wait_ge(s["summed"], t + 1)
                nc.scalar.sqrt(sr[:, u, :], ss[:, u, :]).then_inc(roots, 1)
                act.wait_ge(turned, t + 2)
                for n in range(2):
                    op = nc.scalar.copy(yT[:, u, 4 * n:4 * n + 4, :].rearrange("p k t -> p (k t)"), ps[:, n, :])
                op.then_inc(moved, 1)

            def after(t, u):
                act.wait_ge(s["varied"], t + 1)
                nc.scalar.sqrt(sd[:, u, 0:1], mv[:, u, 1:2]).then_inc(s["rooted"], 1)

            def body(t, u, i, r, more):
                if more:
                    before(t + 1, 1 - u)
                after(t, u)
            tiles(act, lambda: before(0, 0), body)

        @block.vector
        def _(dve):
            dve.sem_inc(taken, 2)
            dve.wait_ge(w_ld, 16 * (B_HEADS + 7))
            gb = gn[:, 0:B_HEADS, :]
            nc.vector.tensor_scalar(gb, gb, keep[:], None, ALU.mult).then_inc(s["gn_ready"], 1)
            link = Chain(dve, steps)

            def before(t, u, i):
                dve.wait_ge(squared, t + 1)
                link(nc.vector.reduce_sum(ss[:, u, :], sq[:, u, :, :], AX.X))
                nc.vector.tensor_scalar(ss[:, u, :], ss[:, u, :], 1.0 / HD, EPS, ALU.mult, ALU.add).then_inc(s["summed"], 1)
                dve.wait_ge(roots, t + 1)
                link(nc.vector.reciprocal(rr[:, u, :], sr[:, u, :]))
                y = yt[:, u, A:].rearrange("p (h e) -> p h e", e=HD)
                link(nc.vector.tensor_tensor(y, y, rr[:, u, :].unsqueeze(2).to_broadcast([P, NH, HD]), ALU.mult))
                dve.wait_ge(gains, t + 1)
                nc.vector.tensor_tensor(yt[:, u, :], yt[:, u, :], gt[:, u, :], ALU.mult).then_inc(ready, 1)

            def after(t, u, r):
                dve.wait_ge(prod, t + 1)
                link(nc.vector.tensor_tensor(res[:, u, :], ps[:, 2 + 2 * u:4 + 2 * u, :].rearrange("p n w -> p (n w)"),
                                             gate[:, r, :], ALU.mult))
                dve.sem_inc(taken, 1)
                link(nc.vector.scalar_tensor_tensor(out=res[:, u, :], in0=xt[:, u, :], scalar=ALPHA, in1=res[:, u, :],
                                                    op0=ALU.mult, op1=ALU.add))
                for n in range(2):
                    op = nc.vector.bn_stats(bn[:, u, n, :], res[:, u, n * W:(n + 1) * W])
                link(op)
                nc.vector.memset(sd[:, u, 1:2], 0.0)
                link(nc.vector.bn_aggr(mv[:, u, :], bn[:, u, :, :].rearrange("p n s -> p (n s)")))
                nc.vector.tensor_scalar(mv[:, u, 1:2], mv[:, u, 1:2], EPS, None, ALU.add).then_inc(s["varied"], 1)
                dve.wait_ge(s["rooted"], t + 1)
                link(nc.vector.reciprocal(sd[:, u, 1:2], sd[:, u, 0:1]))
                nc.vector.tensor_scalar(res[:, u, :], res[:, u, :], mv[:, u, 0:1], sd[:, u, 1:2],
                                        ALU.subtract, ALU.mult).then_inc(centred, 1)

            def first():
                before(0, 0, 0)
                assert link.n == PRE

            def body(t, u, i, r, more):
                link.turn(PRE + (PRE + POST) * t if more else PRE * NT + POST * (NT - 1))
                if more:
                    before(t + 1, 1 - u, i + u)
                after(t, u, r)
                assert link.n == POST + (PRE if more else 0)
            tiles(dve, first, body)



def later_stages(k, l, stages):
    on = lambda name: stages is None or name in stages
    if on("c"):
        with ExitStack() as st:
            mlstm(k, l, k.semaphores(st, "mlstm", (
                "cleared", "g_ld", "v_ld", "gate_steps", "gate_exps", "row_st", "staged", "turned", "kept",
                "d_ld", "weighed", "prod", "stepped", "m_ld", "cleared2", "cleared3", "logits", "gated", "scored", "mixed",
                "intra", "inter", "inter_free", "den_steps", "ready", "y_done"), {"k_ld": 2, "c_ld": 2, "y_st": 2}))
    if on("a"):
        with ExitStack() as st:
            window(k, l, k.semaphores(st, "window", (
                "c_ld", "cleared", "scored", "maxed", "chain", "weighed", "turned", "ev_a", "ev_d", "summed", "o_out",
                "back", "y_done"), {"ld": 2, "y_st": 2}))
    if on("b"):
        with ExitStack() as st:
            nlam = st.enter_context(k.nc.sbuf_tensor("nlam", [P, 1], F32))
            s = k.semaphores(st, "diff", (
                "lam_ld", "lam_steps", "lam_exps", "v_ready", "s_ld", "v_ld", "y_st", "cleared", "scored", "maxed",
                "chain", "weighed", "mixed", "turned", "ev_a", "ev_d", "summed", "o_out", "back", "y_done", "xy_st",
                "x_cleared", "x_scored", "x_chain", "x_weighed", "x_turned", "x_summed", "x_back"), {"xs_ld": 2})
            lambdas(k, l, s, nlam)
            differential(k, l, s, nlam)
            differential_context(k, l, s, nlam)
    if on("o"):
        with ExitStack() as st:
            output(k, l, k.semaphores(st, "out", (
                "w_ld", "squared", "steps", "roots", "gains", "ready", "turned", "moved", "prod", "taken", "centred",
                "done", "scaled", "gn_ready", "summed", "varied", "rooted"), {"ld": 2, "o_st": 2}))


def more_constants():
    keep = np.ones((64, TOK), np.float32)
    keep[0:32, 0::P] = 0.0
    keep[32:64, P - 1::P] = 0.0
    t = np.arange(P)
    causal = np.stack([np.where(t[:, None] <= t[None], 0.0, NEG), np.where(t[:, None] >= t[None], 0.0, NEG)], 1)
    q, j = np.arange(P)[:, None], np.arange(3 * WIN)[None]
    near = np.abs(j - WIN - q) <= WIN
    window = np.stack([near & (j >= WIN), near, near & (j < 2 * WIN)], 1)
    lam = np.array([[0.8 - 0.6 * np.exp(-0.3 * n)] for n in range(DEPTH)])
    return {"lam_init": lam.astype(np.float32), "lam_keep": (1.0 - lam).astype(np.float32),
            "window": np.where(window, 0.0, NEG).astype(np.float32), "keep": keep, "causal": causal.astype(np.float32)}


def setup(k):
    nc, io, d = k.nc, k.io, k.d
    with ExitStack() as st:
        sb = k.buffers(st)
        zero = sb("zero", [P, A_KV * HD])
        cols = sb("cond", [P, KT, 2])
        x_cp, c_ld, i_ld, z_st, silu, cleared = k.semaphores(
            st, "setup", ("x_copied", "cond_ld", "ident_ld", "pad_st", "silu", "cleared")).values()
        block = st.enter_context(nc.Block())

        @block.sync
        def _(sp):
            sp.dma_start(k.ident[:], io["ident"]).then_inc(i_ld, 16)
            for r in range(2):
                sp.dma_start(cols[:, :, r], io["cond"][r, :].rearrange("(k p) -> p k", p=P),
                             allow_slow_non_contiguous=True).then_inc(c_ld, 16)
            sp.dma_start(d["x"][0:SEQ, :], io["x"]).then_inc(x_cp, 16)
            sp.dma_start(d["x"][SEQ:TOK, :], io["ctx"]).then_inc(x_cp, 16)
            sp.wait_ge(cleared, 1)
            for row in (0, CTX0 - WIN):
                sp.dma_start(d["va"][row:row + WIN, :], zero[:]).then_inc(z_st, 16)
                sp.dma_start(d["ka"][:, row:row + WIN], zero[:]).then_inc(z_st, 16)
            sp.wait_ge(x_cp, 32)
            sp.wait_ge(z_st, 64)
            sp.wait_ge(i_ld, 16)

        @block.vector
        def _(dve):
            nc.vector.memset(zero[:], 0.0).then_inc(cleared, 1)

        @block.scalar
        def _(act):
            act.wait_ge(c_ld, 32)
            nc.scalar.activation(k.silu_c[:], cols[:], ACT.Silu).then_inc(silu, 1)
            act.wait_ge(silu, 1)


def program(nc, io, out, d, stages):
    with ExitStack() as stack:
        k = Core(nc, stack, io, d)
        k.out = out
        k.ps = stack.enter_context(nc.psum_tensor("ps", [P, 8, 512], F32))
        k.ident = stack.enter_context(nc.sbuf_tensor("ident_sb", [P, P], F32))
        k.silu_c = stack.enter_context(nc.sbuf_tensor("silu_c", [P, KT, 2], F32))
        k.modc = stack.enter_context(nc.sbuf_tensor("modc", [P, 2, 2, KT], F32))
        setup(k)
        with nc.Fori(0, DEPTH if stages is None or "2" in stages else 1) as l:
            with ExitStack() as st:
                modulation(k, l, k.semaphores(st, "mod", ("b_ld", "done", "added", "stored", "cols_ld"), {"w_ld": 3}))
            with nc.sbuf_tensor("hT", [P, KT, TOK], F32) as hT:
                with ExitStack() as st:
                    natural_project(k, l, hT, k.semaphores(
                        st, "nat", ("turned", "h_ready", "kept", "prod", "evac", "v_free", "z_free", "n_ready"),
                        {"w_ld": NCH, "x_ld": 2, "n_st": 2}))
                latent_row = lambda t0: LAT0 + t0 if t0 < SEQ else CTX0
                ta = lambda i, u, b, t0, w, ob: [(d["qa"][u, :, t0:t0 + w], ob[:, 0, :])]
                tk = lambda i, u, b, t0, w, ob: [(d["ka"][:, latent_row(t0):latent_row(t0) + w], ob[:, 0, :])] if u == 0 else \
                    [(d["gates"][:, t0:t0 + w], ob[0:24, 0, :])]
                tb = lambda i, u, b, t0, w, ob: [
                    (d["qkb"][u, part, bass.ds(i * P, P), t0:t0 + w], ob[:, part, :]) for part in range(3)]
                tc = lambda i, u, b, t0, w, ob: [(d["qkc"][u, bass.ds(i * P, P), t0:t0 + w], ob[:, 0, :])]
                for kinds, first, pairs, out_of in ((("rope_a", "rope_a"), 0, 1, ta), (("rope_a", 1.0), 2, 1, tk),
                                                    (("rope_b", "rope_b"), 4, 3, tb), ((HD ** -0.5, 1.0), 10, 3, tc)):
                    with ExitStack() as st:
                        transposed_project(k, l, hT, k.semaphores(
                            st, "tr", ("tab_ld", "prod", "evac", "rot", "rot_free", "done", "chain"),
                            {"w_ld": 2, "o_st": 2}), kinds, first, pairs, out_of)
            later_stages(k, l, stages)


def constants():
    def tables(dim):
        nf = dim // 4
        inv = (np.float32(10000.0) ** (-np.arange(nf, dtype=np.float32) / nf)).astype(np.float32)
        tok = np.arange(SEQ)
        ar = (tok // GRID_W).astype(np.float32)[:, None] * inv
        ac = (tok % GRID_W).astype(np.float32)[:, None] * inv
        ang = np.concatenate([ar, ar, ac, ac], -1).T
        both = np.stack([np.cos(ang.astype(np.float64)), np.sin(ang.astype(np.float64))], 1).astype(np.float32)
        return np.tile(both, (P // dim, 1, 1))

    def rotation(dim):
        m = np.zeros((P, P), np.float32)
        q = dim // 4
        for j in range(P):
            if (j % dim) // q % 2 == 0:
                m[j + q, j] = -1.0
            else:
                m[j - q, j] = 1.0
        return m
    c = {"rope": np.stack([tables(HD), tables(B_QK)]), "perm": np.stack([rotation(HD), rotation(B_QK)]),
         "ident": np.eye(P, dtype=np.float32)}
    c.update(more_constants())
    return c


def lay_out(inputs):
    f = {n: np.asarray(a) for n, a in inputs.items()}
    w = f["w_in"]
    at = np.cumsum([0, 256, 128, 128, 256, 384, 384, 384, 384, 384, 384, 384, 384, 384, 24])
    qa, ka, va, za, qb, kb, vb, zb, qm, km, vm, om, zm, gm = (w[:, :, at[n]:at[n + 1]] for n in range(14))
    nat = np.concatenate([va, za, vb, zb, vm, om, zm], 2).reshape(DEPTH, KT, P, NCH, CW).transpose(0, 3, 2, 1, 4)
    gate = np.concatenate([gm, np.zeros((DEPTH, DM, P - gm.shape[2]), w.dtype)], 2)
    third = lambda a, n: a[:, :, n * P:(n + 1) * P]
    tiles = [third(qa, 0), third(qa, 1), ka, gate]
    for q, kk in ((qb, kb), (qm, km)):
        for n in range(3):
            tiles += [third(q, n), third(kk, n)]
    tr = np.stack(tiles, 1).reshape(DEPTH, TILES, KT, P, P).transpose(0, 1, 3, 2, 4)
    a = {"x": f["x"][0], "ctx": f["ctx"][0], "cond": np.concatenate([f["c"], f["c_ctx"][None]], 0),
         "w_mod": f["w_mod"], "b_mod": f["b_mod"], "w_nat": nat, "w_tr": tr}
    a["w_out"] = f["w_out"].reshape(DEPTH, KT, P, DM).transpose(0, 2, 1, 3)
    for n in ("attn_sink", "diff_lambda", "diff_norm_g", "mlstm_norm_g", "ln_g", "ln_b"):
        a[n] = f[n]
    a["i_bias"], a["f_bias"] = f["mlstm_i_bias"], f["mlstm_f_bias"]
    a.update(constants())
    return {n: np.ascontiguousarray(v) for n, v in a.items()}


SCRATCH = {"x": ([TOK, DM], F32), "mod": ([2, 3 * DM], F32), "nat": ([TOK, NW], F32), "va": ([PADTOK, P], F32),
           "qa": ([2, P, TOK], F32), "ka": ([P, PADTOK], F32), "gates": ([24, TOK], F32),
           "qkb": ([2, 3, 3 * P, TOK], BF16), "qkc": ([2, 3 * P, TOK], F32),
           "u": ([12, TOK], F32), "decay": ([12, NT], F32), "y": ([TOK, DM], F32)}


def kernel(**inputs):
    import concourse.bacc as bacc
    from concourse.bass_utils import run_bass_kernel_spmd

    nc = bacc.Bacc("TRN2", target_bir_lowering=False, num_devices=1)
    arrays = lay_out(inputs)
    io = {n: nc.dram_tensor(f"in_{n}", a.shape, mybir.dt.from_np(a.dtype), kind="ExternalInput").ap() for n, a in arrays.items()}
    out = nc.dram_tensor("out_0", (SEQ, DM), F32, kind="ExternalOutput").ap()
    scratch = {n: nc.dram_tensor(f"work_{n}", s, t, kind="Internal").ap() for n, (s, t) in SCRATCH.items()}
    program(nc, io, out, scratch, None)
    result = run_bass_kernel_spmd(nc, [{f"in_{n}": a for n, a in arrays.items()}], core_ids=[0])
    return result.results[0]["out_0"].reshape(1, SEQ, DM)
```

```python
from contextlib import ExitStack

import numpy as np

import concourse.bass as bass
from concourse import mybir

F32 = mybir.dt.float32
BF16 = mybir.dt.bfloat16
ALU = mybir.AluOpType
ACT = mybir.ActivationFunctionType
AX = mybir.AxisListType

P = 128
DM = 1024
KT = DM // P
DEPTH = 2
SEQ, CTX = 2048, 256
TOK = SEQ + CTX
NT = TOK // P
NTL = SEQ // P
HD = 64
A_HEADS, A_KV = 4, 2
B_HEADS, B_QK = 6, 32
C_HEADS = 6
GRID_W = 64
EPS = 1e-5
ALPHA = (2 * DEPTH) ** 0.25
WIN = 128
NEG = -1.0e30
CW, NCH = 384, 6
VA, SA, VB, SB, VM, SC, NW = 0, 128, 384, 768, 1152, 1536, 1920
TILES = 16
PADTOK = TOK + 2 * WIN
LAT0, CTX0 = WIN, SEQ + 2 * WIN
TB = [(512 * b, 512) for b in range(4)] + [(SEQ, CTX)]


class Chain:

    def __init__(self, eng, sem):
        self.eng, self.sem, self.base, self.n = eng, sem, 0, 0

    def turn(self, base):
        self.base, self.n = base, 0

    def __call__(self, instruction):
        self.n += 1
        instruction.then_inc(self.sem, 1)
        self.eng.wait_ge(self.sem, self.base + self.n)


class Core:

    def __init__(self, nc, stack, io, d):
        self.nc, self.stack, self.io, self.d = nc, stack, io, d
        self.stage = 0

    def semaphores(self, stack, prefix, single, several=()):
        self.stage += 1
        made = {n: stack.enter_context(self.nc.semaphore(f"{prefix}_{n}_{self.stage}")) for n in single}
        made.update({n: [stack.enter_context(self.nc.semaphore(f"{prefix}_{n}{u}_{self.stage}")) for u in range(count)]
                     for n, count in dict(several).items()})
        for s in made.values():
            for one in s if isinstance(s, list) else [s]:
                self.nc.sync.sem_clear(one)
        self.nc.all_engine_barrier()
        return made

    def buffers(self, stack):
        self.stage += 1
        stage = self.stage
        return lambda name, shape, dtype=F32: stack.enter_context(self.nc.sbuf_tensor(f"{name}_{stage}", shape, dtype))


def modulation(k, l, names):
    nc, io, d, ps = k.nc, k.io, k.d, k.ps
    with ExitStack() as st:
        sb = k.buffers(st)
        NC2, W = 6, 512
        wm = sb("mod_w", [P, 3, KT, W])
        brow = sb("mod_bias", [2, 3 * DM])
        mod = sb("mod_rows", [2, 3 * DM])
        w_ld, b_ld, done, added, stored, cols_ld = names["w_ld"], names["b_ld"], names["done"], names["added"], names["stored"], names["cols_ld"]
        block = st.enter_context(nc.Block())
        wv = io["w_mod"].rearrange("l (k p) n -> l p k n", p=P)
        modv = d["mod"].rearrange("r (j k p) -> p j r k", j=3, p=P)

        @block.sync
        def _(sp):
            sp.dma_start(brow[:], io["b_mod"][l, :].partition_broadcast(2)).then_inc(b_ld, 16)
            for c in range(NC2):
                if c >= 3:
                    sp.wait_ge(done, c - 2)
                sp.dma_start(wm[:, c % 3, :, :], wv[l, :, :, c * W:(c + 1) * W]).then_inc(w_ld[c % 3], 16)
            sp.wait_ge(added, NC2)
            sp.dma_start(d["mod"], mod[:]).then_inc(stored, 16)
            sp.wait_ge(stored, 16)
            for j in range(2):
                for r in range(2):
                    sp.dma_start(k.modc[:, j, r, :], modv[:, j, r, :], allow_slow_non_contiguous=True).then_inc(cols_ld, 16)
            sp.wait_ge(cols_ld, 64)

        @block.tensor
        def _(pe):
            for c in range(NC2):
                pe.wait_ge(w_ld[c % 3], 16 * (c // 3 + 1))
                for j in range(KT):
                    mm = nc.tensor.matmul(ps[0:2, c, 0:W], k.silu_c[:, j, :], wm[:, c % 3, j, :],
                                          start=(j == 0), stop=(j == KT - 1))
                mm.then_inc(done, 1)

        @block.vector
        def _(dve):
            dve.wait_ge(b_ld, 16)
            for c in range(NC2):
                dve.wait_ge(done, c + 1)
                nc.vector.tensor_tensor(mod[:, c * W:(c + 1) * W], ps[0:2, c, 0:W],
                                        brow[:, c * W:(c + 1) * W], ALU.add).then_inc(added, 1)
            dve.wait_ge(cols_ld, 64)
            nc.vector.tensor_scalar(k.modc[:, 1, :, :], k.modc[:, 1, :, :], 1.0, None, ALU.add).then_inc(added, 1)
            dve.wait_ge(added, NC2 + 1)


def natural_project(k, l, hT, s):
    nc, io, d, ps = k.nc, k.io, k.d, k.ps
    with ExitStack() as st:
        sb = k.buffers(st)
        wn = sb("wn", [P, NCH, KT, CW])
        xt = sb("xt", [P, 2, DM])
        hs = sb("hs", [P, 2, KT, P])
        nt = sb("nt", [P, 2, NW])
        sz = sb("sz", [P, 2, CW])
        block = st.enter_context(nc.Block())
        w_ld, x_ld, n_st = s["w_ld"], s["x_ld"], s["n_st"]
        turned, h_ready, kept = s["turned"], s["h_ready"], s["kept"]
        prod, evac, v_free, z_free, n_ready = s["prod"], s["evac"], s["v_free"], s["z_free"], s["n_ready"]
        PAIRS = NT // 2
        HEAD = 2 * NCH

        @block.sync
        def _(sp):
            for u in range(2):
                sp.sem_inc(n_st[u], 16)
                sp.dma_start(xt[:, u, :], d["x"][u * P:(u + 1) * P, :]).then_inc(x_ld[u], 16)
            for c in range(NCH):
                sp.dma_start(wn[:, c, :, :], io["w_nat"][l, c, :, :, :]).then_inc(w_ld[c], 16)

            def store(i, u):
                sp.wait_ge(n_ready, 2 * i + (u + 1))
                sp.dma_start(d["nat"][bass.ds(i * (2 * P) + u * P, P), :], nt[:, u, :]).then_inc(n_st[u], 16)

            def store_va(i, u, row):
                sp.dma_start(d["va"][bass.ds(row, P), :], nt[:, u, 0:P]).then_inc(n_st[u], 16)

            with sp.Fori(0, PAIRS - 1) as i:
                for u in range(2):
                    sp.wait_ge(turned, 2 * i + (u + 1))
                    sp.dma_start(xt[:, u, :], d["x"][bass.ds(i * (2 * P) + (u + 2) * P, P), :]).then_inc(x_ld[u], 16)
                    store(i, u)
                    store_va(i, u, i * (2 * P) + u * P + LAT0)
            for u in range(2):
                store(PAIRS - 1, u)
                store_va(PAIRS - 1, u, CTX0 + u * P)
            for u in range(2):
                sp.wait_ge(n_st[u], 16 + 32 * PAIRS)

        @block.tensor
        def _(pe):
            pe.sem_inc(prod, HEAD)

            def turn(i, u, t):
                for j in range(KT):
                    tr = nc.tensor.transpose(ps[:, j // 4, (j % 4) * P:(j % 4 + 1) * P],
                                             xt[:, u, j * P:(j + 1) * P], k.ident[:])
                tr.then_inc(turned, 1)

            def product(i, u):
                pe.wait_ge(h_ready, 2 * i + (u + 1))
                for c in range(NCH):
                    free = v_free if c in (1, 3, 4) else z_free
                    n = {1: 0, 3: 1, 4: 2, 0: 0, 2: 1, 5: 2}[c]
                    pe.wait_ge(free, 6 * i + (3 * u + n + 1))
                    for j in range(KT):
                        mm = nc.tensor.matmul(ps[:, 2 + c, 0:CW], hs[:, u, j, :], wn[:, c, j, :],
                                              start=(j == 0), stop=(j == KT - 1))
                    mm.then_inc(prod, 1)

            pe.wait_ge(x_ld[0], 16)
            turn(0, 0, 0)
            for c in range(NCH):
                pe.wait_ge(w_ld[c], 16)
            with pe.Fori(0, PAIRS - 1) as i:
                pe.wait_ge(x_ld[1], 16 * i + 16)
                pe.wait_ge(h_ready, 2 * i + 1)
                turn(i, 1, None)
                product(i, 0)
                pe.wait_ge(x_ld[0], 16 * i + 32)
                pe.wait_ge(h_ready, 2 * i + 2)
                turn(i, 0, None)
                product(i, 1)
            i = PAIRS - 1
            pe.wait_ge(x_ld[1], 16 * i + 16)
            pe.wait_ge(h_ready, 2 * i + 1)
            turn(i, 1, None)
            product(i, 0)
            product(i, 1)

        @block.vector
        def _(dve):
            dve.sem_inc(z_free, 3)

            def modulate(t, u, r):
                dve.wait_ge(turned, t + 1)
                dve.wait_ge(prod, 6 * t + 6)
                dve.wait_ge(kept, t + 1)
                for j in range(KT):
                    op = nc.vector.tensor_scalar(hs[:, u, j, :], ps[:, j // 4, (j % 4) * P:(j % 4 + 1) * P],
                                                 k.modc[:, 1, r, j:j + 1], k.modc[:, 0, r, j:j + 1],
                                                 ALU.mult, ALU.add)
                op.then_inc(h_ready, 1)

            def gates(i, u):
                base = 6 * i + 3 * u
                zb = 6 * i + (3 * u + 3)
                dve.wait_ge(evac, base + 1)
                nc.vector.tensor_tensor(nt[:, u, SA:VB], nt[:, u, SA:VB], ps[:, 2, P:CW], ALU.mult).then_inc(z_free, 1)
                dve.wait_ge(evac, base + 2)
                nc.vector.tensor_tensor(nt[:, u, SB:VM], nt[:, u, SB:VM], ps[:, 4, 0:CW], ALU.mult).then_inc(z_free, 1)
                dve.wait_ge(evac, base + 3)
                nc.vector.tensor_tensor(sz[:, u, :], sz[:, u, :], ps[:, 7, 0:CW], ALU.mult).then_inc(z_free, 1)
                dve.wait_ge(z_free, zb + 3)
                nc.vector.tensor_tensor(nt[:, u, SC:NW], nt[:, u, SC:NW], sz[:, u, :], ALU.mult).then_inc(n_ready, 1)

            modulate(0, 0, 0)
            with dve.Fori(0, PAIRS - 2) as i:
                modulate(2 * i + 1, 1, 0)
                gates(i, 0)
                modulate(2 * i + 2, 0, 0)
                gates(i, 1)
            i = PAIRS - 2
            modulate(2 * i + 1, 1, 0)
            gates(i, 0)
            modulate(2 * i + 2, 0, 1)
            gates(i, 1)
            i = PAIRS - 1
            modulate(2 * i + 1, 1, 1)
            gates(i, 0)
            gates(i, 1)

        @block.scalar
        def _(act):
            act.sem_inc(v_free, 3)

            def body(i, u):
                base = 12 * i + (6 * u + HEAD)
                act.wait_ge(n_st[u], 32 * i + 16)

                def chunk(c):
                    act.wait_ge(prod, base + (c + 1))
                chunk(0)
                nc.scalar.copy(nt[:, u, VA:SA], ps[:, 2, 0:P])
                nc.scalar.activation(nt[:, u, SA:VB], ps[:, 2, P:CW], ACT.Sigmoid).then_inc(evac, 1)
                chunk(1)
                nc.scalar.copy(nt[:, u, VB:SB], ps[:, 3, 0:CW]).then_inc(v_free, 1)
                chunk(2)
                nc.scalar.activation(nt[:, u, SB:VM], ps[:, 4, 0:CW], ACT.Sigmoid).then_inc(evac, 1)
                chunk(3)
                nc.scalar.copy(nt[:, u, VM:SC], ps[:, 5, 0:CW]).then_inc(v_free, 1)
                chunk(4)
                nc.scalar.activation(nt[:, u, SC:NW], ps[:, 6, 0:CW], ACT.Sigmoid).then_inc(v_free, 1)
                chunk(5)
                nc.scalar.activation(sz[:, u, :], ps[:, 7, 0:CW], ACT.Sigmoid).then_inc(evac, 1)

            with act.Fori(0, PAIRS) as i:
                for u in range(2):
                    body(i, u)

        @block.gpsimd
        def _(pool):
            pool.sem_inc(kept, 2)
            with pool.Fori(0, PAIRS) as i:
                for u in range(2):
                    pool.wait_ge(h_ready, 2 * i + (u + 1))
                    nc.gpsimd.tensor_copy(hT[:, :, bass.ds(i * (2 * P) + u * P, P)], hs[:, u, :, :]).then_inc(kept, 1)


def transposed_project(k, l, hT, s, kinds, first, pairs, out):
    nc, io, d, ps = k.nc, k.io, k.d, k.ps
    rope = [isinstance(kind, str) for kind in kinds]
    split = kinds[0] == "rope_b"
    parts = 3 if split else 1
    NB = len(TB)
    R = sum(rope) * 4
    with ExitStack() as st:
        sb = k.buffers(st)
        wt = sb("wt", [P, 2, KT, P])
        qs = sb("qs", [P, 2, 512])
        tab = sb("tab", [P, 2, SEQ])
        perm = sb("perm", [P, P])
        t1 = sb("t1", [P, 2, 512])
        t2 = sb("t2", [P, 2, 512])
        ob = sb("ob", [P, 2, 3, 512], BF16) if split else sb("ob", [P, 2, 1, 512])
        block = st.enter_context(nc.Block())
        w_ld, tab_ld, o_st, prod, evac, rot, rot_free, done, chain = (
            s["w_ld"], s["tab_ld"], s["o_st"], s["prod"], s["evac"], s["rot"], s["rot_free"], s["done"], s["chain"])
        which = 1 if split else 0
        blocks = [(u, b) for u in range(2) for b in range(NB)]

        @block.sync
        def _(sp):
            for u in range(2):
                sp.sem_inc(o_st[u], 16 * parts)
                sp.dma_start(wt[:, u, :, :], io["w_tr"][l, first + u, :, :, :]).then_inc(w_ld[u], 16)
            if R:
                sp.dma_start(tab[:], io["rope"][which, :, :, :]).then_inc(tab_ld, 16)
                sp.dma_start(perm[:], io["perm"][which, :, :]).then_inc(tab_ld, 16)

            def store(i, n, u, b):
                sp.wait_ge(done, 2 * NB * i + (n + 3))
                t0, w = TB[b]
                for dst, src in out(i, u, b, t0, w, ob[:, n % 2, :, 0:w]):
                    sp.dma_start(dst, src).then_inc(o_st[n % 2], 16)

            def turn(i, more):
                for n, (u, b) in enumerate(blocks):
                    store(i, n, u, b)
                    if b == NB - 1 and more:
                        sp.wait_ge(prod, 2 * NB * i + NB * (u + 1))
                        sp.dma_start(wt[:, u, :, :], io["w_tr"][l, bass.ds(2 * i + (first + 2 + u), 1), :, :, :]
                                     .rearrange("o p k n -> p (o k) n")).then_inc(w_ld[u], 16)

            if pairs > 1:
                with sp.Fori(0, pairs - 1) as i:
                    turn(i, True)
            turn(pairs - 1, False)
            for u in range(2):
                sp.wait_ge(o_st[u], 16 * parts * (1 + NB * pairs))

        def loop(eng, body):
            if pairs > 1:
                with eng.Fori(0, pairs) as i:
                    body(i)
            else:
                body(0)

        @block.tensor
        def _(pe):
            if R:
                pe.wait_ge(tab_ld, 32)

            def body(i):
                r = 0
                for n, (u, b) in enumerate(blocks):
                    if b == 0:
                        pe.wait_ge(w_ld[u], 16 * i + 16)
                    t0, w = TB[b]
                    pe.wait_ge(evac, 2 * NB * i + (n + 1))
                    for j in range(KT):
                        mm = nc.tensor.matmul(ps[:, b, 0:w], wt[:, u, j, :], hT[:, j, t0:t0 + w],
                                              start=(j == 0), stop=(j == KT - 1))
                    mm.then_inc(prod, 1)
                    if rope[u] and b >= 1:
                        pe.wait_ge(evac, 2 * NB * i + (n + NB))
                        pe.wait_ge(rot_free, R * i + (r + 1))
                        nc.tensor.matmul(ps[:, 5 + r % 2, 0:512], perm[:], qs[:, (n - 1) % 2, 0:512],
                                         start=True, stop=True).then_inc(rot, 1)
                        r += 1
            loop(pe, body)

        @block.scalar
        def _(act):
            act.sem_inc(evac, NB)

            def body(i):
                for n, (u, b) in enumerate(blocks):
                    w = TB[b][1]
                    act.wait_ge(prod, 2 * NB * i + (n + 1))
                    act.wait_ge(done, 2 * NB * i + (n + 1))
                    nc.scalar.copy(qs[:, n % 2, 0:w], ps[:, b, 0:w]).then_inc(evac, 1)
            loop(act, body)

        @block.vector
        def _(dve):
            link = Chain(dve, chain)
            steps = 3 * 2 * NB + R
            dve.sem_inc(rot_free, 2)
            dve.sem_inc(done, 2)
            if R:
                dve.wait_ge(tab_ld, 32)

            def body(i):
                link.turn(steps * i)
                r = 0
                for n, (u, b) in enumerate(blocks):
                    t0, w = TB[b]
                    v = n % 2
                    src = qs[:, v, 0:w]
                    dve.wait_ge(evac, 2 * NB * i + (n + 1 + NB))
                    dve.wait_ge(o_st[v], 16 * parts * NB * i + 16 * parts * (n // 2 + 1))
                    if rope[u] and b < 4:
                        nc.vector.tensor_tensor(t1[:, v, 0:w], src, tab[:, 0, t0:t0 + w], ALU.mult)
                        dve.wait_ge(rot, R * i + (r + 1))
                        nc.vector.tensor_tensor(t2[:, v, 0:w], ps[:, 5 + r % 2, 0:w], tab[:, 1, t0:t0 + w],
                                                ALU.mult).then_inc(rot_free, 1)
                        r += 1
                        dve.wait_ge(rot_free, R * i + (r + 2))
                        if split:
                            link(nc.vector.tensor_tensor(t1[:, v, 0:w], t1[:, v, 0:w], t2[:, v, 0:w], ALU.add))
                            src = t1[:, v, 0:w]
                        else:
                            last = nc.vector.tensor_tensor(ob[:, v, 0, 0:w], t1[:, v, 0:w], t2[:, v, 0:w], ALU.add)
                    elif not split:
                        factor = 1.0 if rope[u] else kinds[u]
                        last = nc.vector.tensor_scalar(ob[:, v, 0, 0:w], src, factor, None, ALU.mult)
                    if split:
                        link(nc.vector.tensor_copy(ob[:, v, 0, 0:w], src))
                        link(nc.vector.tensor_tensor(t2[:, v, 0:w], src, ob[:, v, 0, 0:w], ALU.subtract))
                        link(nc.vector.tensor_copy(ob[:, v, 1, 0:w], t2[:, v, 0:w]))
                        last = nc.vector.tensor_tensor(ob[:, v, 2, 0:w], t2[:, v, 0:w], ob[:, v, 1, 0:w], ALU.subtract)
                    last.then_inc(done, 1)
                assert not split or link.n == steps
            loop(dve, body)


UNITS = 2 * C_HEADS
PAIRS_C = C_HEADS // 2
SV = HD + 1
PV = 2 * SV
KEY, INTER, UPDATE, FLOOR = range(4)
DIRS = ((0, 32), (32, 64))


def mlstm_gates(k, l, s, cols, knat, v1):
    nc, io, d, ps = k.nc, k.io, k.d, k.ps
    with ExitStack() as st:
        sb = k.buffers(st)
        gi, gf, keep, tmp, logf, b, m = (sb(n, [64, TOK]) for n in ("gi", "gf", "keep", "tmp", "logf", "b", "m"))
        stat = sb("stat", [64, 4, TOK])
        turn = sb("turn", [64, 2, 4, P])
        ib, fb = sb("ib", [64, 1]), sb("fb", [64, 1])
        mprev, delta, decay = (sb(n, [64, NT]) for n in ("mprev", "delta", "decay"))
        kc = sb("kc", [P, 2, PAIRS_C, P])
        block = st.enter_context(nc.Block())
        cleared, g_ld, v_ld, k_ld, dve_s, act_s, row_st = (
            s[n] for n in ("cleared", "g_ld", "v_ld", "k_ld", "gate_steps", "gate_exps", "row_st"))
        staged, turned, kept = s["staged"], s["turned"], s["kept"]

        @block.sync
        def _(sp):
            for u in range(2):
                sp.dma_start(kc[:, u, :, :], d["qkc"][1, :, u * P:(u + 1) * P].rearrange("(c p) t -> p c t", p=P)
                             ).then_inc(k_ld[u], 16)
            sp.dma_start(keep[:], io["keep"]).then_inc(g_ld, 16)
            sp.wait_ge(dve_s, 1)
            for way, (lo, _) in enumerate(DIRS):
                sp.dma_start(gi[lo:lo + 6, :], d["gates"][12 * way:12 * way + 6, :]).then_inc(g_ld, 16)
                sp.dma_start(gf[lo:lo + 6, :], d["gates"][12 * way + 6:12 * way + 12, :]).then_inc(g_ld, 16)
                sp.dma_start(ib[lo:lo + 6, :], io["i_bias"][l, way, :].unsqueeze(1)).then_inc(g_ld, 16)
                sp.dma_start(fb[lo:lo + 6, :], io["f_bias"][l, way, :].unsqueeze(1)).then_inc(g_ld, 16)
            sp.wait_ge(cleared, 1)
            for h in range(C_HEADS):
                sp.dma_start(v1[:, :, h, 0:HD], d["nat"][:, VM + h * HD:VM + (h + 1) * HD].rearrange("(c p) v -> p c v", p=P)
                             ).then_inc(v_ld, 16)
            with sp.Fori(0, NT // 2 - 1) as i:
                for u in range(2):
                    sp.wait_ge(turned, 2 * i + (u + 3))
                    sp.dma_start(kc[:, u, :, :], d["qkc"][1, :, bass.ds(i * (2 * P) + (2 + u) * P, P)].rearrange("(c p) t -> p c t", p=P)
                                 ).then_inc(k_ld[u], 16)
            sp.wait_ge(act_s, 6)
            for way, (lo, _) in enumerate(DIRS):
                sp.dma_start(d["u"][6 * way:6 * way + 6, :], tmp[lo:lo + 6, :]).then_inc(row_st, 16)
                sp.dma_start(d["decay"][6 * way:6 * way + 6, :], decay[lo:lo + 6, :]).then_inc(row_st, 16)
            sp.wait_ge(row_st, 64)
            sp.wait_ge(v_ld, 16 * C_HEADS)

        @block.gpsimd
        def _(pool):
            nc.gpsimd.memset(v1[:], 1.0).then_inc(cleared, 1)
            pool.wait_ge(cleared, 1)

        @block.vector
        def _(dve):
            link = Chain(dve, dve_s)
            for t in (gi, gf, ib, fb):
                last = nc.vector.memset(t[:], 0.0)
            link(last)
            dve.wait_ge(g_ld, 16 * 9)
            link(nc.vector.tensor_scalar(gi[:], gi[:], ib[:], None, ALU.add))
            link(nc.vector.tensor_scalar(gf[:], gf[:], fb[:], None, ALU.add))
            link(nc.vector.scalar_tensor_tensor(out=tmp[:], in0=gf[:], scalar=-1.0, in1=gf[:],
                                                op0=ALU.mult, op1=ALU.max))
            dve.wait_ge(act_s, 2)
            link(nc.vector.scalar_tensor_tensor(out=logf[:], in0=gf[:], scalar=0.0, in1=tmp[:],
                                                op0=ALU.min, op1=ALU.subtract))
            scan = nc.vector.tensor_tensor_scan
            scan(out=b[0:32, :], data0=keep[0:32, :], data1=logf[0:32, :], initial=0.0, op0=ALU.mult, op1=ALU.add)
            scan(out=b[32:64, ::-1], data0=keep[32:64, ::-1], data1=logf[32:64, ::-1], initial=0.0, op0=ALU.mult, op1=ALU.add)
            scan(out=m[32:64, ::-1], data0=logf[32:64, ::-1], data1=gi[32:64, ::-1], initial=0.0, op0=ALU.add, op1=ALU.max)
            link(scan(out=m[0:32, SEQ:TOK], data0=logf[0:32, SEQ:TOK], data1=gi[0:32, SEQ:TOK], initial=0.0,
                      op0=ALU.add, op1=ALU.max))
            link(scan(out=m[0:32, 0:SEQ], data0=logf[0:32, 0:SEQ], data1=gi[0:32, 0:SEQ],
                      initial=m[0:32, TOK - 1:TOK], op0=ALU.add, op1=ALU.max))
            chunks = lambda t: t.rearrange("r (c t) -> r c t", t=P)
            mc, bc = chunks(m[:]), chunks(b[:])
            nc.vector.tensor_tensor(tmp[:], b[:], m[:], ALU.subtract)
            nc.vector.tensor_tensor(stat[:, KEY, :], gi[:], b[:], ALU.subtract)
            nc.vector.memset(mprev[:], 0.0)
            nc.vector.tensor_tensor(delta[0:32, :], bc[0:32, :, P - 1], mc[0:32, :, P - 1], ALU.subtract)
            link(nc.vector.tensor_tensor(delta[32:64, :], bc[32:64, :, 0], mc[32:64, :, 0], ALU.subtract))
            nc.vector.tensor_copy(mprev[0:32, 1:NTL], mc[0:32, 0:NTL - 1, P - 1])
            nc.vector.tensor_copy(mprev[0:32, 0:1], mc[0:32, NT - 1, P - 1:P])
            nc.vector.tensor_copy(mprev[0:32, NTL + 1:NT], mc[0:32, NTL:NT - 1, P - 1])
            link(nc.vector.tensor_copy(mprev[32:64, 0:NT - 1], mc[32:64, 1:NT, 0]))
            wide = lambda t: t[:].unsqueeze(2).to_broadcast([64, NT, P])
            nc.vector.tensor_tensor(chunks(stat[:, INTER, :]), chunks(tmp[:]), wide(mprev), ALU.add)
            nc.vector.tensor_tensor(chunks(stat[:, UPDATE, :]), chunks(stat[:, KEY, :]), wide(delta), ALU.add)
            link(nc.vector.tensor_tensor(decay[:], delta[:], mprev[:], ALU.add))
            dve.wait_ge(act_s, 6)
            with dve.Fori(0, NT // 2) as i:
                for u in range(2):
                    dve.wait_ge(turned, 2 * i + (u + 1))
                    nc.vector.tensor_copy(turn[:, u, :, :], stat[:, :, bass.ds(i * (2 * P) + u * P, P)]).then_inc(staged, 1)

        @block.scalar
        def _(act):
            link = Chain(act, act_s)
            act.wait_ge(dve_s, 4)
            link(nc.scalar.activation(tmp[:], tmp[:], ACT.Exp, scale=-1.0))
            link(nc.scalar.activation(tmp[:], tmp[:], ACT.Ln, bias=1.0))
            act.wait_ge(dve_s, 10)
            link(nc.scalar.activation(stat[:, INTER, :], stat[:, INTER, :], ACT.Exp))
            link(nc.scalar.activation(stat[:, UPDATE, :], stat[:, UPDATE, :], ACT.Exp))
            link(nc.scalar.activation(stat[:, FLOOR, :], m[:], ACT.Exp, scale=-1.0))
            link(nc.scalar.activation(decay[:], decay[:], ACT.Exp))
            act.sem_inc(kept, 2)
            with act.Fori(0, NT // 2) as i:
                for u in range(2):
                    act.wait_ge(turned, 2 * i + (u + 3))
                    nc.scalar.copy(cols[:, bass.ds(2 * i + u, 1), :, :].rearrange("p o f (w h) -> p (o f) w h", w=2),
                                   ps[:, u, 0:256].rearrange("p (f w h) -> p f w h", f=4, w=2)[:, :, :, 0:C_HEADS])
                    nc.scalar.copy(knat[:, bass.ds(2 * i + u, 1), :].rearrange("p o c -> p (o c)"),
                                   ps[:, 2 + u, 0:PAIRS_C * P]).then_inc(kept, 1)

        @block.tensor
        def _(pe):
            pe.sem_inc(turned, 2)
            with pe.Fori(0, NT // 2) as i:
                for u in range(2):
                    pe.wait_ge(k_ld[u], 16 * i + 16)
                    pe.wait_ge(kept, 2 * i + (u + 1))
                    pe.wait_ge(staged, 2 * i + (u + 1))
                    for p in range(PAIRS_C):
                        nc.tensor.transpose(ps[:, 2 + u, p * P:(p + 1) * P], kc[:, u, p, :], k.ident[:])
                    for f in range(4):
                        tr = nc.tensor.transpose(ps[:, u, f * 64:(f + 1) * 64], turn[:, u, f, :], k.ident[0:64, 0:64])
                    tr.then_inc(turned, 1)


def mlstm_states(k, l, s, cols, knat, v1, states):
    nc, io, d, ps = k.nc, k.io, k.d, k.ps
    with ExitStack() as st:
        sb = k.buffers(st)
        kw = sb("kw", [P, 2, 2, C_HEADS, HD])
        dec = sb("dec", [P, 2, PAIRS_C, NT])
        block = st.enter_context(nc.Block())
        d_ld, weighed, prod, stepped = s["d_ld"], s["weighed"], s["prod"], s["stepped"]
        head = [(NT - 2, NT - 1, NT - 1, NT - 2), (NT - 1, NT - 2, 0, NTL - 1)]

        def steps(eng, body):
            for n, c in enumerate(head):
                body(n, n % 2, *c)
            with eng.Fori(0, (NTL - 2) // 2) as i:
                for u in range(2):
                    body(2 * i + (2 + u), u, 2 * i + u, (NTL - 1 - u) - 2 * i, 2 * i + (u + 1), (NTL - 2 - u) - 2 * i)
            body(NTL, 0, NTL - 2, 1, NTL - 1, 0)

        @block.sync
        def _(sp):
            by_half = d["decay"].rearrange("(w p h) c -> h w p c", w=2, h=2)
            for h in range(2):
                sp.dma_start(dec[64 * h:64 * h + 64, :, :, :], by_half[h, :, :, :].partition_broadcast(64)).then_inc(d_ld, 16)
            sp.wait_ge(d_ld, 32)

        @block.gpsimd
        def _(pool):
            nc.gpsimd.memset(states[:, NT // 2:NTL, :, :, :], 0.0).then_inc(s["cleared3"], 1)

            def body(n, u, f, b, fn, bn):
                pool.wait_ge(prod, n + 1)
                for way, c in ((0, f), (1, b)):
                    op = nc.gpsimd.tensor_tensor(
                        kw[:, u, way, :, :], knat[:, bass.ds(c, 1), :].rearrange("p o (h e) -> p (o h) e", e=HD),
                        cols[:, bass.ds(c, 1), UPDATE, way * C_HEADS:(way + 1) * C_HEADS].rearrange("p o h -> p (o h)")
                        .unsqueeze(2).to_broadcast([P, C_HEADS, HD]), ALU.mult)
                op.then_inc(weighed, 1)
            steps(pool, body)

        @block.tensor
        def _(pe):
            pe.sem_inc(prod, 2)

            def body(n, u, f, b, fn, bn):
                pe.wait_ge(weighed, n + 1)
                pe.wait_ge(stepped, n + 1)
                for way, c in ((0, f), (1, b)):
                    for p in range(PAIRS_C):
                        mm = nc.tensor.matmul(ps[:, 2 * u + way, p * PV:(p + 1) * PV],
                                              kw[:, u, way, 2 * p:2 * p + 2, :].rearrange("p h e -> p (h e)"),
                                              v1[:, bass.ds(c, 1), 2 * p:2 * p + 2, :].rearrange("p o h e -> p (o h e)"),
                                              start=True, stop=True)
                mm.then_inc(prod, 1)
            steps(pe, body)

        @block.vector
        def _(dve):
            dve.sem_inc(stepped, 1)
            nc.vector.memset(states[:, 0:NT // 2, :, :, :], 0.0)
            nc.vector.memset(states[:, NTL:, :, :, :], 0.0).then_inc(stepped, 1)
            dve.wait_ge(d_ld, 32)
            dve.wait_ge(s["cleared3"], 1)

            def body(n, u, f, b, fn, bn):
                dve.wait_ge(prod, n + 3)
                dve.wait_ge(stepped, n + 2)
                for way, c, cn in ((0, f, fn), (1, b, bn)):
                    for p in range(PAIRS_C):
                        for h in range(2):
                            half, at = slice(64 * h, 64 * h + 64), slice(h * SV, (h + 1) * SV)
                            state = lambda c: states[half, bass.ds(c, 1), way, p, at].rearrange("p o e -> p (o e)")
                            op = nc.vector.scalar_tensor_tensor(
                                out=state(cn), in0=state(c), scalar=dec[half, way, p, bass.ds(c, 1)],
                                in1=ps[half, 2 * u + way, p * PV + h * SV:p * PV + (h + 1) * SV],
                                op0=ALU.mult, op1=ALU.add)
                op.then_inc(stepped, 1)
            steps(dve, body)


def mlstm_outputs(k, l, s, cols, v1, states, with_ctx):
    nc, io, d, ps = k.nc, k.io, k.d, k.ps
    CHUNKS = NT if with_ctx else NTL
    with ExitStack() as st:
        sb = k.buffers(st)
        mask = sb("mask", [P, 2, P])
        kt = sb("kt", [P, 2, PAIRS_C, P])
        qt = sb("qt", [P, 2, PAIRS_C, P])
        qd = sb("qd", [P, 2, PAIRS_C, 2, P])
        ur = sb("ur", [P, 2, UNITS, P])
        gate = sb("gate", [P, 2, UNITS, P])
        mt = sb("mt", [P, UNITS, P])
        num = sb("num", [P, 2, UNITS, SV])
        den = sb("den", [P, 2, UNITS])
        both = sb("both", [P, 2, UNITS, HD])
        yt = sb("yt", [P, 2, C_HEADS * HD])
        block = st.enter_context(nc.Block())
        (m_ld, c_ld, y_st, cleared, logits, gated, scored, mixed, intra, inter, inter_free, chain, ready, y_done) = (
            s[n] for n in ("m_ld", "c_ld", "y_st", "cleared2", "logits", "gated", "scored", "mixed", "intra", "inter",
                           "inter_free", "den_steps", "ready", "y_done"))
        LOADS = 5

        @block.sync
        def _(sp):
            sp.dma_start(mask[:], io["causal"]).then_inc(m_ld, 16)
            sp.wait_ge(cleared, 1)

            def load(c, u):
                span = bass.ds(c * P, P)
                pairs = lambda j: d["qkc"][j, :, span].rearrange("(c p) t -> p c t", p=P)
                sp.dma_start(kt[:, u, :, :], pairs(1)).then_inc(c_ld[u], 16)
                sp.dma_start(qt[:, u, :, :], pairs(0)).then_inc(c_ld[u], 16)
                for h in range(2):
                    half = slice(64 * h, 64 * h + 64)
                    sp.dma_start(qd[half, u, :, h, :], pairs(0)[half, :, :]).then_inc(c_ld[u], 16)
                sp.dma_start(ur[:, u, :, :], d["u"][:, span].partition_broadcast(P)).then_inc(c_ld[u], 16)

            def store(c, u):
                sp.wait_ge(y_done, c + (1 + 2))
                sp.dma_start(d["y"][bass.ds(c * P, P), 640:DM], yt[:, u, :]).then_inc(y_st[u], 16)
            for u in range(2):
                sp.sem_inc(y_st[u], 16)
                load(u, u)
            with sp.Fori(0, CHUNKS // 2 - 1) as i:
                for u in range(2):
                    sp.wait_ge(inter, 2 * i + (u + 1))
                    sp.wait_ge(logits, 2 * i + (u + 1))
                    load(2 * i + (u + 2), u)
                    store(2 * i + u, u)
            for u in range(2):
                store(CHUNKS - 2 + u, u)
            for u in range(2):
                sp.wait_ge(y_st[u], 16 + 16 * (CHUNKS // 2))

        def over_chunks(eng, first, body):
            first()
            with eng.Fori(0, CHUNKS // 2 - 1) as i:
                for u in range(2):
                    body(2 * i + u, u, i, True)
            body(CHUNKS - 2, 0, CHUNKS // 2 - 1, True)
            body(CHUNKS - 1, 1, CHUNKS // 2 - 1, False)

        @block.tensor
        def _(pe):
            def score(c, u, turn):
                pe.wait_ge(c_ld[u], 16 * LOADS * turn + 16 * LOADS)
                for p in range(PAIRS_C):
                    mm = nc.tensor.matmul(ps[:, p // 2, (p % 2) * 256:(p % 2) * 256 + 256], kt[:, u, p, :],
                                          qd[:, u, p, :, :].rearrange("p h t -> p (h t)"), start=True, stop=True)
                mm.then_inc(scored, 1)

            def incoming(c, u):
                for p in range(PAIRS_C):
                    mm = nc.tensor.matmul(ps[:, 4 + p, 0:2 * PV], qt[:, u, p, :],
                                          states[:, bass.ds(c, 1), :, p, :].rearrange("p o w e -> p (o w) e"),
                                          start=True, stop=True)
                mm.then_inc(inter, 1)

            def within(c, u):
                for way in range(2):
                    pe.wait_ge(mixed, 2 * c + (way + 1))
                    for h in range(C_HEADS):
                        mm = nc.tensor.matmul(ps[:, 2 + way, h * SV:(h + 1) * SV], mt[:, way * C_HEADS + h, :],
                                              v1[:, bass.ds(c, 1), h, :].rearrange("p o e -> p (o e)"), start=True, stop=True)
                mm.then_inc(intra, 1)

            def first():
                score(0, 0, 0)
                incoming(0, 0)
                within(0, 0)

            def body(c, u, i, more):
                if more:
                    score(c + 1, 1 - u, i + u)
                    pe.wait_ge(inter_free, 2 * c + 2)
                    incoming(c + 1, 1 - u)
                    within(c + 1, 1 - u)
            over_chunks(pe, first, body)

        @block.scalar
        def _(act):
            def one(c, u):
                act.wait_ge(logits, c + 1)
                nc.scalar.activation(gate[:, u, :, :], gate[:, u, :, :], ACT.Exp).then_inc(gated, 1)
            with act.Fori(0, CHUNKS // 2) as i:
                for u in range(2):
                    one(2 * i + u, u)

        @block.vector
        def _(dve):
            link = Chain(dve, chain)
            nc.vector.memset(qd[:], 0.0).then_inc(cleared, 1)
            dve.wait_ge(m_ld, 16)

            def logit(c, u, turn):
                dve.wait_ge(c_ld[u], 16 * LOADS * turn + 16 * LOADS)
                for n in range(UNITS):
                    op = nc.vector.scalar_tensor_tensor(
                        out=gate[:, u, n, :], in0=ur[:, u, n, :],
                        scalar=cols[:, bass.ds(c, 1), KEY, n], in1=mask[:, n // C_HEADS, :],
                        op0=ALU.add, op1=ALU.add)
                op.then_inc(logits, 1)

            def mix(c, u):
                dve.wait_ge(scored, c + 1)
                dve.wait_ge(gated, c + 1)
                for way in range(2):
                    span = slice(way * C_HEADS, (way + 1) * C_HEADS)
                    nc.vector.tensor_tensor(mt[:, span, :].rearrange("p n t -> p (n t)"),
                                            ps[:, 0:2, :].rearrange("p b t -> p (b t)")[:, 0:C_HEADS * P],
                                            gate[:, u, span, :].rearrange("p n t -> p (n t)"), ALU.mult).then_inc(mixed, 1)

            def finish(c, u):
                stat = lambda f, lo, hi: cols[:, bass.ds(c, 1), f, lo:hi].rearrange("p o n -> p (o n)")
                link.turn(5 * c)
                dve.wait_ge(inter, c + 1)
                dve.wait_ge(y_done, c + 1)
                for way in range(2):
                    lo = way * C_HEADS
                    nc.vector.tensor_tensor(
                        num[:, u, lo:lo + C_HEADS, :].rearrange("p (q h) e -> p q h e", h=2),
                        ps[:, 4:7, way * PV:(way + 1) * PV].rearrange("p q (h e) -> p q h e", h=2),
                        stat(INTER, lo, lo + C_HEADS).rearrange("p (q h) -> p q h", h=2).unsqueeze(3)
                        .to_broadcast([P, PAIRS_C, 2, SV]), ALU.mult).then_inc(inter_free, 1)
                dve.wait_ge(inter_free, 2 * c + 2)
                dve.wait_ge(intra, c + 1)
                link(nc.vector.tensor_tensor(num[:, u, :, :].rearrange("p (w h) e -> p w (h e)", w=2),
                                             num[:, u, :, :].rearrange("p (w h) e -> p w (h e)", w=2),
                                             ps[:, 2:4, 0:C_HEADS * SV], ALU.add))
                norm = num[:, u, :, HD:SV].rearrange("p n o -> p (n o)")
                link(nc.vector.scalar_tensor_tensor(out=den[:, u, :], in0=norm, scalar=-1.0, in1=norm,
                                                    op0=ALU.mult, op1=ALU.max))
                link(nc.vector.tensor_tensor(den[:, u, :], den[:, u, :], stat(FLOOR, 0, UNITS), ALU.max))
                link(nc.vector.reciprocal(den[:, u, :], den[:, u, :]))
                link(nc.vector.tensor_tensor(both[:, u, :, :], num[:, u, :, 0:HD],
                                             den[:, u, :].unsqueeze(2).to_broadcast([P, UNITS, HD]), ALU.mult))

            def first():
                logit(0, 0, 0)
                mix(0, 0)

            def body(c, u, i, more):
                if more:
                    logit(c + 1, 1 - u, i + u)
                finish(c, u)
                if more:
                    mix(c + 1, 1 - u)
            over_chunks(dve, first, body)

        @block.gpsimd
        def _(pool):
            pool.sem_inc(y_done, 2)
            with pool.Fori(0, CHUNKS // 2) as i:
                for u in range(2):
                    c = 2 * i + u
                    pool.wait_ge(chain, 5 * c + 5)
                    pool.wait_ge(y_st[u], 16 * i + 16)
                    nc.gpsimd.tensor_tensor(yt[:, u, :].rearrange("p (h e) -> p h e", e=HD), both[:, u, 0:C_HEADS, :],
                                            both[:, u, C_HEADS:, :], ALU.add).then_inc(y_done, 1)


def mlstm(k, l, s, with_ctx):
    with ExitStack() as st:
        sb = k.buffers(st)
        cols = sb("cols", [P, NT, 4, UNITS])
        v1 = sb("v1", [P, NT, C_HEADS, SV])
        knat = sb("knat", [P, NT, C_HEADS * HD])
        mlstm_gates(k, l, s, cols, knat, v1)
        states = sb("states", [P, NT, 2, PAIRS_C, PV])
        mlstm_states(k, l, s, cols, knat, v1, states)
        mlstm_outputs(k, l, s, cols, v1, states, with_ctx)


def window(k, l, s, with_ctx):
    nc, io, d, ps = k.nc, k.io, k.d, k.ps
    SCALE = HD ** -0.5
    NK = CTX + 3 * WIN
    BLOCKS = NT if with_ctx else NTL
    with ExitStack() as st:
        sb = k.buffers(st)
        masks = sb("masks", [P, 3, 3 * WIN])
        maskb = sb("maskb", [P, 3, 3 * WIN], BF16)
        identb = sb("identb", [P, P], BF16)
        kx, vx = sb("kx", [P, CTX]), sb("vx", [P, 2, P])
        sink, nsink = sb("sink", [P, A_HEADS]), sb("nsink", [P, A_HEADS])
        qt = sb("qt", [P, 2, A_HEADS, P])
        kw = sb("kw", [P, 2, 3 * WIN])
        vw = sb("vw", [P, 2, 3, P])
        pr = sb("pr", [P, A_HEADS, NK])
        pt = sb("pt", [P, 2, 5, 2 * P])
        mx, nm, sums, es, rs = (sb(n, [P, 2, A_HEADS]) for n in ("mx", "nm", "sums", "es", "rs"))
        ot = sb("ot", [P, 2 * P])
        yt = sb("yt", [P, 2, A_HEADS * HD])
        block = st.enter_context(nc.Block())
        c_ld, ld, y_st, cleared, scored, maxed, chain, weighed, turned, ev_a, ev_d, summed, o_out, back, y_done = (
            s[n] for n in ("c_ld", "ld", "y_st", "cleared", "scored", "maxed", "chain", "weighed", "turned", "ev_a",
                           "ev_d", "summed", "o_out", "back", "y_done"))
        banks = lambda nk: {t: (4 + t // 2, (t % 2) * 256) for t in range(5)} if nk == 5 else {0: (4, 0), 1: (5, 0)}

        def blocks(eng, body, last):
            for u in range(2):
                body(u, u, 0, 5, 1 - (u == 0), u > 0)
            with eng.Fori(1, NTL // 2 - 1) as i:
                for u in range(2):
                    body(2 * i + u, u, i, 5, 1, True)
            for u in range(2):
                body(NTL - 2 + u, u, NTL // 2 - 1, 5, 1 + u, True)
            if with_ctx:
                for u in range(2):
                    body(NTL + u, u, NTL // 2, 2, None, True)
                last(NT, 2)
            else:
                last(NTL, 5)

        @block.sync
        def _(sp):
            sp.dma_start(masks[:], io["window"]).then_inc(c_ld, 16)
            sp.dma_start(kx[:], d["ka"][:, CTX0:CTX0 + CTX]).then_inc(c_ld, 16)
            sp.dma_start(vx[:], d["va"][CTX0:CTX0 + CTX, :].rearrange("(c p) v -> p c v", p=P)).then_inc(c_ld, 16)
            sp.dma_start(sink[:], io["attn_sink"][l, :].partition_broadcast(P)).then_inc(c_ld, 16)
            sp.wait_ge(cleared, 1)

            def load(n, u, local):
                for g in range(A_KV):
                    sp.dma_start(qt[64 * g:64 * g + 64, u, 2 * g:2 * g + 2, :],
                                 d["qa"][g, :, bass.ds(n * P, P)].rearrange("(h e) t -> e h t", e=HD)).then_inc(ld[u], 16)
                if local:
                    sp.dma_start(kw[:, u, :], d["ka"][:, bass.ds(n * P, 3 * WIN)]).then_inc(ld[u], 16)
                    sp.dma_start(vw[:, u, :, :], d["va"][bass.ds(n * P, 3 * WIN), :].rearrange("(c p) v -> p c v", p=P)
                                 ).then_inc(ld[u], 16)

            def store(n, u):
                sp.wait_ge(y_done, n + 1)
                sp.dma_start(d["y"][bass.ds(n * P, P), 0:A_HEADS * HD], yt[:, u, :]).then_inc(y_st[u], 16)
            for u in range(2):
                sp.sem_inc(y_st[u], 16)
                load(u, u, True)

            def turn(i, local):
                for u in range(2):
                    sp.wait_ge(summed, 4 * i + (2 * u + 4))
                    load(2 * i + (u + 2), u, local)
                    store(2 * i + u, u)
            with sp.Fori(0, NTL // 2 - 1) as i:
                turn(i, True)
            if with_ctx:
                turn(NTL // 2 - 1, False)
            for u in range(2):
                store(BLOCKS - 2 + u, u)
            for u in range(2):
                sp.wait_ge(y_st[u], 16 + 16 * (BLOCKS // 2))

        @block.tensor
        def _(pe):
            pe.sem_inc(summed, 2)
            pe.sem_inc(turned, 2)
            pe.wait_ge(maxed, 1)
            pe.wait_ge(c_ld, 64)

            def score(n, u, g, nk, mask):
                for h in (2 * g, 2 * g + 1):
                    q = qt[:, u, h, :]
                    b = 2 * (h % 2)
                    pe.wait_ge(weighed, 4 * n + (h + 1))
                    mm = nc.tensor.matmul(ps[:, b, 0:CTX], q, kx[:], start=True, stop=True)
                    if nk == 5:
                        for dst, w in ((ps[:, b, CTX:512], slice(0, 256)), (ps[:, b + 1, 0:P], slice(256, 384))):
                            nc.tensor.matmul(dst, q, kw[:, u, w], start=True, stop=False)
                            mm = nc.tensor.matmul(dst, identb[:], maskb[:, mask, w], start=False, stop=True)
                    mm.then_inc(scored, 1)

            def turn(n, g, nk, more=None):
                pe.wait_ge(weighed, 4 * n + (2 * g + 4))
                pe.wait_ge(ev_a, 2 * n + (g + 1))
                pe.wait_ge(ev_d, 2 * n + (g + 1))
                for t in range(nk):
                    bank, at = banks(nk)[t]
                    if t == 4 and more is not None:
                        pe.wait_ge(y_done, more)
                    for h in range(2):
                        tr = nc.tensor.transpose(ps[:, bank, at + h * P:at + (h + 1) * P],
                                                 pr[:, 2 * g + h, t * P:(t + 1) * P], k.ident[:])
                tr.then_inc(turned, 1)

            def values(n, u, g, nk):
                pe.wait_ge(ev_a, 2 * n + (g + 2))
                pe.wait_ge(ev_d, 2 * n + (g + 2))
                if g == 0:
                    pe.wait_ge(o_out, n + 1)
                for t in range(nk):
                    v = vx[:, t, 64 * g:64 * g + 64] if t < 2 else vw[:, u, t - 2, 64 * g:64 * g + 64]
                    mm = nc.tensor.matmul(ps[64 * g:64 * g + 64, 7, 0:2 * P], v, pt[:, g, t, :],
                                          start=(t == 0), stop=(t == nk - 1))
                mm.then_inc(summed, 1)

            def turn_back(n):
                pe.wait_ge(o_out, n + 2)
                for h in range(2):
                    tr = nc.tensor.transpose(ps[:, 6, 256 + h * P:256 + (h + 1) * P], ot[:, h * P:(h + 1) * P], k.ident[:])
                tr.then_inc(back, 1)

            def body(n, u, i, nk, mask, before):
                pe.wait_ge(ld[u], 64 * i + (64 if nk == 5 else 32))
                score(n, u, 0, nk, mask)
                if before:
                    pnk = 2 if (nk == 2 and u == 1) else 5
                    turn(n - 1, 1, pnk)
                    values(n - 1, 1 - u, 1, pnk)
                score(n, u, 1, nk, mask)
                if before:
                    turn_back(n - 1)
                turn(n, 0, nk, n if before else None)
                values(n, u, 0, nk)

            def last(n, nk):
                turn(n - 1, 1, nk)
                values(n - 1, 1, 1, nk)
                turn_back(n - 1)
            blocks(pe, body, last)

        @block.scalar
        def _(act):
            act.sem_inc(ev_a, 1)
            act.sem_inc(weighed, 2)

            def weigh(n, u, h, nk):
                act.wait_ge(maxed, 4 * n + (h + 2))
                act.wait_ge(turned, 2 * n + (h // 2 + 1))
                width = NK if nk == 5 else CTX
                nc.scalar.activation(es[:, u, h:h + 1], sink[:, h:h + 1], ACT.Exp, bias=nm[:, u, h:h + 1])
                nc.scalar.activation(pr[:, h, 0:width], ps[:, 2 * (h % 2):2 * (h % 2) + 2, :].rearrange("p b t -> p (b t)")[:, 0:width],
                                     ACT.Exp, bias=nm[:, u, h:h + 1], scale=SCALE,
                                     accum_out=sums[:, u, h:h + 1]).then_inc(weighed, 1)

            def move(n, g, nk):
                act.wait_ge(turned, 2 * n + (g + 3))
                act.wait_ge(summed, 2 * n + (g + 1))
                if nk == 5:
                    nc.scalar.copy(pt[:, g, 4, :], ps[:, 6, 0:256])
                    nc.scalar.copy(pt[:, g, 0:2, :].rearrange("p t q -> p (t q)"), ps[:, 4, :]).then_inc(ev_a, 1)
                else:
                    nc.scalar.copy(pt[:, g, 0, :], ps[:, 4, 0:256]).then_inc(ev_a, 1)

            def body(n, u, i, nk, mask, before):
                weigh(n, u, 0, nk)
                weigh(n, u, 1, nk)
                if before:
                    move(n - 1, 1, 2 if (nk == 2 and u == 1) else 5)
                weigh(n, u, 2, nk)
                weigh(n, u, 3, nk)
                move(n, 0, nk)
            blocks(act, body, lambda n, nk: move(n - 1, 1, nk))

        @block.vector
        def _(dve):
            link = Chain(dve, chain)
            nc.vector.memset(qt[:], 0.0).then_inc(cleared, 1)
            dve.wait_ge(c_ld, 64)
            nc.vector.tensor_copy(maskb[:], masks[:])
            nc.vector.tensor_copy(identb[:], k.ident[:])
            nc.vector.tensor_scalar(nsink[:], sink[:], -1.0, None, ALU.mult).then_inc(maxed, 1)
            dve.wait_ge(maxed, 1)
            dve.sem_inc(ev_d, 1)
            dve.sem_inc(o_out, 1)

            def most(n, u, h, nk):
                dve.wait_ge(scored, 4 * n + (h + 1))
                width = NK if nk == 5 else CTX
                link(nc.vector.reduce_max(mx[:, u, h:h + 1], ps[:, 2 * (h % 2):2 * (h % 2) + 2, :].rearrange("p b t -> p (b t)")[:, 0:width], AX.X))
                nc.vector.tensor_scalar(nm[:, u, h:h + 1], mx[:, u, h:h + 1], -SCALE, nsink[:, h:h + 1],
                                        ALU.mult, ALU.min).then_inc(maxed, 1)

            def move(n, g, nk):
                dve.wait_ge(turned, 2 * n + (g + 3))
                dve.wait_ge(summed, 2 * n + (g + 1))
                if nk == 5:
                    nc.vector.tensor_copy(pt[:, g, 2:4, :].rearrange("p t q -> p (t q)"), ps[:, 5, :]).then_inc(ev_d, 1)
                else:
                    nc.vector.tensor_copy(pt[:, g, 1, :], ps[:, 5, 0:256]).then_inc(ev_d, 1)

            def take_sums(n):
                dve.wait_ge(summed, 2 * n + 4)
                dve.wait_ge(back, n) if not isinstance(n, int) or n > 0 else None
                nc.vector.tensor_copy(ot[:], ps[:, 7, 0:2 * P]).then_inc(o_out, 1)

            def finish(n, u, turn_of):
                dve.wait_ge(weighed, 4 * n + 6)
                link(nc.vector.tensor_tensor(rs[:, u, :], sums[:, u, :], es[:, u, :], ALU.add))
                link(nc.vector.reciprocal(rs[:, u, :], rs[:, u, :]))
                dve.wait_ge(back, n + 1)
                dve.wait_ge(y_st[u], turn_of)
                nc.vector.tensor_tensor(
                    yt[:, u, :].rearrange("p (g h e) -> p h g e", g=2, h=2),
                    ps[:, 6, 256:512].rearrange("p (h g e) -> p h g e", h=2, g=2),
                    rs[:, u, :].rearrange("p (g h) -> p h g", g=2).unsqueeze(3).to_broadcast([P, 2, 2, HD]),
                    ALU.mult).then_inc(y_done, 1)

            def body(n, u, i, nk, mask, before):
                link.turn(6 * n - 2 if before else 0)
                most(n, u, 0, nk)
                most(n, u, 1, nk)
                if before:
                    move(n - 1, 1, 2 if (nk == 2 and u == 1) else 5)
                    take_sums(n - 1)
                most(n, u, 2, nk)
                most(n, u, 3, nk)
                if before:
                    finish(n - 1, 1 - u, 16 * i + 16 * u)
                move(n, 0, nk)

            def last(n, nk):
                link.turn(6 * n - 2)
                move(n - 1, 1, nk)
                take_sums(n - 1)
                finish(n - 1, 1, 16 * (BLOCKS // 2))
            blocks(dve, body, last)


UB = 4
GB = 2
GQ = GB * P
NG = SEQ // GQ
TURNS = SEQ // (UB * P)
VHALF = NT // 2
VALUE_PARTS = ((0, 5), (5, 9), (9, 14), (14, 18))
PIECES = ((0, 4), (4, 4), (8, 4), (12, 4), (16, 2))
MAX_PARTS = ((0, 512, (0,)), (512, 1536, (1, 2)), (1536, TOK, (3, 4)))
EXP_PARTS = ((0, 1024, (0, 1)), (1024, 1536, (2,)), (1536, TOK, (3, 4)))


def stack_loads(sp, sem, d, dst_q, dst_k, h, m, q_span, k_span):
    rows = bass.ds(h * (2 * B_QK) + m * B_QK, B_QK)
    q = lambda part: d["qkb"][0, part, rows, q_span]
    kk = lambda part: d["qkb"][1, part, rows, k_span]
    for dst, part, order in ((dst_q, q, ((0, 0, 1, 1), (0, 1, 2, 2))), (dst_k, kk, ((0, 1, 0, 1), (2, 2, 0, 1)))):
        for a in range(2):
            for n in range(4):
                sp.dma_start(dst(m, a)[B_QK * n:B_QK * n + B_QK], part(order[a][n])).then_inc(sem, 16)


STACK_LOADS = 32


def lambdas(k, l, s, nlam):
    nc, io = k.nc, k.io
    with ExitStack() as st:
        sb = k.buffers(st)
        lv, pv, e, li = sb("lv", [P, 4, B_QK]), sb("pv", [P, 2, B_QK]), sb("e", [P, 2]), sb("li", [P, 1])
        ld, steps, exps = s["lam_ld"], s["lam_steps"], s["lam_exps"]
        block = st.enter_context(nc.Block())

        @block.sync
        def _(sp):
            sp.dma_start(lv[:], io["diff_lambda"][l, :, :].partition_broadcast(P)).then_inc(ld, 16)
            sp.dma_start(li[:], io["lam_init"][l, 0:1].partition_broadcast(P)).then_inc(ld, 16)

        @block.vector
        def _(dve):
            link = Chain(dve, steps)
            dve.wait_ge(ld, 32)
            pairs = lv[:].rearrange("p (a b) e -> p a b e", b=2)
            link(nc.vector.tensor_tensor(pv[:], pairs[:, :, 0, :], pairs[:, :, 1, :], ALU.mult))
            link(nc.vector.reduce_sum(e[:], pv[:], AX.X))
            dve.wait_ge(exps, 1)
            link(nc.vector.tensor_tensor(e[:, 1:2], e[:, 1:2], e[:, 0:1], ALU.subtract))
            link(nc.vector.tensor_tensor(nlam[:], e[:, 1:2], li[:], ALU.subtract))

        @block.scalar
        def _(act):
            act.wait_ge(steps, 2)
            nc.scalar.activation(e[:], e[:], ACT.Exp).then_inc(exps, 1)


def differential(k, l, s, nlam):
    nc, io, d, ps = k.nc, k.io, k.d, k.ps
    SCALE = B_QK ** -0.5
    with ExitStack() as st:
        sb = k.buffers(st)
        kst = sb("kst", [P, 2, 2, 2, TOK], BF16)
        qst = sb("qst", [P, 2, 2, 2, SEQ], BF16)
        vt = sb("vt", [P, NT, HD])
        pr = sb("pr", [P, 2, 2, TOK])
        pt = sb("pt", [P, 2, NT, GQ])
        mx = sb("mx", [P, 2, 4])
        nm, rl, ls = (sb(n, [P, 2, 2]) for n in ("nm", "rl", "ls"))
        sums = sb("sums", [P, 2, 2, len(EXP_PARTS)])
        cc = sb("cc", [P, 2, 1])
        recent = sb("recent", [P, 2 * UB])
        ot = sb("ot", [P, GQ])
        yt = sb("yt", [P, 2, GB, HD])
        block = st.enter_context(nc.Block())
        s_ld, v_ld, y_st = s["s_ld"], s["v_ld"], s["y_st"]
        v_ready, cleared, scored, maxed, chain, weighed, mixed, turned, ev_a, ev_d, half_summed, summed, o_out, back, y_done = (
            s[n] for n in ("v_ready", "cleared", "scored", "maxed", "chain", "weighed", "mixed", "turned",
                           "ev_a", "ev_d", "half_summed", "summed", "o_out", "back", "y_done"))
        STEPS = 8 * UB + 1
        MISSED = 5
        MX, EX = len(MAX_PARTS), len(EXP_PARTS)
        row = ps[:, 0:5, :].rearrange("p b t -> p (b t)")

        class Turn:
            def __init__(self, lead, tail=False):
                self.lead, self.tail = lead, tail
                self.blocks = range(UB + 1 if tail else UB)

            def block(self, at):
                return UB * self.lead + at >= 0 and (at < 0 or not self.tail)

            def group(self, at):
                return 2 * self.lead + at >= 0 and (at < 0 or not self.tail)

        def turns(eng, body):
            body(0, 0, 0, 0, Turn(0))
            body(0, 0, 1, 1, Turn(1))
            with eng.Fori(2, TURNS) as g:
                body(0, 0, g, g, Turn(2))
            with eng.Fori(0, TURNS) as g:
                body(1, 1, g, TURNS + g, Turn(2))
            with eng.Fori(1, B_HEADS // 2) as i:
                for u in range(2):
                    with eng.Fori(0, TURNS) as g:
                        body(2 * i + u, u, g, i * (2 * TURNS) + g + u * TURNS, Turn(2))
            body(None, None, None, TURNS * B_HEADS, Turn(2, True))

        @block.sync
        def _(sp):
            def stacks(h, hs):
                for m in range(2):
                    stack_loads(sp, s_ld, d, lambda m, a: qst[:, hs, m, a, :], lambda m, a: kst[:, hs, m, a, :],
                                h, m, slice(0, SEQ), slice(0, TOK))

            def values(h, half):
                t0 = half * VHALF
                sp.dma_start(vt[:, t0:t0 + VHALF, :], d["nat"][t0 * P:(t0 + VHALF) * P, bass.ds(h * HD + VB, HD)]
                             .rearrange("(c p) v -> p c v", p=P)).then_inc(v_ld[half], 16)

            def store(h, w, g, slot):
                sp.wait_ge(y_done, w + 1)
                sp.dma_start(d["y"][bass.ds(g * GQ, GQ), bass.ds(h * HD + 256, HD)].rearrange("(b p) e -> p b e", p=P),
                             yt[:, slot, :, :]).then_inc(y_st[slot], 16)

            for slot in range(2):
                sp.sem_inc(y_st[slot], 16)
                values(0, slot)
            stacks(0, 0)
            for half in range(2):
                sp.wait_ge(v_ld[half], 16)
                sp.sem_inc(v_ready[half], NG)
            sp.wait_ge(s_ld, 16 * STACK_LOADS)
            stacks(1, 1)

            for h in range(B_HEADS):
                more = h + 1 < B_HEADS
                with sp.Fori(0, NG // 2 - 1) as i:
                    for u in range(2):
                        store(h, 2 * i + (h * NG + u), 2 * i + u, u)
                if more:
                    sp.wait_ge(half_summed, NG * (h + 1))
                    values(h + 1, 0)
                store(h, h * NG + NG - 2, NG - 2, 0)
                if more:
                    sp.wait_ge(summed, NG * (h + 1))
                    values(h + 1, 1)
                    for half in range(2):
                        sp.wait_ge(v_ld[half], 16 * (h + 2))
                        sp.sem_inc(v_ready[half], NG)
                if h + 2 < B_HEADS:
                    sp.wait_ge(s_ld, 16 * STACK_LOADS * (h + 2))
                    stacks(h + 2, h % 2)
                store(h, h * NG + NG - 1, NG - 1, 1)
            for slot in range(2):
                sp.wait_ge(y_st[slot], 16 + 16 * NG * B_HEADS // 2)

        @block.tensor
        def _(pe):
            def score(n, hs, q0, m):
                for bank in range(5):
                    for e, (lo, hi, banks) in enumerate(EXP_PARTS):
                        if bank == banks[0]:
                            pe.wait_ge(weighed, 2 * EX * n + (EX * m + e + 1))
                    w = min(512, TOK - 512 * bank)
                    for a in range(2):
                        mm = nc.tensor.matmul(ps[:, bank, 0:w], qst[:, hs, m, a, bass.ds(q0, P)],
                                              kst[:, hs, m, a, 512 * bank:512 * bank + w], start=(a == 0), stop=(a == 1))
                    if any(bank == banks[-1] for _, _, banks in MAX_PARTS):
                        mm.then_inc(scored, 1)

            def turn(n, v, pieces):
                for j in pieces:
                    t0, nt = PIECES[j]
                    if j == 0:
                        pe.wait_ge(mixed, 2 * n + 1)
                        pe.wait_ge(ev_d, n + 1)
                    if j == 2:
                        pe.wait_ge(mixed, 2 * n + 2)
                    if j > 0:
                        pe.wait_ge(ev_a, 4 * n + j)
                    for t in range(nt):
                        tr = nc.tensor.transpose(ps[:, 5 + j % 2, t * P:(t + 1) * P],
                                                 pr[:, v, 0, (t0 + t) * P:(t0 + t + 1) * P], k.ident[:])
                    tr.then_inc(turned, 1)

            def values(w, slot, part):
                if part == 0:
                    pe.wait_ge(v_ready[0], w + 1)
                    pe.wait_ge(ev_a, 8 * w + 7)
                    pe.wait_ge(o_out, w + 1)
                if part == 1:
                    pe.wait_ge(ev_a, 8 * w + 9)
                    pe.wait_ge(ev_d, 2 * w + 3)
                if part == 2:
                    pe.wait_ge(v_ready[1], w + 1)
                for t in range(*VALUE_PARTS[part]):
                    mm = nc.tensor.matmul(ps[0:HD, 7, 0:GQ], vt[:, t, :], pt[:, slot, t, :], start=(t == 0), stop=(t == NT - 1))
                if part == 1:
                    mm.then_inc(half_summed, 1)
                if part == 3:
                    mm.then_inc(summed, 1)

            def turn_back():
                for b in range(GB):
                    tr = nc.tensor.transpose(ps[:, 5, 256 + b * P:256 + (b + 1) * P], ot[:, b * P:(b + 1) * P], k.ident[:])
                tr.then_inc(back, 1)

            def body(h, hs, g, w, at):
                if not at.tail:
                    pe.wait_ge(s_ld, 16 * STACK_LOADS * h + 16 * STACK_LOADS)
                for b in at.blocks:
                    n, even, gr = UB * w + b, b % 2 == 0, b // 2
                    slot = gr % 2
                    if not at.tail:
                        score(n, hs, g * (UB * P) + b * P, 0)
                    out = even and at.group(gr - 3)
                    if at.block(b - 2):
                        turn(n - 2, b % 2, (2, 3))
                        pe.wait_ge(ev_a, 4 * (n - 2) + 4)
                    if out:
                        pe.wait_ge(o_out, 2 * w + (gr - 3 + 2))
                        turn_back()
                    if at.block(b - 2):
                        turn(n - 2, b % 2, (4,))
                    if at.group(gr - 2):
                        values(2 * w + (gr - 2), slot, 1 if even else 3)
                    if not at.tail:
                        score(n, hs, g * (UB * P) + b * P, 1)
                    if at.block(b - 1):
                        if even and at.group(gr - 3):
                            pe.wait_ge(y_done, 2 * w + (gr - 3 + 1))
                        turn(n - 1, (b - 1) % 2, (0, 1))
                    if even and at.group(gr - 2):
                        values(2 * w + (gr - 2), slot, 2)
                    if not even and at.group(gr - 1):
                        values(2 * w + (gr - 1), 1 - slot, 0)
            turns(pe, body)

        @block.scalar
        def _(act):
            act.sem_inc(weighed, EX)
            act.sem_inc(ev_a, 1)

            def weigh(n, v, m, old):
                act.wait_ge(maxed, 2 * n + (m + 1))
                for e, (lo, hi, banks) in enumerate(EXP_PARTS):
                    if m == 0 and e == EX - 1 and old:
                        act.wait_ge(turned, 5 * (n - 2) + 5)
                    nc.scalar.activation(pr[:, v, m, lo:hi], row[:, lo:hi], ACT.Exp, bias=nm[:, v, m:m + 1],
                                         scale=SCALE, accum_out=sums[:, v, m, e:e + 1]).then_inc(weighed, 1)

            def move(n, at, j):
                t0, nt = PIECES[j]
                act.wait_ge(turned, 5 * n + (j + 1))
                nc.scalar.copy(pt[:, at // 2, t0:t0 + nt, (at % 2) * P:(at % 2 + 1) * P],
                               ps[:, 5 + j % 2, 0:nt * P].rearrange("p (t q) -> p t q", q=P)).then_inc(ev_a, 1)

            def body(h, hs, g, w, at):
                for b in at.blocks:
                    n, v = UB * w + b, b % 2
                    old, last = at.block(b - 2), at.block(b - 1)
                    if old:
                        move(n - 2, (b - 2) % UB, 2)
                    if not at.tail:
                        weigh(n, v, 0, old)
                    if old:
                        move(n - 2, (b - 2) % UB, 3)
                    if last:
                        if b % 2 == 1 and at.group(b // 2 - 2):
                            act.wait_ge(summed, 2 * w + (b // 2 - 1))
                        move(n - 1, (b - 1) % UB, 0)
                    if not at.tail:
                        weigh(n, v, 1, old)
                    if last:
                        move(n - 1, (b - 1) % UB, 1)
            turns(act, body)

        @block.vector
        def _(dve):
            link = Chain(dve, chain)
            for counter in (ev_d, o_out, back):
                dve.sem_inc(counter, 1)
            nc.vector.memset(ot[:], 0.0)
            nc.vector.memset(recent[:], 1.0).then_inc(cleared, 1)
            dve.wait_ge(cleared, 1)

            def most(n, v, m):
                for j, (lo, hi, banks) in enumerate(MAX_PARTS):
                    dve.wait_ge(scored, 2 * MX * n + (MX * m + j + 1))
                    op = nc.vector.reduce_max(mx[:, m, j:j + 1], row[:, lo:hi], AX.X)
                    if j == 1:
                        link(op)
                        nc.vector.tensor_scalar(mx[:, m, 3:4], mx[:, m, 0:1], mx[:, m, 1:2], None, ALU.max)
                link(op)
                nc.vector.tensor_scalar(nm[:, v, m:m + 1], mx[:, m, 2:3], mx[:, m, 3:4], -SCALE,
                                        ALU.max, ALU.mult).then_inc(maxed, 1)

            def factors(n, v, b):
                dve.wait_ge(weighed, 2 * EX * n + 3 * EX)
                link(nc.vector.reduce_sum(ls[:, v, :], sums[:, v, :, :], AX.X))
                link(nc.vector.reciprocal(rl[:, v, :], ls[:, v, :]))
                link(nc.vector.tensor_copy(recent[:, UB + b:UB + b + 1], rl[:, v, 0:1]))
                link(nc.vector.scalar_tensor_tensor(out=cc[:, v, :], in0=ls[:, v, 0:1], scalar=nlam[:], in1=rl[:, v, 1:2],
                                                    op0=ALU.mult, op1=ALU.mult))

            def mix(v, lo, hi):
                nc.vector.scalar_tensor_tensor(out=pr[:, v, 0, lo:hi], in0=pr[:, v, 1, lo:hi], scalar=cc[:, v, :],
                                               in1=pr[:, v, 0, lo:hi], op0=ALU.mult, op1=ALU.add).then_inc(mixed, 1)

            def move(n, at):
                t0, nt = PIECES[4]
                dve.wait_ge(turned, 5 * n + 5)
                nc.vector.tensor_copy(pt[:, at // 2, t0:t0 + nt, (at % 2) * P:(at % 2 + 1) * P],
                                      ps[:, 5, 0:nt * P].rearrange("p (t q) -> p t q", q=P)).then_inc(ev_d, 1)

            def take_sums(w):
                dve.wait_ge(summed, w + 1)
                dve.wait_ge(back, w + 1)
                nc.vector.tensor_copy(ot[0:HD, :], ps[0:HD, 7, 0:GQ]).then_inc(o_out, 1)

            def finish(w, slot, stored, r):
                dve.wait_ge(back, w + 2)
                dve.wait_ge(y_st[slot], stored)
                nc.vector.tensor_tensor(yt[:, slot, :, :], ps[:, 5, 256:512].rearrange("p (b e) -> p b e", e=P)[:, :, 0:HD],
                                        recent[:, r:r + GB].unsqueeze(2).to_broadcast([P, GB, HD]), ALU.mult).then_inc(y_done, 1)

            def body(h, hs, g, w, at):
                link.turn(w * STEPS - (MISSED if at.lead else 0))
                for b in at.blocks:
                    n, v, gr = UB * w + b, b % 2, b // 2
                    if not at.tail:
                        most(n, v, 0)
                    if at.block(b - 2):
                        move(n - 2, (b - 2) % UB)
                    if b % 2 == 0 and at.group(gr - 3):
                        if b == 0:
                            finish(2 * w - 3, 1, 16 * w - 16, UB - 1)
                        elif b == 2:
                            finish(2 * w - 2, 0, 16 * w, 1)
                        else:
                            finish(2 * w - 1, 1, 16 * w, UB - 1)
                    if b == 0 and at.lead:
                        if at.group(-3):
                            dve.wait_ge(y_done, 2 * w - 2)
                        link(nc.vector.tensor_copy(recent[:, 0:UB], recent[:, UB:]))
                    if at.block(b - 1):
                        factors(n - 1, 1 - v, b)
                        mix(1 - v, 0, 1024)
                    if b % 2 == 1 and at.group(gr - 2):
                        take_sums(2 * w + (gr - 2))
                    if not at.tail:
                        most(n, v, 1)
                    if at.block(b - 1):
                        mix(1 - v, 1024, TOK)
                assert at.tail or link.n == STEPS - (0 if at.lead else MISSED)
            turns(dve, body)


def differential_context(k, l, s, nlam):
    nc, io, d, ps = k.nc, k.io, k.d, k.ps
    SCALE = B_QK ** -0.5
    QB = CTX // P
    with ExitStack() as st:
        sb = k.buffers(st)
        kst = sb("kst", [P, 2, 2, 2, CTX], BF16)
        qst = sb("qst", [P, 2, 2, 2, CTX], BF16)
        vt = sb("vt", [P, 2, QB, HD])
        pr = sb("pr", [P, QB, 2, CTX])
        pt = sb("pt", [P, QB, CTX])
        mx, nm, sums, rl = (sb(n, [P, QB, 2]) for n in ("mx", "nm", "sums", "rl"))
        cc = sb("cc", [P, QB, 1])
        ot = sb("ot", [P, CTX])
        yt = sb("yt", [P, QB, B_HEADS, HD])
        block = st.enter_context(nc.Block())
        s_ld, y_st, cleared, scored, chain, weighed, turned, summed, back = (
            s[n] for n in ("xs_ld", "xy_st", "x_cleared", "x_scored", "x_chain", "x_weighed", "x_turned", "x_summed", "x_back"))
        LOADS = STACK_LOADS + 1
        STEPS = 9
        ctx = slice(SEQ, TOK)

        def heads(eng, body):
            with eng.Fori(0, B_HEADS // 2) as i:
                for u in range(2):
                    body(2 * i + u, u, i)

        @block.sync
        def _(sp):
            def load(h, u):
                for m in range(2):
                    stack_loads(sp, s_ld[u], d, lambda m, a: qst[:, u, m, a, :], lambda m, a: kst[:, u, m, a, :], h, m, ctx, ctx)
                sp.dma_start(vt[:, u, :, :], d["nat"][SEQ:TOK, bass.ds(h * HD + VB, HD)].rearrange("(c p) v -> p c v", p=P)
                             ).then_inc(s_ld[u], 16)
            for u in range(2):
                load(u, u)
            with sp.Fori(0, B_HEADS // 2 - 1) as i:
                for u in range(2):
                    sp.wait_ge(summed, 2 * i + (u + 1))
                    load(2 * i + (u + 2), u)
            sp.wait_ge(chain, STEPS * B_HEADS)
            sp.dma_start(d["y"][ctx, 256:640].rearrange("(b p) e -> p b e", p=P),
                         yt[:].rearrange("p b h e -> p b (h e)")).then_inc(y_st, 16)
            sp.wait_ge(y_st, 16)

        @block.tensor
        def _(pe):
            pe.wait_ge(cleared, 1)

            def body(h, u, i):
                pe.wait_ge(s_ld[u], 16 * LOADS * i + 16 * LOADS)
                for b in range(QB):
                    for m in range(2):
                        for a in range(2):
                            mm = nc.tensor.matmul(ps[:, b, m * CTX:(m + 1) * CTX], qst[:, u, m, a, b * P:(b + 1) * P],
                                                  kst[:, u, m, a, :], start=(a == 0), stop=(a == 1))
                mm.then_inc(scored, 1)
                pe.wait_ge(chain, STEPS * h + 6)
                for t in range(QB):
                    for b in range(QB):
                        tr = nc.tensor.transpose(ps[:, 2, (2 * t + b) * P:(2 * t + b + 1) * P],
                                                 pr[:, b, 0, t * P:(t + 1) * P], k.ident[:])
                tr.then_inc(turned, 1)
                pe.wait_ge(chain, STEPS * h + 7)
                for t in range(QB):
                    mm = nc.tensor.matmul(ps[0:HD, 3, 0:CTX], vt[:, u, t, :], pt[:, t, :], start=(t == 0), stop=(t == QB - 1))
                mm.then_inc(summed, 1)
                pe.wait_ge(chain, STEPS * h + 8)
                for b in range(QB):
                    tr = nc.tensor.transpose(ps[:, 4, b * P:(b + 1) * P], ot[:, b * P:(b + 1) * P], k.ident[:])
                tr.then_inc(back, 1)
            heads(pe, body)

        @block.scalar
        def _(act):
            def body(h, u, i):
                act.wait_ge(chain, STEPS * h + 2)
                for b in range(QB):
                    for m in range(2):
                        nc.scalar.activation(pr[:, b, m, :], ps[:, b, m * CTX:(m + 1) * CTX], ACT.Exp,
                                             bias=nm[:, b, m:m + 1], scale=SCALE,
                                             accum_out=sums[:, b, m:m + 1]).then_inc(weighed, 1)
            heads(act, body)

        @block.vector
        def _(dve):
            link = Chain(dve, chain)
            nc.vector.memset(ot[:], 0.0).then_inc(cleared, 1)

            def body(h, u, i):
                link.turn(STEPS * h)
                dve.wait_ge(scored, h + 1)
                link(nc.vector.reduce_max(mx[:], ps[:, 0:QB, :].rearrange("p b (m t) -> p b m t", m=2), AX.X))
                link(nc.vector.tensor_scalar(nm[:], mx[:], -SCALE, None, ALU.mult))
                dve.wait_ge(weighed, 4 * h + 4)
                link(nc.vector.reciprocal(rl[:], sums[:]))
                for b in range(QB):
                    op = nc.vector.scalar_tensor_tensor(out=cc[:, b, :], in0=sums[:, b, 0:1], scalar=nlam[:],
                                                        in1=rl[:, b, 1:2], op0=ALU.mult, op1=ALU.mult)
                link(op)
                for b in range(QB):
                    link(nc.vector.scalar_tensor_tensor(out=pr[:, b, 0, :], in0=pr[:, b, 1, :], scalar=cc[:, b, :],
                                                        in1=pr[:, b, 0, :], op0=ALU.mult, op1=ALU.add))
                dve.wait_ge(turned, h + 1)
                link(nc.vector.tensor_copy(pt[:].rearrange("p t q -> p (t q)"), ps[:, 2, :]))
                dve.wait_ge(summed, h + 1)
                link(nc.vector.tensor_copy(ot[0:HD, :], ps[0:HD, 3, 0:CTX]))
                dve.wait_ge(back, h + 1)
                link(nc.vector.tensor_tensor(yt[:, :, bass.ds(h, 1), :].rearrange("p b o e -> p b (o e)"),
                                             ps[:, 4, 0:CTX].rearrange("p (b t) -> p b t", b=QB)[:, :, 0:HD],
                                             rl[:, :, 0:1].to_broadcast([P, QB, HD]), ALU.mult))
                assert link.n == STEPS
            heads(dve, body)


def output(k, l, s, with_ctx):
    nc, io, d, ps = k.nc, k.io, k.d, k.ps
    NH = B_HEADS + C_HEADS
    A = A_HEADS * HD
    W = 512
    with ExitStack() as st:
        sb = k.buffers(st)
        wo = sb("wo", [P, KT, DM])
        gn = sb("gn", [P, NH, HD])
        keep = sb("keep", [P, 1])
        gate = sb("gate", [P, 2, DM])
        lng, lnb = sb("lng", [P, DM]), sb("lnb", [P, DM])
        xt, yt, gt = (sb(n, [P, 2, DM]) for n in ("xt", "yt", "gt"))
        sq = sb("sq", [P, 2, NH, HD])
        ss, sr, rr = (sb(n, [P, 2, NH]) for n in ("ss", "sr", "rr"))
        yT = sb("yT", [P, 2, KT, P])
        res = sb("res", [P, 2, DM])
        ot = sb("ot", [P, 2, DM])
        bn = sb("bn", [P, 2, 2, 6])
        mv, sd = sb("mv", [P, 2, 2]), sb("sd", [P, 2, 2])
        block = st.enter_context(nc.Block())
        w_ld, ld, x_ld, o_st, squared, steps, roots, ready, turned, moved, prod, taken, centred, done = (
            s[n] for n in ("w_ld", "ld", "x_ld", "o_st", "squared", "steps", "roots", "ready", "turned", "moved",
                           "prod", "taken", "centred", "done"))
        N = NT if with_ctx else NTL
        PRE, POST = 4, 5

        def tiles(eng, first, body):
            first()
            with eng.Fori(0, NTL // 2 - 1) as i:
                for u in range(2):
                    body(2 * i + u, u, i, 0, True)
            for u in range(2):
                body(NTL - 2 + u, u, NTL // 2 - 1, 0, u == 0 or with_ctx)
            if with_ctx:
                for u in range(2):
                    body(NTL + u, u, NTL // 2, 1, u == 0)

        @block.sync
        def _(sp):
            def load_x(t, u):
                sp.dma_start(xt[:, u, :], d["x"][bass.ds(t * P, P), :]).then_inc(x_ld[u], 16)

            def load(t, u):
                rows = bass.ds(t * P, P)
                sp.dma_start(yt[:, u, :], d["y"][rows, :]).then_inc(ld[u], 16)
                for lo, hi, src in ((0, A, SA), (A, A + 384, SB), (A + 384, DM, SC)):
                    sp.dma_start(gt[:, u, lo:hi], d["nat"][rows, src:src + hi - lo]).then_inc(ld[u], 16)

            target = d["x"] if with_ctx else k.out

            def store(t, u):
                sp.wait_ge(done, t + 3)
                sp.dma_start(target[bass.ds(t * P, P), :], ot[:, u, :]).then_inc(o_st[u], 16)
            for u in range(2):
                sp.sem_inc(o_st[u], 16)
                load(u, u)
                load_x(u, u)
            for h in range(B_HEADS):
                sp.dma_start(gn[:, h, :], io["diff_norm_g"][l, :].partition_broadcast(P)).then_inc(w_ld, 16)
            sp.dma_start(gn[:, B_HEADS:, :].rearrange("p h e -> p (h e)"), io["mlstm_norm_g"][l, :].partition_broadcast(P)).then_inc(w_ld, 16)
            sp.dma_start(keep[:], io["lam_keep"][l, 0:1].partition_broadcast(P)).then_inc(w_ld, 16)
            for r in range(2):
                sp.dma_start(gate[:, r, :], d["mod"][r, 2 * DM:].partition_broadcast(P)).then_inc(w_ld, 16)
            sp.dma_start(lng[:], io["ln_g"][l, :].partition_broadcast(P)).then_inc(w_ld, 16)
            sp.dma_start(lnb[:], io["ln_b"][l, :].partition_broadcast(P)).then_inc(w_ld, 16)
            sp.dma_start(wo[:], io["w_out"][l, :, :, :]).then_inc(w_ld, 16)

            def next_y(t, u):
                sp.wait_ge(turned, t)
                load(t, u)

            def next_x(t, u):
                sp.wait_ge(s["varied"], t - 1)
                load_x(t, u)
            next_y(2, 0)
            next_y(3, 1)
            next_x(2, 0)
            with sp.Fori(0, N // 2 - 2) as i:
                for u in range(2):
                    next_y(2 * i + (4 + u), u)
                    next_x(2 * i + (3 + u), 1 - u)
                    store(2 * i + u, u)
            next_x(N - 1, 1)
            for t in range(N - 4, N):
                store(t, t % 2)
            for u in range(2):
                sp.wait_ge(o_st[u], 16 + 16 * (N // 2))

        @block.tensor
        def _(pe):
            pe.sem_inc(turned, 1)

            def turn(t, u):
                pe.wait_ge(ready, t + 1)
                pe.wait_ge(moved, t + 1)
                for j in range(KT):
                    tr = nc.tensor.transpose(ps[:, j // 4, (j % 4) * P:(j % 4 + 1) * P], yt[:, u, j * P:(j + 1) * P], k.ident[:])
                tr.then_inc(turned, 1)

            def product(t, u, more):
                pe.wait_ge(moved, t + 2)
                pe.wait_ge(taken, t + 1)
                for n in range(DM // W):
                    for j in range(KT):
                        if more and (n, j) == (1, KT // 2):
                            turn(t + 1, 1 - u)
                        mm = nc.tensor.matmul(ps[:, 2 + 2 * u + n, :], yT[:, u, j, :], wo[:, j, n * W:(n + 1) * W],
                                              start=(j == 0), stop=(j == KT - 1))
                mm.then_inc(prod, 1)

            def first():
                turn(0, 0)
                pe.wait_ge(w_ld, 16 * (B_HEADS + 7))

            def body(t, u, i, r, more):
                product(t, u, more)
            tiles(pe, first, body)

        @block.gpsimd
        def _(pool):
            pool.sem_inc(done, 2)
            pool.sem_inc(s["scaled"], 2)

            def after(t, u, i):
                pool.wait_ge(centred, t + 1)
                pool.wait_ge(o_st[u], 16 * i + 16)
                nc.gpsimd.tensor_tensor(ot[:, u, :], res[:, u, :], lng[:], ALU.mult).then_inc(s["scaled"], 1)
                pool.wait_ge(s["scaled"], t + 3)
                nc.gpsimd.tensor_tensor(ot[:, u, :], ot[:, u, :], lnb[:], ALU.add).then_inc(done, 1)

            tiles(pool, lambda: None, lambda t, u, i, r, more: after(t, u, i))

        @block.scalar
        def _(act):
            act.sem_inc(moved, 1)

            def before(t, u, i):
                act.wait_ge(ld[u], 64 * i + 64)
                nc.scalar.square(sq[:, u, :, :], yt[:, u, A:].rearrange("p (h e) -> p h e", e=HD)).then_inc(squared, 1)
                act.wait_ge(s["summed"], t + 1)
                nc.scalar.sqrt(sr[:, u, :], ss[:, u, :]).then_inc(roots, 1)
                act.wait_ge(turned, t + 2)
                for n in range(2):
                    op = nc.scalar.copy(yT[:, u, 4 * n:4 * n + 4, :].rearrange("p k t -> p (k t)"), ps[:, n, :])
                op.then_inc(moved, 1)

            def after(t, u):
                act.wait_ge(s["varied"], t + 1)
                nc.scalar.sqrt(sd[:, u, 0:1], mv[:, u, 1:2]).then_inc(s["rooted"], 1)

            def body(t, u, i, r, more):
                if more:
                    before(t + 1, 1 - u, i + u)
                after(t, u)
            tiles(act, lambda: before(0, 0, 0), body)

        @block.vector
        def _(dve):
            dve.sem_inc(taken, 2)
            dve.wait_ge(w_ld, 16 * (B_HEADS + 7))
            gb = gn[:, 0:B_HEADS, :]
            nc.vector.tensor_scalar(gb, gb, keep[:], None, ALU.mult).then_inc(s["gn_ready"], 1)
            dve.wait_ge(s["gn_ready"], 1)
            link = Chain(dve, steps)

            def before(t, u, i):
                dve.wait_ge(squared, t + 1)
                link(nc.vector.reduce_sum(ss[:, u, :], sq[:, u, :, :], AX.X))
                nc.vector.tensor_scalar(ss[:, u, :], ss[:, u, :], 1.0 / HD, EPS, ALU.mult, ALU.add).then_inc(s["summed"], 1)
                dve.wait_ge(roots, t + 1)
                link(nc.vector.reciprocal(rr[:, u, :], sr[:, u, :]))
                y = yt[:, u, A:].rearrange("p (h e) -> p h e", e=HD)
                link(nc.vector.tensor_tensor(y, y, rr[:, u, :].unsqueeze(2).to_broadcast([P, NH, HD]), ALU.mult))
                link(nc.vector.tensor_tensor(y, y, gn[:], ALU.mult))
                nc.vector.tensor_tensor(yt[:, u, :], yt[:, u, :], gt[:, u, :], ALU.mult).then_inc(ready, 1)

            def after(t, u, i, r):
                dve.wait_ge(prod, t + 1)
                dve.wait_ge(x_ld[u], 16 * i + 16)
                dve.wait_ge(s["scaled"], t + 1)
                link(nc.vector.tensor_tensor(res[:, u, :], ps[:, 2 + 2 * u:4 + 2 * u, :].rearrange("p n w -> p (n w)"),
                                             gate[:, r, :], ALU.mult))
                dve.sem_inc(taken, 1)
                link(nc.vector.scalar_tensor_tensor(out=res[:, u, :], in0=xt[:, u, :], scalar=ALPHA, in1=res[:, u, :],
                                                    op0=ALU.mult, op1=ALU.add))
                for n in range(2):
                    op = nc.vector.bn_stats(bn[:, u, n, :], res[:, u, n * W:(n + 1) * W])
                link(op)
                nc.vector.memset(sd[:, u, 1:2], 0.0)
                link(nc.vector.bn_aggr(mv[:, u, :], bn[:, u, :, :].rearrange("p n s -> p (n s)")))
                nc.vector.tensor_scalar(mv[:, u, 1:2], mv[:, u, 1:2], EPS, None, ALU.add).then_inc(s["varied"], 1)
                dve.wait_ge(s["rooted"], t + 1)
                link(nc.vector.reciprocal(sd[:, u, 1:2], sd[:, u, 0:1]))
                nc.vector.tensor_scalar(res[:, u, :], res[:, u, :], mv[:, u, 0:1], sd[:, u, 1:2],
                                        ALU.subtract, ALU.mult).then_inc(centred, 1)

            def first():
                before(0, 0, 0)
                assert link.n == PRE

            def body(t, u, i, r, more):
                link.turn(PRE + (PRE + POST) * t if more else PRE * N + POST * (N - 1))
                if more:
                    before(t + 1, 1 - u, i + u)
                after(t, u, i, r)
                assert link.n == POST + (PRE if more else 0)
            tiles(dve, first, body)



def later_stages(k, l, with_ctx, stages):
    on = lambda name: stages is None or name in stages
    if on("c"):
        with ExitStack() as st:
            mlstm(k, l, k.semaphores(st, "mlstm", (
                "cleared", "g_ld", "v_ld", "gate_steps", "gate_exps", "row_st", "staged", "turned", "kept",
                "d_ld", "weighed", "prod", "stepped", "m_ld", "cleared2", "cleared3", "logits", "gated", "scored", "mixed",
                "intra", "inter", "inter_free", "den_steps", "ready", "y_done"), {"k_ld": 2, "c_ld": 2, "y_st": 2}), with_ctx)
    if on("a"):
        with ExitStack() as st:
            window(k, l, k.semaphores(st, "window", (
                "c_ld", "cleared", "scored", "maxed", "chain", "weighed", "turned", "ev_a", "ev_d", "summed", "o_out",
                "back", "y_done"), {"ld": 2, "y_st": 2}), with_ctx)
    if on("b"):
        with ExitStack() as st:
            nlam = k.buffers(st)("nlam", [P, 1])
            s = k.semaphores(st, "diff", (
                "lam_ld", "lam_steps", "lam_exps", "s_ld", "cleared", "scored", "maxed",
                "chain", "weighed", "mixed", "turned", "ev_a", "ev_d", "half_summed", "summed", "o_out", "back", "y_done", "xy_st",
                "x_cleared", "x_scored", "x_chain", "x_weighed", "x_turned", "x_summed", "x_back"), {"v_ready": 2, "v_ld": 2, "y_st": 2, "xs_ld": 2})
            lambdas(k, l, s, nlam)
            differential(k, l, s, nlam)
            if with_ctx:
                differential_context(k, l, s, nlam)
    if on("o"):
        with ExitStack() as st:
            output(k, l, k.semaphores(st, "out", (
                "w_ld", "squared", "steps", "roots", "ready", "turned", "moved", "prod", "taken", "centred",
                "done", "scaled", "gn_ready", "summed", "varied", "rooted"), {"ld": 2, "x_ld": 2, "o_st": 2}), with_ctx)


def more_constants():
    keep = np.ones((64, TOK), np.float32)
    keep[0:32, 0::P] = 0.0
    keep[32:64, P - 1::P] = 0.0
    t = np.arange(P)
    causal = np.stack([np.where(t[:, None] <= t[None], 0.0, NEG), np.where(t[:, None] >= t[None], 0.0, NEG)], 1)
    q, j = np.arange(P)[:, None], np.arange(3 * WIN)[None]
    near = np.abs(j - WIN - q) <= WIN
    window = np.stack([near & (j >= WIN), near, near & (j < 2 * WIN)], 1)
    lam = np.array([[0.8 - 0.6 * np.exp(-0.3 * n)] for n in range(DEPTH)])
    return {"lam_init": lam.astype(np.float32), "lam_keep": (1.0 - lam).astype(np.float32),
            "window": np.where(window, 0.0, NEG).astype(np.float32), "keep": keep, "causal": causal.astype(np.float32)}


def setup(k):
    nc, io, d = k.nc, k.io, k.d
    with ExitStack() as st:
        sb = k.buffers(st)
        zero = sb("zero", [P, A_KV * HD])
        cols = sb("cond", [P, KT, 2])
        x_cp, c_ld, i_ld, z_st, silu, cleared = k.semaphores(
            st, "setup", ("x_copied", "cond_ld", "ident_ld", "pad_st", "silu", "cleared")).values()
        block = st.enter_context(nc.Block())

        @block.sync
        def _(sp):
            sp.dma_start(k.ident[:], io["ident"]).then_inc(i_ld, 16)
            for r in range(2):
                sp.dma_start(cols[:, :, r], io["cond"][r, :].rearrange("(k p) -> p k", p=P),
                             allow_slow_non_contiguous=True).then_inc(c_ld, 16)
            sp.dma_start(d["x"][0:SEQ, :], io["x"]).then_inc(x_cp, 16)
            sp.dma_start(d["x"][SEQ:TOK, :], io["ctx"]).then_inc(x_cp, 16)
            sp.wait_ge(cleared, 1)
            for row in (0, CTX0 - WIN):
                sp.dma_start(d["va"][row:row + WIN, :], zero[:]).then_inc(z_st, 16)
                sp.dma_start(d["ka"][:, row:row + WIN], zero[:]).then_inc(z_st, 16)
            sp.wait_ge(x_cp, 32)
            sp.wait_ge(z_st, 64)
            sp.wait_ge(i_ld, 16)

        @block.vector
        def _(dve):
            nc.vector.memset(zero[:], 0.0).then_inc(cleared, 1)

        @block.scalar
        def _(act):
            act.wait_ge(c_ld, 32)
            nc.scalar.activation(k.silu_c[:], cols[:], ACT.Silu).then_inc(silu, 1)
            act.wait_ge(silu, 1)


def layer(k, l, with_ctx, stages):
    d = k.d
    with ExitStack() as st:
        modulation(k, l, k.semaphores(st, "mod", ("b_ld", "done", "added", "stored", "cols_ld"), {"w_ld": 3}))
    with ExitStack() as wide:
        hT = k.buffers(wide)("hT", [P, KT, TOK])
        with ExitStack() as st:
            natural_project(k, l, hT, k.semaphores(
                st, "nat", ("turned", "h_ready", "kept", "prod", "evac", "v_free", "z_free", "n_ready"),
                {"w_ld": NCH, "x_ld": 2, "n_st": 2}))
        latent_row = lambda t0: LAT0 + t0 if t0 < SEQ else CTX0
        ta = lambda i, u, b, t0, w, ob: [(d["qa"][u, :, t0:t0 + w], ob[:, 0, :])]
        tk = lambda i, u, b, t0, w, ob: [(d["ka"][:, latent_row(t0):latent_row(t0) + w], ob[:, 0, :])] if u == 0 else \
            [(d["gates"][:, t0:t0 + w], ob[0:24, 0, :])]
        tb = lambda i, u, b, t0, w, ob: [
            (d["qkb"][u, part, bass.ds(i * P, P), t0:t0 + w], ob[:, part, :]) for part in range(3)]
        tc = lambda i, u, b, t0, w, ob: [(d["qkc"][u, bass.ds(i * P, P), t0:t0 + w], ob[:, 0, :])]
        for kinds, first, pairs, out_of in ((("rope_a", "rope_a"), 0, 1, ta), (("rope_a", 1.0), 2, 1, tk),
                                            (("rope_b", "rope_b"), 4, 3, tb), ((HD ** -0.5, 1.0), 10, 3, tc)):
            with ExitStack() as st:
                transposed_project(k, l, hT, k.semaphores(
                    st, "tr", ("tab_ld", "prod", "evac", "rot", "rot_free", "done", "chain"),
                    {"w_ld": 2, "o_st": 2}), kinds, first, pairs, out_of)
    later_stages(k, l, with_ctx, stages)


def program(nc, io, out, d, stages):
    with ExitStack() as stack:
        k = Core(nc, stack, io, d)
        k.out = out
        k.ps = stack.enter_context(nc.psum_tensor("ps", [P, 8, 512], F32))
        k.ident = stack.enter_context(nc.sbuf_tensor("ident_sb", [P, P], F32))
        k.silu_c = stack.enter_context(nc.sbuf_tensor("silu_c", [P, KT, 2], F32))
        k.modc = stack.enter_context(nc.sbuf_tensor("modc", [P, 2, 2, KT], F32))
        setup(k)
        if DEPTH > 1:
            with nc.Fori(0, DEPTH - 1) as l:
                layer(k, l, True, stages)
        if stages is None or "2" in stages:
            layer(k, DEPTH - 1, False, stages)


def constants():
    def tables(dim):
        nf = dim // 4
        inv = (np.float32(10000.0) ** (-np.arange(nf, dtype=np.float32) / nf)).astype(np.float32)
        tok = np.arange(SEQ)
        ar = (tok // GRID_W).astype(np.float32)[:, None] * inv
        ac = (tok % GRID_W).astype(np.float32)[:, None] * inv
        ang = np.concatenate([ar, ar, ac, ac], -1).T
        both = np.stack([np.cos(ang.astype(np.float64)), np.sin(ang.astype(np.float64))], 1).astype(np.float32)
        return np.tile(both, (P // dim, 1, 1))

    def rotation(dim):
        m = np.zeros((P, P), np.float32)
        q = dim // 4
        for j in range(P):
            if (j % dim) // q % 2 == 0:
                m[j + q, j] = -1.0
            else:
                m[j - q, j] = 1.0
        return m
    c = {"rope": np.stack([tables(HD), tables(B_QK)]), "perm": np.stack([rotation(HD), rotation(B_QK)]),
         "ident": np.eye(P, dtype=np.float32)}
    c.update(more_constants())
    return c


def lay_out(inputs):
    f = {n: np.asarray(a) for n, a in inputs.items()}
    w = f["w_in"]
    at = np.cumsum([0, 256, 128, 128, 256, 384, 384, 384, 384, 384, 384, 384, 384, 384, 24])
    qa, ka, va, za, qb, kb, vb, zb, qm, km, vm, om, zm, gm = (w[:, :, at[n]:at[n + 1]] for n in range(14))
    nat = np.concatenate([va, za, vb, zb, vm, om, zm], 2).reshape(DEPTH, KT, P, NCH, CW).transpose(0, 3, 2, 1, 4)
    gate = np.concatenate([gm, np.zeros((DEPTH, DM, P - gm.shape[2]), w.dtype)], 2)
    third = lambda a, n: a[:, :, n * P:(n + 1) * P]
    tiles = [third(qa, 0), third(qa, 1), ka, gate]
    for q, kk in ((qb, kb), (qm, km)):
        for n in range(3):
            tiles += [third(q, n), third(kk, n)]
    tr = np.stack(tiles, 1).reshape(DEPTH, TILES, KT, P, P).transpose(0, 1, 3, 2, 4)
    a = {"x": f["x"][0], "ctx": f["ctx"][0], "cond": np.concatenate([f["c"], f["c_ctx"][None]], 0),
         "w_mod": f["w_mod"], "b_mod": f["b_mod"], "w_nat": nat, "w_tr": tr}
    a["w_out"] = f["w_out"].reshape(DEPTH, KT, P, DM).transpose(0, 2, 1, 3)
    for n in ("attn_sink", "diff_lambda", "diff_norm_g", "mlstm_norm_g", "ln_g", "ln_b"):
        a[n] = f[n]
    a["i_bias"], a["f_bias"] = f["mlstm_i_bias"], f["mlstm_f_bias"]
    a.update(constants())
    return {n: np.ascontiguousarray(v) for n, v in a.items()}


SCRATCH = {"x": ([TOK, DM], F32), "mod": ([2, 3 * DM], F32), "nat": ([TOK, NW], F32), "va": ([PADTOK, P], F32),
           "qa": ([2, P, TOK], F32), "ka": ([P, PADTOK], F32), "gates": ([24, TOK], F32),
           "qkb": ([2, 3, 3 * P, TOK], BF16), "qkc": ([2, 3 * P, TOK], F32),
           "u": ([12, TOK], F32), "decay": ([12, NT], F32), "y": ([TOK, DM], F32)}


def kernel(**inputs):
    import concourse.bacc as bacc
    from concourse.bass_utils import run_bass_kernel_spmd

    nc = bacc.Bacc("TRN2", target_bir_lowering=False, num_devices=1)
    arrays = lay_out(inputs)
    io = {n: nc.dram_tensor(f"in_{n}", a.shape, mybir.dt.from_np(a.dtype), kind="ExternalInput").ap() for n, a in arrays.items()}
    out = nc.dram_tensor("out_0", (SEQ, DM), F32, kind="ExternalOutput").ap()
    scratch = {n: nc.dram_tensor(f"work_{n}", s, t, kind="Internal").ap() for n, (s, t) in SCRATCH.items()}
    program(nc, io, out, scratch, None)
    result = run_bass_kernel_spmd(nc, [{f"in_{n}": a for n, a in arrays.items()}], core_ids=[0])
    return result.results[0]["out_0"].reshape(1, SEQ, DM)
```

```python
from contextlib import ExitStack

import numpy as np

import concourse.bass as bass
from concourse import mybir

F32 = mybir.dt.float32
BF16 = mybir.dt.bfloat16
ALU = mybir.AluOpType
ACT = mybir.ActivationFunctionType
AX = mybir.AxisListType

P = 128
DM = 1024
KT = DM // P
DEPTH = 2
SEQ, CTX = 2048, 256
TOK = SEQ + CTX
NT = TOK // P
NTL = SEQ // P
HD = 64
A_HEADS, A_KV = 4, 2
B_HEADS, B_QK = 6, 32
C_HEADS = 6
GRID_W = 64
EPS = 1e-5
ALPHA = (2 * DEPTH) ** 0.25
WIN = 128
NEG = -1.0e30
CW, NCH = 384, 6
VALUE_CHUNKS = (0, 1, 3)
VA, SA, VB, SB, VM, SC, NW = 0, 128, 384, 768, 1152, 1536, 1920
TILES = 16
PADTOK = TOK + 2 * WIN
LAT0, CTX0 = WIN, SEQ + 2 * WIN
TB = [(512 * b, 512) for b in range(4)] + [(SEQ, CTX)]


class Chain:

    def __init__(self, eng, sem):
        self.eng, self.sem, self.base, self.n = eng, sem, 0, 0

    def turn(self, base):
        self.base, self.n = base, 0

    def __call__(self, instruction):
        self.n += 1
        instruction.then_inc(self.sem, 1)
        self.eng.wait_ge(self.sem, self.base + self.n)


class Core:

    def __init__(self, nc, stack, io, d):
        self.nc, self.stack, self.io, self.d = nc, stack, io, d
        self.stage = 0

    def semaphores(self, stack, prefix, single, several=()):
        self.stage += 1
        made = {n: stack.enter_context(self.nc.semaphore(f"{prefix}_{n}_{self.stage}")) for n in single}
        made.update({n: [stack.enter_context(self.nc.semaphore(f"{prefix}_{n}{u}_{self.stage}")) for u in range(count)]
                     for n, count in dict(several).items()})
        for s in made.values():
            for one in s if isinstance(s, list) else [s]:
                self.nc.sync.sem_clear(one)
        self.nc.all_engine_barrier()
        return made

    def buffers(self, stack):
        self.stage += 1
        stage = self.stage
        return lambda name, shape, dtype=F32: stack.enter_context(self.nc.sbuf_tensor(f"{name}_{stage}", shape, dtype))


def modulation(k, l, names):
    nc, io, d, ps = k.nc, k.io, k.d, k.ps
    with ExitStack() as st:
        sb = k.buffers(st)
        NC2, W = 6, 512
        wm = sb("mod_w", [P, 3, KT, W])
        brow = sb("mod_bias", [2, 3 * DM])
        mod = sb("mod_rows", [2, 3 * DM])
        w_ld, b_ld, done, added, stored, cols_ld = names["w_ld"], names["b_ld"], names["done"], names["added"], names["stored"], names["cols_ld"]
        block = st.enter_context(nc.Block())
        wv = io["w_mod"].rearrange("l (k p) n -> l p k n", p=P)
        modv = d["mod"].rearrange("r (j k p) -> p j r k", j=3, p=P)

        @block.sync
        def _(sp):
            sp.dma_start(brow[:], io["b_mod"][l, :].partition_broadcast(2)).then_inc(b_ld, 16)
            for c in range(NC2):
                if c >= 3:
                    sp.wait_ge(done, c - 2)
                sp.dma_start(wm[:, c % 3, :, :], wv[l, :, :, c * W:(c + 1) * W]).then_inc(w_ld[c % 3], 16)
            sp.wait_ge(added, NC2)
            sp.dma_start(d["mod"], mod[:]).then_inc(stored, 16)
            sp.wait_ge(stored, 16)
            for j in range(2):
                for r in range(2):
                    sp.dma_start(k.modc[:, j, r, :], modv[:, j, r, :], allow_slow_non_contiguous=True).then_inc(cols_ld, 16)
            sp.wait_ge(cols_ld, 64)

        @block.tensor
        def _(pe):
            for c in range(NC2):
                pe.wait_ge(w_ld[c % 3], 16 * (c // 3 + 1))
                for j in range(KT):
                    mm = nc.tensor.matmul(ps[0:2, c, 0:W], k.silu_c[:, j, :], wm[:, c % 3, j, :],
                                          start=(j == 0), stop=(j == KT - 1))
                mm.then_inc(done, 1)

        @block.vector
        def _(dve):
            dve.wait_ge(b_ld, 16)
            for c in range(NC2):
                dve.wait_ge(done, c + 1)
                nc.vector.tensor_tensor(mod[:, c * W:(c + 1) * W], ps[0:2, c, 0:W],
                                        brow[:, c * W:(c + 1) * W], ALU.add).then_inc(added, 1)
            dve.wait_ge(cols_ld, 64)
            nc.vector.tensor_scalar(k.modc[:, 1, :, :], k.modc[:, 1, :, :], 1.0, None, ALU.add).then_inc(added, 1)
            dve.wait_ge(added, NC2 + 1)


def natural_project(k, l, hT, s, with_ctx):
    nc, io, d, ps = k.nc, k.io, k.d, k.ps
    with ExitStack() as st:
        sb = k.buffers(st)
        wn = sb("wn", [P, NCH, KT, CW])
        xt = sb("xt", [P, 2, DM])
        hs = sb("hs", [P, 2, KT, P])
        nt = sb("nt", [P, 2, NW])
        sz = sb("sz", [P, 2, CW])
        block = st.enter_context(nc.Block())
        w_ld, x_ld, n_st = s["w_ld"], s["x_ld"], s["n_st"]
        turned, h_ready, kept = s["turned"], s["h_ready"], s["kept"]
        prod, evac, v_free, z_free, n_ready = s["prod"], s["evac"], s["v_free"], s["z_free"], s["n_ready"]
        PAIRS = NT // 2
        HEAD = 2 * NCH

        @block.sync
        def _(sp):
            sp.wait_ge(k.copied["x_copied"], 32)
            sp.wait_ge(k.copied["pad_st"], 64)
            for u in range(2):
                sp.sem_inc(n_st[u], 16)
                sp.dma_start(xt[:, u, :], d["x"][u * P:(u + 1) * P, :]).then_inc(x_ld[u], 16)
            for c in range(NCH):
                sp.dma_start(wn[:, c, :, :], io["w_nat"][l, c, :, :, :]).then_inc(w_ld[c], 16)

            def store(i, u, values=False):
                if values:
                    sp.wait_ge(s["values_ready"], u + 1)
                else:
                    sp.wait_ge(n_ready, 2 * i + (u + 1))
                sp.dma_start(d["nat"][bass.ds(i * (2 * P) + u * P, P), :], nt[:, u, :]).then_inc(n_st[u], 16)

            def store_va(i, u, row):
                sp.dma_start(d["va"][bass.ds(row, P), :], nt[:, u, 0:P]).then_inc(n_st[u], 16)

            with sp.Fori(0, PAIRS - 1) as i:
                for u in range(2):
                    sp.wait_ge(turned, 2 * i + (u + 1))
                    sp.dma_start(xt[:, u, :], d["x"][bass.ds(i * (2 * P) + (u + 2) * P, P), :]).then_inc(x_ld[u], 16)
                    store(i, u)
                    store_va(i, u, i * (2 * P) + u * P + LAT0)
            for u in range(2):
                store(PAIRS - 1, u, not with_ctx)
                store_va(PAIRS - 1, u, CTX0 + u * P)
            for u in range(2):
                sp.wait_ge(n_st[u], 16 + 32 * PAIRS)

        @block.tensor
        def _(pe):
            pe.sem_inc(prod, HEAD)

            def turn(i, u, t):
                for j in range(KT):
                    tr = nc.tensor.transpose(ps[:, j // 4, (j % 4) * P:(j % 4 + 1) * P],
                                             xt[:, u, j * P:(j + 1) * P], k.ident[:])
                tr.then_inc(turned, 1)

            def product(i, u, values=False):
                pe.wait_ge(h_ready, 2 * i + (u + 1))
                for c in VALUE_CHUNKS if values else range(NCH):
                    free = v_free if c in (1, 3, 4) or values and u == 1 else z_free
                    n = {1: 0, 3: 1, 4: 2, 0: 0, 2: 1, 5: 2}[c]
                    if values and u == 1:
                        n = VALUE_CHUNKS.index(c)
                    pe.wait_ge(free, 6 * i + (3 * u + n + 1))
                    pe.wait_ge(w_ld[c], 16)
                    for j in range(KT):
                        mm = nc.tensor.matmul(ps[:, 2 + c, 0:CW], hs[:, u, j, :], wn[:, c, j, :],
                                              start=(j == 0), stop=(j == KT - 1))
                    mm.then_inc(prod, 1)

            pe.wait_ge(x_ld[0], 16)
            turn(0, 0, 0)
            with pe.Fori(0, PAIRS - 1) as i:
                pe.wait_ge(x_ld[1], 16 * i + 16)
                pe.wait_ge(h_ready, 2 * i + 1)
                turn(i, 1, None)
                product(i, 0)
                pe.wait_ge(x_ld[0], 16 * i + 32)
                pe.wait_ge(h_ready, 2 * i + 2)
                turn(i, 0, None)
                product(i, 1)
            i = PAIRS - 1
            pe.wait_ge(x_ld[1], 16 * i + 16)
            pe.wait_ge(h_ready, 2 * i + 1)
            turn(i, 1, None)
            product(i, 0, not with_ctx)
            product(i, 1, not with_ctx)

        @block.vector
        def _(dve):
            dve.sem_inc(z_free, 3)

            def modulate(t, u, r):
                dve.wait_ge(turned, t + 1)
                dve.wait_ge(prod, 6 * t + 6)
                dve.wait_ge(kept, t + 1)
                for j in range(KT):
                    op = nc.vector.tensor_scalar(hs[:, u, j, :], ps[:, j // 4, (j % 4) * P:(j % 4 + 1) * P],
                                                 k.modc[:, 1, r, j:j + 1], k.modc[:, 0, r, j:j + 1],
                                                 ALU.mult, ALU.add)
                op.then_inc(h_ready, 1)

            def gates(i, u):
                base = 6 * i + 3 * u
                zb = 6 * i + (3 * u + 3)
                dve.wait_ge(evac, base + 1)
                nc.vector.tensor_tensor(nt[:, u, SA:VB], nt[:, u, SA:VB], ps[:, 2, P:CW], ALU.mult).then_inc(z_free, 1)
                dve.wait_ge(evac, base + 2)
                nc.vector.tensor_tensor(nt[:, u, SB:VM], nt[:, u, SB:VM], ps[:, 4, 0:CW], ALU.mult).then_inc(z_free, 1)
                dve.wait_ge(evac, base + 3)
                nc.vector.tensor_tensor(sz[:, u, :], sz[:, u, :], ps[:, 7, 0:CW], ALU.mult).then_inc(z_free, 1)
                dve.wait_ge(z_free, zb + 3)
                nc.vector.tensor_tensor(nt[:, u, SC:NW], nt[:, u, SC:NW], sz[:, u, :], ALU.mult).then_inc(n_ready, 1)

            modulate(0, 0, 0)
            with dve.Fori(0, PAIRS - 2) as i:
                modulate(2 * i + 1, 1, 0)
                gates(i, 0)
                modulate(2 * i + 2, 0, 0)
                gates(i, 1)
            i = PAIRS - 2
            modulate(2 * i + 1, 1, 0)
            gates(i, 0)
            modulate(2 * i + 2, 0, 1)
            gates(i, 1)
            i = PAIRS - 1
            modulate(2 * i + 1, 1, 1)
            if with_ctx:
                gates(i, 0)
                gates(i, 1)

        @block.scalar
        def _(act):
            act.sem_inc(v_free, 3)

            def body(i, u):
                base = 12 * i + (6 * u + HEAD)
                act.wait_ge(n_st[u], 32 * i + 16)

                def chunk(c):
                    act.wait_ge(prod, base + (c + 1))
                chunk(0)
                nc.scalar.copy(nt[:, u, VA:SA], ps[:, 2, 0:P])
                nc.scalar.activation(nt[:, u, SA:VB], ps[:, 2, P:CW], ACT.Sigmoid).then_inc(evac, 1)
                chunk(1)
                nc.scalar.copy(nt[:, u, VB:SB], ps[:, 3, 0:CW]).then_inc(v_free, 1)
                chunk(2)
                nc.scalar.activation(nt[:, u, SB:VM], ps[:, 4, 0:CW], ACT.Sigmoid).then_inc(evac, 1)
                chunk(3)
                nc.scalar.copy(nt[:, u, VM:SC], ps[:, 5, 0:CW]).then_inc(v_free, 1)
                chunk(4)
                nc.scalar.activation(nt[:, u, SC:NW], ps[:, 6, 0:CW], ACT.Sigmoid).then_inc(v_free, 1)
                chunk(5)
                nc.scalar.activation(sz[:, u, :], ps[:, 7, 0:CW], ACT.Sigmoid).then_inc(evac, 1)

            def values(i, u):
                for n, (c, lo, w) in enumerate(((0, VA, P), (1, VB, CW), (3, VM, CW))):
                    act.wait_ge(prod, 12 * i + (3 * u + HEAD + n + 1))
                    nc.scalar.copy(nt[:, u, lo:lo + w], ps[:, 2 + c, 0:w]).then_inc(v_free, 1)
                act.wait_ge(v_free, 6 * i + (3 * u + 6))
                act.sem_inc(s["values_ready"], 1)

            with act.Fori(0, PAIRS if with_ctx else PAIRS - 1) as i:
                for u in range(2):
                    body(i, u)
            if not with_ctx:
                for u in range(2):
                    act.wait_ge(n_st[u], 32 * (PAIRS - 1) + 16)
                    values(PAIRS - 1, u)

        @block.gpsimd
        def _(pool):
            pool.sem_inc(kept, 2)
            with pool.Fori(0, PAIRS) as i:
                for u in range(2):
                    pool.wait_ge(h_ready, 2 * i + (u + 1))
                    nc.gpsimd.tensor_copy(hT[:, :, bass.ds(i * (2 * P) + u * P, P)], hs[:, u, :, :]).then_inc(kept, 1)


def transposed_project(k, l, hT, s, kinds, first, pairs, out):
    nc, io, d, ps = k.nc, k.io, k.d, k.ps
    rope = [isinstance(kind, str) for kind in kinds]
    split = kinds[0] == "rope_b"
    parts = 3 if split else 1
    NB = len(TB)
    R = sum(rope) * 4
    with ExitStack() as st:
        sb = k.buffers(st)
        wt = sb("wt", [P, 2, KT, P])
        qs = sb("qs", [P, 2, 512])
        tab = sb("tab", [P, 2, SEQ])
        perm = sb("perm", [P, P])
        t1 = sb("t1", [P, 2, 512])
        t2 = sb("t2", [P, 2, 512])
        ob = sb("ob", [P, 2, 3, 512], BF16) if split else sb("ob", [P, 2, 1, 512])
        block = st.enter_context(nc.Block())
        w_ld, tab_ld, o_st, prod, evac, rot, rot_free, done, chain = (
            s["w_ld"], s["tab_ld"], s["o_st"], s["prod"], s["evac"], s["rot"], s["rot_free"], s["done"], s["chain"])
        which = 1 if split else 0
        blocks = [(u, b) for u in range(2) for b in range(NB)]

        @block.sync
        def _(sp):
            for u in range(2):
                sp.sem_inc(o_st[u], 16 * parts)
                sp.dma_start(wt[:, u, :, :], io["w_tr"][l, first + u, :, :, :]).then_inc(w_ld[u], 16)
            if R:
                sp.dma_start(tab[:], io["rope"][which, :, :, :]).then_inc(tab_ld, 16)
                sp.dma_start(perm[:], io["perm"][which, :, :]).then_inc(tab_ld, 16)

            def store(i, n, u, b):
                sp.wait_ge(done, 2 * NB * i + (n + 3))
                t0, w = TB[b]
                for dst, src in out(i, u, b, t0, w, ob[:, n % 2, :, 0:w]):
                    sp.dma_start(dst, src).then_inc(o_st[n % 2], 16)

            def turn(i, more):
                for n, (u, b) in enumerate(blocks):
                    store(i, n, u, b)
                    if b == NB - 1 and more:
                        sp.wait_ge(prod, 2 * NB * i + NB * (u + 1))
                        sp.dma_start(wt[:, u, :, :], io["w_tr"][l, bass.ds(2 * i + (first + 2 + u), 1), :, :, :]
                                     .rearrange("o p k n -> p (o k) n")).then_inc(w_ld[u], 16)

            if pairs > 1:
                with sp.Fori(0, pairs - 1) as i:
                    turn(i, True)
            turn(pairs - 1, False)
            for u in range(2):
                sp.wait_ge(o_st[u], 16 * parts * (1 + NB * pairs))

        def loop(eng, body):
            if pairs > 1:
                with eng.Fori(0, pairs) as i:
                    body(i)
            else:
                body(0)

        @block.tensor
        def _(pe):
            def body(i):
                r = 0
                for n, (u, b) in enumerate(blocks):
                    if b == 0:
                        pe.wait_ge(w_ld[u], 16 * i + 16)
                    t0, w = TB[b]
                    pe.wait_ge(evac, 2 * NB * i + (n + 1))
                    for j in range(KT):
                        mm = nc.tensor.matmul(ps[:, b, 0:w], wt[:, u, j, :], hT[:, j, t0:t0 + w],
                                              start=(j == 0), stop=(j == KT - 1))
                    mm.then_inc(prod, 1)
                    if rope[u] and b >= 1:
                        pe.wait_ge(evac, 2 * NB * i + (n + NB))
                        pe.wait_ge(rot_free, R * i + (r + 1))
                        if r == 0:
                            pe.wait_ge(tab_ld, 32)
                        nc.tensor.matmul(ps[:, 5 + r % 2, 0:512], perm[:], qs[:, (n - 1) % 2, 0:512],
                                         start=True, stop=True).then_inc(rot, 1)
                        r += 1
            loop(pe, body)

        @block.scalar
        def _(act):
            act.sem_inc(evac, NB)

            def body(i):
                for n, (u, b) in enumerate(blocks):
                    w = TB[b][1]
                    act.wait_ge(prod, 2 * NB * i + (n + 1))
                    act.wait_ge(done, 2 * NB * i + (n + 1))
                    if split and u == 0:
                        nc.scalar.activation(qs[:, n % 2, 0:w], ps[:, b, 0:w], ACT.Copy, scale=B_QK ** -0.5).then_inc(evac, 1)
                    else:
                        nc.scalar.copy(qs[:, n % 2, 0:w], ps[:, b, 0:w]).then_inc(evac, 1)
            loop(act, body)

        @block.vector
        def _(dve):
            link = Chain(dve, chain)
            steps = 3 * 2 * NB + R
            dve.sem_inc(rot_free, 2)
            dve.sem_inc(done, 2)
            if R:
                dve.wait_ge(tab_ld, 32)

            def body(i):
                link.turn(steps * i)
                r = 0
                for n, (u, b) in enumerate(blocks):
                    t0, w = TB[b]
                    v = n % 2
                    src = qs[:, v, 0:w]
                    dve.wait_ge(evac, 2 * NB * i + (n + 1 + NB))
                    dve.wait_ge(o_st[v], 16 * parts * NB * i + 16 * parts * (n // 2 + 1))
                    if rope[u] and b < 4:
                        nc.vector.tensor_tensor(t1[:, v, 0:w], src, tab[:, 0, t0:t0 + w], ALU.mult)
                        dve.wait_ge(rot, R * i + (r + 1))
                        nc.vector.tensor_tensor(t2[:, v, 0:w], ps[:, 5 + r % 2, 0:w], tab[:, 1, t0:t0 + w],
                                                ALU.mult).then_inc(rot_free, 1)
                        r += 1
                        dve.wait_ge(rot_free, R * i + (r + 2))
                        if split:
                            link(nc.vector.tensor_tensor(t1[:, v, 0:w], t1[:, v, 0:w], t2[:, v, 0:w], ALU.add))
                            src = t1[:, v, 0:w]
                        else:
                            last = nc.vector.tensor_tensor(ob[:, v, 0, 0:w], t1[:, v, 0:w], t2[:, v, 0:w], ALU.add)
                    elif not split:
                        factor = 1.0 if rope[u] else kinds[u]
                        last = nc.vector.tensor_scalar(ob[:, v, 0, 0:w], src, factor, None, ALU.mult)
                    if split:
                        link(nc.vector.tensor_copy(ob[:, v, 0, 0:w], src))
                        link(nc.vector.tensor_tensor(t2[:, v, 0:w], src, ob[:, v, 0, 0:w], ALU.subtract))
                        link(nc.vector.tensor_copy(ob[:, v, 1, 0:w], t2[:, v, 0:w]))
                        last = nc.vector.tensor_tensor(ob[:, v, 2, 0:w], t2[:, v, 0:w], ob[:, v, 1, 0:w], ALU.subtract)
                    last.then_inc(done, 1)
                assert not split or link.n == steps
            loop(dve, body)


UNITS = 2 * C_HEADS
PAIRS_C = C_HEADS // 2
SV = HD + 1
PV = 2 * SV
KEY, INTER, UPDATE, FLOOR = range(4)
DIRS = ((0, 32), (32, 64))


def mlstm_gates(k, l, s, cols, knat, v1):
    nc, io, d, ps = k.nc, k.io, k.d, k.ps
    with ExitStack() as st:
        sb = k.buffers(st)
        gi, gf, keep, tmp, logf, b, m = (sb(n, [64, TOK]) for n in ("gi", "gf", "keep", "tmp", "logf", "b", "m"))
        stat = sb("stat", [64, 4, TOK])
        turn = sb("turn", [P, 2, 4, P])
        ib, fb = sb("ib", [64, 1]), sb("fb", [64, 1])
        mprev, delta, decay = (sb(n, [64, NT]) for n in ("mprev", "delta", "decay"))
        kc = sb("kc", [P, 2, PAIRS_C, P])
        block = st.enter_context(nc.Block())
        cleared, g_ld, v_ld, k_ld, dve_s, act_s, row_st = (
            s[n] for n in ("cleared", "g_ld", "v_ld", "k_ld", "gate_steps", "gate_exps", "row_st"))
        staged, turned, kept, k_turned, k_kept = s["staged"], s["turned"], s["kept"], s["k_turned"], s["k_kept"]

        @block.sync
        def _(sp):
            sp.wait_ge(dve_s, 1)
            sp.dma_start(gf[:], d["gates"][64:P, :]).then_inc(g_ld, 16)
            for u in range(2):
                sp.dma_start(kc[:, u, :, :], d["qkc"][1, :, u * P:(u + 1) * P].rearrange("(c p) t -> p c t", p=P)
                             ).then_inc(k_ld[u], 16)
            sp.dma_start(gi[:], d["gates"][0:64, :]).then_inc(g_ld, 16)
            sp.dma_start(keep[:], io["keep"]).then_inc(g_ld, 16)
            for way, (lo, _) in enumerate(DIRS):
                sp.dma_start(ib[lo:lo + 6, :], io["i_bias"][l, way, :].unsqueeze(1)).then_inc(g_ld, 16)
                sp.dma_start(fb[lo:lo + 6, :], io["f_bias"][l, way, :].unsqueeze(1)).then_inc(g_ld, 16)
            sp.wait_ge(cleared, 1)
            for h in range(C_HEADS):
                sp.dma_start(v1[:, :, h, 0:HD], d["nat"][:, VM + h * HD:VM + (h + 1) * HD].rearrange("(c p) v -> p c v", p=P)
                             ).then_inc(v_ld, 16)
            with sp.Fori(0, NT // 2 - 1) as i:
                for u in range(2):
                    sp.wait_ge(k_turned, 2 * i + (u + 1))
                    sp.dma_start(kc[:, u, :, :], d["qkc"][1, :, bass.ds(i * (2 * P) + (2 + u) * P, P)].rearrange("(c p) t -> p c t", p=P)
                                 ).then_inc(k_ld[u], 16)
            sp.wait_ge(act_s, 6)
            for way, (lo, _) in enumerate(DIRS):
                sp.dma_start(d["u"][6 * way:6 * way + 6, :], tmp[lo:lo + 6, :]).then_inc(row_st, 16)
                sp.dma_start(d["decay"][6 * way:6 * way + 6, :], decay[lo:lo + 6, :]).then_inc(row_st, 16)
            sp.wait_ge(row_st, 64)
            sp.wait_ge(v_ld, 16 * C_HEADS)

        @block.gpsimd
        def _(pool):
            nc.gpsimd.memset(v1[:], 1.0).then_inc(cleared, 1)
            pool.wait_ge(cleared, 1)
        @block.vector
        def _(dve):
            link = Chain(dve, dve_s)
            for t in (ib[:], fb[:], turn[64:P, :, :, :]):
                last = nc.vector.memset(t, 0.0)
            link(last)
            dve.wait_ge(g_ld, 16 * 7)
            link(nc.vector.tensor_scalar(gf[:], gf[:], fb[:], None, ALU.add))
            link(nc.vector.scalar_tensor_tensor(out=tmp[:], in0=gf[:], scalar=-1.0, in1=gf[:],
                                                op0=ALU.mult, op1=ALU.max))
            link(nc.vector.tensor_scalar(gi[:], gi[:], ib[:], None, ALU.add))
            dve.wait_ge(act_s, 2)
            link(nc.vector.scalar_tensor_tensor(out=logf[:], in0=gf[:], scalar=0.0, in1=tmp[:],
                                                op0=ALU.min, op1=ALU.subtract))
            scan = nc.vector.tensor_tensor_scan
            scan(out=b[0:32, :], data0=keep[0:32, :], data1=logf[0:32, :], initial=0.0, op0=ALU.mult, op1=ALU.add)
            scan(out=b[32:64, ::-1], data0=keep[32:64, ::-1], data1=logf[32:64, ::-1], initial=0.0, op0=ALU.mult, op1=ALU.add)
            scan(out=m[32:64, ::-1], data0=logf[32:64, ::-1], data1=gi[32:64, ::-1], initial=0.0, op0=ALU.add, op1=ALU.max)
            link(scan(out=m[0:32, SEQ:TOK], data0=logf[0:32, SEQ:TOK], data1=gi[0:32, SEQ:TOK], initial=0.0,
                      op0=ALU.add, op1=ALU.max))
            link(scan(out=m[0:32, 0:SEQ], data0=logf[0:32, 0:SEQ], data1=gi[0:32, 0:SEQ],
                      initial=m[0:32, TOK - 1:TOK], op0=ALU.add, op1=ALU.max))
            chunks = lambda t: t.rearrange("r (c t) -> r c t", t=P)
            mc, bc = chunks(m[:]), chunks(b[:])
            nc.vector.tensor_tensor(tmp[:], b[:], m[:], ALU.subtract)
            nc.vector.tensor_tensor(stat[:, KEY, :], gi[:], b[:], ALU.subtract)
            nc.vector.memset(mprev[:], 0.0)
            nc.vector.tensor_tensor(delta[0:32, :], bc[0:32, :, P - 1], mc[0:32, :, P - 1], ALU.subtract)
            link(nc.vector.tensor_tensor(delta[32:64, :], bc[32:64, :, 0], mc[32:64, :, 0], ALU.subtract))
            nc.vector.tensor_copy(mprev[0:32, 1:NTL], mc[0:32, 0:NTL - 1, P - 1])
            nc.vector.tensor_copy(mprev[0:32, 0:1], mc[0:32, NT - 1, P - 1:P])
            nc.vector.tensor_copy(mprev[0:32, NTL + 1:NT], mc[0:32, NTL:NT - 1, P - 1])
            link(nc.vector.tensor_copy(mprev[32:64, 0:NT - 1], mc[32:64, 1:NT, 0]))
            wide = lambda t: t[:].unsqueeze(2).to_broadcast([64, NT, P])
            nc.vector.tensor_tensor(chunks(stat[:, INTER, :]), chunks(tmp[:]), wide(mprev), ALU.add)
            nc.vector.tensor_tensor(chunks(stat[:, UPDATE, :]), chunks(stat[:, KEY, :]), wide(delta), ALU.add)
            link(nc.vector.tensor_tensor(decay[:], delta[:], mprev[:], ALU.add))
            dve.wait_ge(act_s, 6)
            with dve.Fori(0, NT // 2) as i:
                for u in range(2):
                    dve.wait_ge(turned, 2 * i + (u + 1))
                    nc.vector.tensor_copy(turn[0:64, u, :, :], stat[:, :, bass.ds(i * (2 * P) + u * P, P)]).then_inc(staged, 1)

        @block.scalar
        def _(act):
            link = Chain(act, act_s)
            act.sem_inc(k_kept, 2)

            def keys():
                with act.Fori(0, NT // 2) as i:
                    for u in range(2):
                        act.wait_ge(k_turned, 2 * i + (u + 1))
                        nc.scalar.copy(knat[:, bass.ds(2 * i + u, 1), :].rearrange("p o c -> p (o c)"),
                                       ps[:, 2 + u, 0:PAIRS_C * P]).then_inc(k_kept, 1)
            act.wait_ge(dve_s, 3)
            link(nc.scalar.activation(tmp[:], tmp[:], ACT.Exp, scale=-1.0))
            link(nc.scalar.activation(tmp[:], tmp[:], ACT.Ln, bias=1.0))
            keys()
            act.wait_ge(dve_s, 10)
            link(nc.scalar.activation(stat[:, INTER, :], stat[:, INTER, :], ACT.Exp))
            link(nc.scalar.activation(stat[:, UPDATE, :], stat[:, UPDATE, :], ACT.Exp))
            link(nc.scalar.activation(stat[:, FLOOR, :], m[:], ACT.Exp, scale=-1.0))
            link(nc.scalar.activation(decay[:], decay[:], ACT.Exp))
            act.sem_inc(kept, 2)
            with act.Fori(0, NT // 2) as i:
                for u in range(2):
                    act.wait_ge(turned, 2 * i + (u + 3))
                    nc.scalar.copy(cols[:, bass.ds(2 * i + u, 1), :, :].rearrange("p o f (w h) -> p (o f) w h", w=2),
                                   ps[:, u, :].rearrange("p (f w h) -> p f w h", f=4, w=4)[:, :, 0:2, 0:C_HEADS]
                                   ).then_inc(kept, 1)

        @block.tensor
        def _(pe):
            pe.sem_inc(turned, 2)
            with pe.Fori(0, NT // 2) as i:
                for u in range(2):
                    pe.wait_ge(k_ld[u], 16 * i + 16)
                    pe.wait_ge(k_kept, 2 * i + (u + 1))
                    for p in range(PAIRS_C):
                        tr = nc.tensor.transpose(ps[:, 2 + u, p * P:(p + 1) * P], kc[:, u, p, :], k.ident[:])
                    tr.then_inc(k_turned, 1)
            with pe.Fori(0, NT // 2) as i:
                for u in range(2):
                    pe.wait_ge(kept, 2 * i + (u + 1))
                    pe.wait_ge(staged, 2 * i + (u + 1))
                    for f in range(4):
                        tr = nc.tensor.transpose(ps[:, u, f * P:(f + 1) * P], turn[:, u, f, :], k.ident[:])
                    tr.then_inc(turned, 1)


def mlstm_states(k, l, s, cols, knat, v1, states):
    nc, io, d, ps = k.nc, k.io, k.d, k.ps
    with ExitStack() as st:
        sb = k.buffers(st)
        kw = sb("kw", [P, 2, 2, C_HEADS, HD])
        dec = sb("dec", [P, 2, PAIRS_C, NT])
        block = st.enter_context(nc.Block())
        d_ld, weighed, prod, stepped = s["d_ld"], s["weighed"], s["prod"], s["stepped"]
        head = [(NT - 2, NT - 1, NT - 1, NT - 2), (NT - 1, NT - 2, 0, NTL - 1)]

        def steps(eng, body):
            for n, c in enumerate(head):
                body(n, n % 2, *c)
            with eng.Fori(0, (NTL - 2) // 2) as i:
                for u in range(2):
                    body(2 * i + (2 + u), u, 2 * i + u, (NTL - 1 - u) - 2 * i, 2 * i + (u + 1), (NTL - 2 - u) - 2 * i)
            body(NTL, 0, NTL - 2, 1, NTL - 1, 0)

        @block.sync
        def _(sp):
            by_half = d["decay"].rearrange("(w p h) c -> h w p c", w=2, h=2)
            for h in range(2):
                sp.dma_start(dec[64 * h:64 * h + 64, :, :, :], by_half[h, :, :, :].partition_broadcast(64)).then_inc(d_ld, 16)
            sp.wait_ge(d_ld, 32)

        @block.gpsimd
        def _(pool):
            nc.gpsimd.memset(states[:, NT // 2:NTL, :, :, :], 0.0).then_inc(s["cleared3"], 1)

            def body(n, u, f, b, fn, bn):
                pool.wait_ge(prod, n + 1)
                for way, c in ((0, f), (1, b)):
                    op = nc.gpsimd.tensor_tensor(
                        kw[:, u, way, :, :], knat[:, bass.ds(c, 1), :].rearrange("p o (h e) -> p (o h) e", e=HD),
                        cols[:, bass.ds(c, 1), UPDATE, way * C_HEADS:(way + 1) * C_HEADS].rearrange("p o h -> p (o h)")
                        .unsqueeze(2).to_broadcast([P, C_HEADS, HD]), ALU.mult)
                op.then_inc(weighed, 1)
            steps(pool, body)

        @block.tensor
        def _(pe):
            pe.sem_inc(prod, 2)

            def body(n, u, f, b, fn, bn):
                pe.wait_ge(weighed, n + 1)
                pe.wait_ge(stepped, n + 1)
                for way, c in ((0, f), (1, b)):
                    for p in range(PAIRS_C):
                        mm = nc.tensor.matmul(ps[:, 2 * u + way, p * PV:(p + 1) * PV],
                                              kw[:, u, way, 2 * p:2 * p + 2, :].rearrange("p h e -> p (h e)"),
                                              v1[:, bass.ds(c, 1), 2 * p:2 * p + 2, :].rearrange("p o h e -> p (o h e)"),
                                              start=True, stop=True)
                mm.then_inc(prod, 1)
            steps(pe, body)

        @block.vector
        def _(dve):
            dve.sem_inc(stepped, 1)
            nc.vector.memset(states[:, 0:NT // 2, :, :, :], 0.0)
            nc.vector.memset(states[:, NTL:, :, :, :], 0.0).then_inc(stepped, 1)
            dve.wait_ge(d_ld, 32)
            dve.wait_ge(s["cleared3"], 1)

            def body(n, u, f, b, fn, bn):
                dve.wait_ge(prod, n + 3)
                dve.wait_ge(stepped, n + 2)
                for way, c, cn in ((0, f, fn), (1, b, bn)):
                    for p in range(PAIRS_C):
                        for h in range(2):
                            half, at = slice(64 * h, 64 * h + 64), slice(h * SV, (h + 1) * SV)
                            state = lambda c: states[half, bass.ds(c, 1), way, p, at].rearrange("p o e -> p (o e)")
                            op = nc.vector.scalar_tensor_tensor(
                                out=state(cn), in0=state(c), scalar=dec[half, way, p, bass.ds(c, 1)],
                                in1=ps[half, 2 * u + way, p * PV + h * SV:p * PV + (h + 1) * SV],
                                op0=ALU.mult, op1=ALU.add)
                op.then_inc(stepped, 1)
            steps(dve, body)


def mlstm_outputs(k, l, s, cols, v1, states, with_ctx):
    nc, io, d, ps = k.nc, k.io, k.d, k.ps
    CHUNKS = NT if with_ctx else NTL
    with ExitStack() as st:
        sb = k.buffers(st)
        mask = sb("mask", [P, 2, P])
        kt = sb("kt", [P, 2, PAIRS_C, P])
        qt = sb("qt", [P, 2, PAIRS_C, P])
        qd = sb("qd", [P, 2, PAIRS_C, 2, P])
        ur = sb("ur", [P, 2, UNITS, P])
        gate = sb("gate", [P, 2, UNITS, P])
        mt = sb("mt", [P, UNITS, P])
        num = sb("num", [P, 2, UNITS, SV])
        den = sb("den", [P, 2, UNITS])
        both = sb("both", [P, 2, UNITS, HD])
        yt = sb("yt", [P, 2, C_HEADS * HD])
        block = st.enter_context(nc.Block())
        (m_ld, c_ld, y_st, cleared, logits, gated, scored, mixed, intra, inter, inter_free, chain, y_done) = (
            s[n] for n in ("m_ld", "c_ld", "y_st", "cleared2", "logits", "gated", "scored", "mixed", "intra", "inter",
                           "inter_free", "den_steps", "y_done"))
        LOADS = 5

        @block.sync
        def _(sp):
            sp.dma_start(mask[:], io["causal"]).then_inc(m_ld, 16)
            sp.wait_ge(cleared, 1)

            def load(c, u):
                span = bass.ds(c * P, P)
                pairs = lambda j: d["qkc"][j, :, span].rearrange("(c p) t -> p c t", p=P)
                sp.dma_start(ur[:, u, :, :], d["u"][:, span].partition_broadcast(P)).then_inc(c_ld[u], 16)
                sp.dma_start(kt[:, u, :, :], pairs(1)).then_inc(c_ld[u], 16)
                sp.dma_start(qt[:, u, :, :], pairs(0)).then_inc(c_ld[u], 16)
                for h in range(2):
                    half = slice(64 * h, 64 * h + 64)
                    sp.dma_start(qd[half, u, :, h, :], pairs(0)[half, :, :]).then_inc(c_ld[u], 16)

            def store(c, u):
                sp.wait_ge(y_done, c + (1 + 2))
                sp.dma_start(d["y"][bass.ds(c * P, P), 640:DM], yt[:, u, :]).then_inc(y_st[u], 16)
            for u in range(2):
                sp.sem_inc(y_st[u], 16)
                load(u, u)
            def load_next(c, u):
                sp.wait_ge(logits, c - 1)
                sp.wait_ge(inter, c - 1)
                load(c, u)
            load_next(2, 0)
            with sp.Fori(0, CHUNKS // 2 - 2) as i:
                for u in range(2):
                    load_next(2 * i + (3 + u), 1 - u)
                    store(2 * i + u, u)
            load_next(CHUNKS - 1, 1)
            for c in range(CHUNKS - 4, CHUNKS):
                store(c, c % 2)
            for u in range(2):
                sp.wait_ge(y_st[u], 16 + 16 * (CHUNKS // 2))

        def over_chunks(eng, first, body):
            first()
            with eng.Fori(0, CHUNKS // 2 - 1) as i:
                for u in range(2):
                    body(2 * i + u, u, i, True)
            body(CHUNKS - 2, 0, CHUNKS // 2 - 1, True)
            body(CHUNKS - 1, 1, CHUNKS // 2 - 1, False)

        @block.tensor
        def _(pe):
            def score(c, u, turn):
                pe.wait_ge(c_ld[u], 16 * LOADS * turn + 16 * LOADS)
                for p in range(PAIRS_C):
                    mm = nc.tensor.matmul(ps[:, p // 2, (p % 2) * 256:(p % 2) * 256 + 256], kt[:, u, p, :],
                                          qd[:, u, p, :, :].rearrange("p h t -> p (h t)"), start=True, stop=True)
                mm.then_inc(scored, 1)

            def incoming(c, u):
                for p in range(PAIRS_C):
                    mm = nc.tensor.matmul(ps[:, 4 + p, 0:2 * PV], qt[:, u, p, :],
                                          states[:, bass.ds(c, 1), :, p, :].rearrange("p o w e -> p (o w) e"),
                                          start=True, stop=True)
                mm.then_inc(inter, 1)

            def within(c, u):
                for way in range(2):
                    pe.wait_ge(mixed, 2 * c + (way + 5))
                    for h in range(C_HEADS):
                        mm = nc.tensor.matmul(ps[:, 2 + way, h * SV:(h + 1) * SV], mt[:, way * C_HEADS + h, :],
                                              v1[:, bass.ds(c, 1), h, :].rearrange("p o e -> p (o e)"), start=True, stop=True)
                mm.then_inc(intra, 1)

            def first():
                score(0, 0, 0)
                incoming(0, 0)
                within(0, 0)

            def body(c, u, i, more):
                if more:
                    score(c + 1, 1 - u, i + u)
                    pe.wait_ge(inter_free, 2 * c + 2)
                    incoming(c + 1, 1 - u)
                    within(c + 1, 1 - u)
            over_chunks(pe, first, body)

        @block.scalar
        def _(act):
            def one(c, u):
                act.wait_ge(logits, c + 1)
                for n in range(UNITS):
                    op = nc.scalar.activation(gate[:, u, n, :], gate[:, u, n, :], ACT.Exp,
                                              bias=cols[:, bass.ds(c, 1), KEY, n])
                op.then_inc(gated, 1)
            with act.Fori(0, CHUNKS // 2) as i:
                for u in range(2):
                    one(2 * i + u, u)

        @block.vector
        def _(dve):
            link = Chain(dve, chain)
            nc.vector.memset(qd[:], 0.0).then_inc(cleared, 1)
            def mix(c, u):
                dve.wait_ge(scored, c + 1)
                dve.wait_ge(gated, c + 1)
                for way in range(2):
                    span = slice(way * C_HEADS, (way + 1) * C_HEADS)
                    nc.vector.tensor_tensor(mt[:, span, :].rearrange("p n t -> p (n t)"),
                                            ps[:, 0:2, :].rearrange("p b t -> p (b t)")[:, 0:C_HEADS * P],
                                            gate[:, u, span, :].rearrange("p n t -> p (n t)"), ALU.mult).then_inc(mixed, 1)

            def finish(c, u):
                stat = lambda f, lo, hi: cols[:, bass.ds(c, 1), f, lo:hi].rearrange("p o n -> p (o n)")
                link.turn(5 * c)
                dve.wait_ge(inter, c + 1)
                dve.wait_ge(y_done, c + 1)
                for way in range(2):
                    lo = way * C_HEADS
                    nc.vector.tensor_tensor(
                        num[:, u, lo:lo + C_HEADS, :].rearrange("p (q h) e -> p q h e", h=2),
                        ps[:, 4:7, way * PV:(way + 1) * PV].rearrange("p q (h e) -> p q h e", h=2),
                        stat(INTER, lo, lo + C_HEADS).rearrange("p (q h) -> p q h", h=2).unsqueeze(3)
                        .to_broadcast([P, PAIRS_C, 2, SV]), ALU.mult).then_inc(inter_free, 1)
                dve.wait_ge(inter_free, 2 * c + 2)
                dve.wait_ge(intra, c + 1)
                link(nc.vector.tensor_tensor(num[:, u, :, :].rearrange("p (w h) e -> p w (h e)", w=2),
                                             num[:, u, :, :].rearrange("p (w h) e -> p w (h e)", w=2),
                                             ps[:, 2:4, 0:C_HEADS * SV], ALU.add))
                norm = num[:, u, :, HD:SV].rearrange("p n o -> p (n o)")
                link(nc.vector.scalar_tensor_tensor(out=den[:, u, :], in0=norm, scalar=-1.0, in1=norm,
                                                    op0=ALU.mult, op1=ALU.max))
                link(nc.vector.tensor_tensor(den[:, u, :], den[:, u, :], stat(FLOOR, 0, UNITS), ALU.max))
                link(nc.vector.reciprocal(den[:, u, :], den[:, u, :]))
                link(nc.vector.tensor_tensor(both[:, u, :, :], num[:, u, :, 0:HD],
                                             den[:, u, :].unsqueeze(2).to_broadcast([P, UNITS, HD]), ALU.mult))

            def first():
                mix(0, 0)

            def body(c, u, i, more):
                finish(c, u)
                if more:
                    mix(c + 1, 1 - u)
            over_chunks(dve, first, body)

        @block.gpsimd
        def _(pool):
            pool.sem_inc(y_done, 2)
            pool.sem_inc(mixed, 4)
            pool.wait_ge(m_ld, 16)

            def logit(c, u, turn):
                pool.wait_ge(c_ld[u], 16 * LOADS * turn + 16 * LOADS)
                pool.wait_ge(mixed, 2 * c + 2)
                nc.gpsimd.tensor_tensor(gate[:, u, :, :].rearrange("p (w h) t -> p w h t", w=2),
                                        ur[:, u, :, :].rearrange("p (w h) t -> p w h t", w=2),
                                        mask[:].unsqueeze(2).to_broadcast([P, 2, C_HEADS, P]), ALU.add).then_inc(logits, 1)

            def add(c, u, turn):
                pool.wait_ge(chain, 5 * c + 5)
                pool.wait_ge(y_st[u], 16 * turn + 16)
                nc.gpsimd.tensor_tensor(yt[:, u, :].rearrange("p (h e) -> p h e", e=HD), both[:, u, 0:C_HEADS, :],
                                        both[:, u, C_HEADS:, :], ALU.add).then_inc(y_done, 1)

            def first():
                logit(0, 0, 0)
                logit(1, 1, 0)

            def body(c, u, i, more):
                if not isinstance(c, int) or c + 2 < CHUNKS:
                    logit(c + 2, u, i + 1)
                add(c, u, i)
            over_chunks(pool, first, body)


def mlstm(k, l, s, with_ctx):
    with ExitStack() as st:
        sb = k.buffers(st)
        cols = sb("cols", [P, NT, 4, UNITS])
        v1 = sb("v1", [P, NT, C_HEADS, SV])
        knat = sb("knat", [P, NT, C_HEADS * HD])
        mlstm_gates(k, l, s, cols, knat, v1)
        states = sb("states", [P, NT, 2, PAIRS_C, PV])
        mlstm_states(k, l, s, cols, knat, v1, states)
        mlstm_outputs(k, l, s, cols, v1, states, with_ctx)


def window(k, l, s, with_ctx, ahead):
    nc, io, d, ps = k.nc, k.io, k.d, k.ps
    SCALE = HD ** -0.5
    NK = CTX + 3 * WIN
    BLOCKS = NT if with_ctx else NTL
    with ExitStack() as st:
        sb = k.buffers(st)
        masks = sb("masks", [P, 3, 3 * WIN])
        maskb = sb("maskb", [P, 3, 3 * WIN], BF16)
        identb = sb("identb", [P, P], BF16)
        kx, vx = sb("kx", [P, CTX]), sb("vx", [P, 2, P])
        sink, nsink = sb("sink", [P, A_HEADS]), sb("nsink", [P, A_HEADS])
        qt = sb("qt", [P, 2, A_HEADS, P])
        kw = sb("kw", [P, 2, 3 * WIN])
        vw = sb("vw", [P, 2, 3, P])
        pr = sb("pr", [P, A_HEADS, NK])
        pt = sb("pt", [P, 2, 5, 2 * P])
        mx, nm, sums, es, rs = (sb(n, [P, 2, A_HEADS]) for n in ("mx", "nm", "sums", "es", "rs"))
        ot = sb("ot", [P, 2 * P])
        yt = sb("yt", [P, 2, A_HEADS * HD])
        block = st.enter_context(nc.Block())
        c_ld, ld, v_ld, y_st, cleared, scored, maxed, chain, weighed, turned, ev_a, ev_d, summed, o_out, back, y_done = (
            s[n] for n in ("c_ld", "ld", "v_ld", "y_st", "cleared", "scored", "maxed", "chain", "weighed", "turned", "ev_a",
                           "ev_d", "summed", "o_out", "back", "y_done"))
        banks = lambda nk: {t: (4 + t // 2, (t % 2) * 256) for t in range(5)} if nk == 5 else {0: (4, 0), 1: (5, 0)}

        def blocks(eng, body, last):
            for u in range(2):
                body(u, u, 0, 5, 1 - (u == 0), u)
            with eng.Fori(1, NTL // 2 - 1) as i:
                for u in range(2):
                    body(2 * i + u, u, i, 5, 1, 2)
            for u in range(2):
                body(NTL - 2 + u, u, NTL // 2 - 1, 5, 1 + u, 2)
            if with_ctx:
                for u in range(2):
                    body(NTL + u, u, NTL // 2, 2, None, 2)
                last(NT, 2)
            else:
                last(NTL, 5)

        @block.sync
        def _(sp):
            sp.dma_start(masks[:], io["window"]).then_inc(c_ld, 16)
            sp.dma_start(kx[:], d["ka"][:, CTX0:CTX0 + CTX]).then_inc(c_ld, 16)
            sp.dma_start(vx[:], d["va"][CTX0:CTX0 + CTX, :].rearrange("(c p) v -> p c v", p=P)).then_inc(c_ld, 16)
            sp.dma_start(sink[:], io["attn_sink"][l, :].partition_broadcast(P)).then_inc(c_ld, 16)
            sp.wait_ge(cleared, 1)

            def load(n, u, local):
                for g in range(A_KV):
                    sp.dma_start(qt[64 * g:64 * g + 64, u, 2 * g:2 * g + 2, :],
                                 d["qa"][g, :, bass.ds(n * P, P)].rearrange("(h e) t -> e h t", e=HD)).then_inc(ld[u], 16)
                if local:
                    sp.dma_start(kw[:, u, :], d["ka"][:, bass.ds(n * P, 3 * WIN)]).then_inc(ld[u], 16)

            def load_v(n, u):
                sp.dma_start(vw[:, u, :, :], d["va"][bass.ds(n * P, 3 * WIN), :].rearrange("(c p) v -> p c v", p=P)
                             ).then_inc(v_ld[u], 16)

            def next_load(n, u, local):
                sp.wait_ge(scored, 4 * n - 4)
                load(n, u, local)

            def next_v(n, u):
                sp.wait_ge(summed, 2 * n)
                load_v(n, u)

            def store(n, u):
                sp.wait_ge(y_done, n + 2)
                sp.dma_start(d["y"][bass.ds(n * P, P), 0:A_HEADS * HD], yt[:, u, :]).then_inc(y_st[u], 16)
            for u in range(2):
                sp.sem_inc(y_st[u], 16)
                load(u, u, True)
                load_v(u, u)
            ahead(sp)
            next_load(2, 0, True)
            next_load(3, 1, True)
            next_v(2, 0)
            with sp.Fori(1, NTL // 2 - 1) as i:
                for u in range(2):
                    next_load(2 * i + (u + 2), u, True)
                    next_v(2 * i + (u + 1), 1 - u)
                    store(2 * i + (u - 2), u)
            for u in range(2):
                if with_ctx:
                    next_load(NTL + u, u, False)
                if u == 0:
                    next_v(NTL - 1, 1)
                store(NTL - 4 + u, u)
            for n in range(NTL - 2, BLOCKS):
                store(n, n % 2)
            for u in range(2):
                sp.wait_ge(y_st[u], 16 + 16 * (BLOCKS // 2))

        @block.tensor
        def _(pe):
            pe.sem_inc(summed, 2)
            pe.sem_inc(turned, 2)
            pe.wait_ge(maxed, 1)
            pe.wait_ge(c_ld, 64)

            def score(n, u, g, nk, mask):
                for h in (2 * g, 2 * g + 1):
                    q = qt[:, u, h, :]
                    b = 2 * (h % 2)
                    pe.wait_ge(weighed, 4 * n + (h + 1))
                    mm = nc.tensor.matmul(ps[:, b, 0:CTX], q, kx[:], start=True, stop=True)
                    if nk == 5:
                        for dst, w in ((ps[:, b, CTX:512], slice(0, 256)), (ps[:, b + 1, 0:P], slice(256, 384))):
                            nc.tensor.matmul(dst, q, kw[:, u, w], start=True, stop=False)
                            mm = nc.tensor.matmul(dst, identb[:], maskb[:, mask, w], start=False, stop=True)
                    mm.then_inc(scored, 1)

            def turn(n, g, nk, outputs=None, among=None):
                pe.wait_ge(weighed, 4 * n + (2 * g + 4))
                pe.wait_ge(ev_a, 2 * n + (g + 1))
                pe.wait_ge(ev_d, 2 * n + (g + 1))
                for t in range(nk):
                    bank, at = banks(nk)[t]
                    if t == 4 and outputs is not None:
                        pe.wait_ge(y_done, outputs)
                    if t == 4 and among:
                        among()
                    for h in range(2):
                        tr = nc.tensor.transpose(ps[:, bank, at + h * P:at + (h + 1) * P],
                                                 pr[:, 2 * g + h, t * P:(t + 1) * P], k.ident[:])
                tr.then_inc(turned, 1)
                if nk == 2 and among:
                    among()

            def values(n, u, g, nk, loaded):
                pe.wait_ge(ev_a, 2 * n + (g + 2))
                pe.wait_ge(ev_d, 2 * n + (g + 2))
                if g == 0:
                    pe.wait_ge(o_out, n + 1)
                    if nk == 5:
                        pe.wait_ge(v_ld[u], loaded)
                for t in range(nk):
                    v = vx[:, t, 64 * g:64 * g + 64] if t < 2 else vw[:, u, t - 2, 64 * g:64 * g + 64]
                    mm = nc.tensor.matmul(ps[64 * g:64 * g + 64, 7, 0:2 * P], v, pt[:, g, t, :],
                                          start=(t == 0), stop=(t == nk - 1))
                mm.then_inc(summed, 1)

            def turn_back(n):
                pe.wait_ge(y_done, n + 1)
                pe.wait_ge(o_out, n + 2)
                for h in range(2):
                    tr = nc.tensor.transpose(ps[:, 6, 256 + h * P:256 + (h + 1) * P], ot[:, h * P:(h + 1) * P], k.ident[:])
                tr.then_inc(back, 1)

            def body(n, u, i, nk, mask, before):
                pe.wait_ge(ld[u], 48 * i + (48 if nk == 5 else 32))
                pnk = 2 if (nk == 2 and u == 1) else 5
                score(n, u, 0, nk, mask)
                if before:
                    turn(n - 1, 1, pnk, None, (lambda: turn_back(n - 2)) if before == 2 else None)
                    values(n - 1, 1 - u, 0, pnk, 16 * i + 16 * u)
                score(n, u, 1, nk, mask)
                turn(n, 0, nk, n if before == 2 else None)
                if before:
                    values(n - 1, 1 - u, 1, pnk, None)

            def last(n, nk):
                turn(n - 1, 1, nk, None, lambda: turn_back(n - 2))
                values(n - 1, 1, 0, nk, 16 * (NTL // 2))
                values(n - 1, 1, 1, nk, None)
                turn_back(n - 1)
            blocks(pe, body, last)

        @block.scalar
        def _(act):
            act.sem_inc(ev_a, 1)
            act.sem_inc(weighed, 2)

            def weigh(n, u, h, nk):
                act.wait_ge(maxed, 4 * n + (h + 2))
                act.wait_ge(turned, 2 * n + (h // 2 + 1))
                width = NK if nk == 5 else CTX
                nc.scalar.activation(es[:, u, h:h + 1], sink[:, h:h + 1], ACT.Exp, bias=nm[:, u, h:h + 1])
                nc.scalar.activation(pr[:, h, 0:width], ps[:, 2 * (h % 2):2 * (h % 2) + 2, :].rearrange("p b t -> p (b t)")[:, 0:width],
                                     ACT.Exp, bias=nm[:, u, h:h + 1], scale=SCALE,
                                     accum_out=sums[:, u, h:h + 1]).then_inc(weighed, 1)

            def move(n, g, nk):
                act.wait_ge(turned, 2 * n + (g + 3))
                act.wait_ge(summed, 2 * n + (g + 1))
                if nk == 5:
                    nc.scalar.copy(pt[:, g, 4, :], ps[:, 6, 0:256])
                    nc.scalar.copy(pt[:, g, 0:2, :].rearrange("p t q -> p (t q)"), ps[:, 4, :]).then_inc(ev_a, 1)
                else:
                    nc.scalar.copy(pt[:, g, 0, :], ps[:, 4, 0:256]).then_inc(ev_a, 1)

            def body(n, u, i, nk, mask, before):
                weigh(n, u, 0, nk)
                weigh(n, u, 1, nk)
                if before:
                    move(n - 1, 1, 2 if (nk == 2 and u == 1) else 5)
                weigh(n, u, 2, nk)
                weigh(n, u, 3, nk)
                move(n, 0, nk)
            blocks(act, body, lambda n, nk: move(n - 1, 1, nk))

        @block.vector
        def _(dve):
            link = Chain(dve, chain)
            nc.vector.memset(qt[:], 0.0).then_inc(cleared, 1)
            dve.wait_ge(c_ld, 64)
            nc.vector.tensor_copy(maskb[:], masks[:])
            nc.vector.tensor_copy(identb[:], k.ident[:])
            nc.vector.tensor_scalar(nsink[:], sink[:], -1.0, None, ALU.mult).then_inc(maxed, 1)
            dve.wait_ge(maxed, 1)
            dve.sem_inc(ev_d, 1)
            for counter in (o_out, back, y_done):
                dve.sem_inc(counter, 1)

            def most(n, u, h, nk):
                dve.wait_ge(scored, 4 * n + (h + 1))
                width = NK if nk == 5 else CTX
                link(nc.vector.reduce_max(mx[:, u, h:h + 1], ps[:, 2 * (h % 2):2 * (h % 2) + 2, :].rearrange("p b t -> p (b t)")[:, 0:width], AX.X))
                nc.vector.tensor_scalar(nm[:, u, h:h + 1], mx[:, u, h:h + 1], -SCALE, nsink[:, h:h + 1],
                                        ALU.mult, ALU.min).then_inc(maxed, 1)

            def move(n, g, nk):
                dve.wait_ge(turned, 2 * n + (g + 3))
                dve.wait_ge(summed, 2 * n + (g + 1))
                if nk == 5:
                    nc.vector.tensor_copy(pt[:, g, 2:4, :].rearrange("p t q -> p (t q)"), ps[:, 5, :]).then_inc(ev_d, 1)
                else:
                    nc.vector.tensor_copy(pt[:, g, 1, :], ps[:, 5, 0:256]).then_inc(ev_d, 1)

            def take_sums(n):
                dve.wait_ge(summed, 2 * n + 4)
                dve.wait_ge(back, n + 1)
                nc.vector.tensor_copy(ot[:], ps[:, 7, 0:2 * P]).then_inc(o_out, 1)

            def factors(n, u):
                dve.wait_ge(weighed, 4 * n + 6)
                link(nc.vector.tensor_tensor(rs[:, u, :], sums[:, u, :], es[:, u, :], ALU.add))
                link(nc.vector.reciprocal(rs[:, u, :], rs[:, u, :]))

            def finish(n, u, stored, moves):
                dve.wait_ge(back, n + 2)
                dve.wait_ge(ev_a, moves)
                dve.wait_ge(y_st[u], stored)
                nc.vector.tensor_tensor(
                    yt[:, u, :].rearrange("p (g h e) -> p h g e", g=2, h=2),
                    ps[:, 6, 256:512].rearrange("p (h g e) -> p h g e", h=2, g=2),
                    rs[:, u, :].rearrange("p (g h) -> p h g", g=2).unsqueeze(3).to_broadcast([P, 2, 2, HD]),
                    ALU.mult).then_inc(y_done, 1)

            def body(n, u, i, nk, mask, before):
                link.turn(6 * n - 2 if before else 0)
                most(n, u, 0, nk)
                most(n, u, 1, nk)
                if before:
                    move(n - 1, 1, 2 if (nk == 2 and u == 1) else 5)
                    factors(n - 1, 1 - u)
                if before == 2:
                    finish(n - 2, u, 16 * i, 2 * n + 1)
                most(n, u, 2, nk)
                most(n, u, 3, nk)
                move(n, 0, nk)
                if before:
                    take_sums(n - 1)

            def last(n, nk):
                link.turn(6 * n - 2)
                move(n - 1, 1, nk)
                factors(n - 1, 1)
                finish(n - 2, 0, 16 * (BLOCKS // 2), 2 * n + 1)
                take_sums(n - 1)
                finish(n - 1, 1, 16 * (BLOCKS // 2), 2 * n + 1)
            blocks(dve, body, last)




UB = 4
GB = 2
GQ = GB * P
NG = SEQ // GQ
TURNS = SEQ // (UB * P)
VHALF = NT // 2
VALUE_PARTS = ((0, 5), (5, 9), (9, 14), (14, 18))
PIECES = ((0, 4), (4, 4), (8, 4), (12, 4), (16, 2))
MAX_PARTS = ((0, 512, (0,)), (512, 1536, (1, 2)), (1536, TOK, (3, 4)))
EXP_PARTS = ((0, 1024, (0, 1)), (1024, 1536, (2,)), (1536, TOK, (3, 4)))


def stack_loads(sp, sem, d, dst_q, dst_k, h, m, q_span, k_span):
    K = 2 * B_QK

    def rows(which, part, parts, span):
        x = d["qkb"][which, bass.ds(2 * h + m, 1), part:part + parts, :, span]
        return x.rearrange("o a r t -> (o a r) t")

    def twice(x):
        return x.unsqueeze(0).to_broadcast([2] + list(x.shape))
    q, kk = (lambda part, parts: rows(0, part, parts, q_span)), (lambda part, parts: rows(1, part, parts, k_span))
    sp.dma_start(dst_q(m, 0), twice(q(0, 2))).then_inc(sem, 16)
    sp.dma_start(dst_q(m, 1)[0:K], q(0, 2)).then_inc(sem, 16)
    sp.dma_start(dst_q(m, 1)[K:], twice(q(2, 1))).then_inc(sem, 16)
    sp.dma_start(dst_k(m, 0)[0:K], twice(kk(0, 1))).then_inc(sem, 16)
    sp.dma_start(dst_k(m, 0)[K:], twice(kk(1, 1))).then_inc(sem, 16)
    sp.dma_start(dst_k(m, 1)[0:K], twice(kk(2, 1))).then_inc(sem, 16)
    sp.dma_start(dst_k(m, 1)[K:], kk(0, 2)).then_inc(sem, 16)


STACK_LOADS = 14


def lambdas(k, l, s, nlam):
    nc, io = k.nc, k.io
    with ExitStack() as st:
        sb = k.buffers(st)
        lv, pv, e, li = sb("lv", [P, 4, B_QK]), sb("pv", [P, 2, B_QK]), sb("e", [P, 2]), sb("li", [P, 1])
        ld, steps, exps = s["lam_ld"], s["lam_steps"], s["lam_exps"]
        block = st.enter_context(nc.Block())

        @block.sync
        def _(sp):
            sp.dma_start(lv[:], io["diff_lambda"][l, :, :].partition_broadcast(P)).then_inc(ld, 16)
            sp.dma_start(li[:], io["lam_init"][l, 0:1].partition_broadcast(P)).then_inc(ld, 16)

        @block.vector
        def _(dve):
            link = Chain(dve, steps)
            dve.wait_ge(ld, 32)
            pairs = lv[:].rearrange("p (a b) e -> p a b e", b=2)
            link(nc.vector.tensor_tensor(pv[:], pairs[:, :, 0, :], pairs[:, :, 1, :], ALU.mult))
            link(nc.vector.reduce_sum(e[:], pv[:], AX.X))
            dve.wait_ge(exps, 1)
            link(nc.vector.tensor_tensor(e[:, 1:2], e[:, 1:2], e[:, 0:1], ALU.subtract))
            link(nc.vector.tensor_tensor(nlam[:], e[:, 1:2], li[:], ALU.subtract))

        @block.scalar
        def _(act):
            act.wait_ge(steps, 2)
            nc.scalar.activation(e[:], e[:], ACT.Exp).then_inc(exps, 1)


def differential(k, l, s, nlam):
    nc, io, d, ps = k.nc, k.io, k.d, k.ps
    MX, EX = len(MAX_PARTS), len(EXP_PARTS)
    with ExitStack() as st:
        sb = k.buffers(st)
        kst = sb("kst", [P, 2, 2, 2, TOK], BF16)
        qst = sb("qst", [P, 2, 2, 2, SEQ], BF16)
        vt = sb("vt", [P, NT, HD])
        pr = sb("pr", [P, 2, 2, TOK])
        pt = sb("pt", [P, 2, NT, GQ])
        mx = sb("mx", [P, 2, MX])
        nm, rl, ls = (sb(n, [P, 2, 2]) for n in ("nm", "rl", "ls"))
        sums = sb("sums", [P, 2, 2, len(EXP_PARTS)])
        cc = sb("cc", [P, 2, 1])
        recent = sb("recent", [P, 2 * UB])
        ot = sb("ot", [P, GQ])
        yt = sb("yt", [P, 2, GB, HD])
        block = st.enter_context(nc.Block())
        s_ld, v_ld, y_st = s["s_ld"], s["v_ld"], s["y_st"]
        v_ready, cleared, scored, maxed, chain, act_chain, weighed, mixed, turned, evac, half_summed, summed, o_out, back, y_done = (
            s[n] for n in ("v_ready", "cleared", "scored", "maxed", "chain", "act_chain", "weighed", "mixed", "turned",
                           "evac", "half_summed", "summed", "o_out", "back", "y_done"))
        STEPS, ACT_STEPS = 5 * UB, UB + 1
        MISSED, ACT_MISSED = 3, 2
        row = ps[:, 0:5, :].rearrange("p b t -> p (b t)")

        class Turn:
            def __init__(self, lead, tail=False):
                self.lead, self.tail = lead, tail
                self.blocks = range(UB + 1 if tail else UB)

            def block(self, at):
                return UB * self.lead + at >= 0 and (at < 0 or not self.tail)

            def group(self, at):
                return 2 * self.lead + at >= 0 and (at < 0 or not self.tail)

        def turns(eng, body):
            body(0, 0, 0, 0, Turn(0))
            body(0, 0, 1, 1, Turn(1))
            with eng.Fori(2, TURNS) as g:
                body(0, 0, g, g, Turn(2))
            with eng.Fori(0, TURNS) as g:
                body(1, 1, g, TURNS + g, Turn(2))
            with eng.Fori(1, B_HEADS // 2) as i:
                for u in range(2):
                    with eng.Fori(0, TURNS) as g:
                        body(2 * i + u, u, g, i * (2 * TURNS) + g + u * TURNS, Turn(2))
            body(None, None, None, TURNS * B_HEADS, Turn(2, True))

        @block.sync
        def _(sp):
            def stacks(h, hs):
                for m in range(2):
                    stack_loads(sp, s_ld, d, lambda m, a: qst[:, hs, m, a, :], lambda m, a: kst[:, hs, m, a, :],
                                h, m, slice(0, SEQ), slice(0, TOK))

            def values(h, half):
                t0 = half * VHALF
                sp.dma_start(vt[:, t0:t0 + VHALF, :], d["nat"][t0 * P:(t0 + VHALF) * P, bass.ds(h * HD + VB, HD)]
                             .rearrange("(c p) v -> p c v", p=P)).then_inc(v_ld[half], 16)

            def store(h, w, g, slot):
                sp.wait_ge(y_done, w + 1)
                sp.dma_start(d["y"][bass.ds(g * GQ, GQ), bass.ds(h * HD + 256, HD)].rearrange("(b p) e -> p b e", p=P),
                             yt[:, slot, :, :]).then_inc(y_st[slot], 16)

            for slot in range(2):
                sp.sem_inc(y_st[slot], 16)
                values(0, slot)
            stacks(0, 0)
            for half in range(2):
                sp.wait_ge(v_ld[half], 16)
                sp.sem_inc(v_ready[half], NG)
            sp.wait_ge(s_ld, 16 * STACK_LOADS)
            stacks(1, 1)

            for h in range(B_HEADS):
                more = h + 1 < B_HEADS
                with sp.Fori(0, NG // 2 - 1) as i:
                    for u in range(2):
                        store(h, 2 * i + (h * NG + u), 2 * i + u, u)
                if more:
                    sp.wait_ge(half_summed, NG * (h + 1))
                    values(h + 1, 0)
                store(h, h * NG + NG - 2, NG - 2, 0)
                if more:
                    sp.wait_ge(summed, NG * (h + 1))
                    values(h + 1, 1)
                    for half in range(2):
                        sp.wait_ge(v_ld[half], 16 * (h + 2))
                        sp.sem_inc(v_ready[half], NG)
                if h + 2 < B_HEADS:
                    sp.wait_ge(s_ld, 16 * STACK_LOADS * (h + 2))
                    stacks(h + 2, h % 2)
                store(h, h * NG + NG - 1, NG - 1, 1)
            for slot in range(2):
                sp.wait_ge(y_st[slot], 16 + 16 * NG * B_HEADS // 2)

        @block.tensor
        def _(pe):
            pe.wait_ge(cleared, 1)

            def score(n, hs, q0, m):
                for bank in range(5):
                    for e, (lo, hi, banks) in enumerate(EXP_PARTS):
                        if bank == banks[0]:
                            pe.wait_ge(weighed, 2 * EX * n + (EX * m + e + 1))
                    w = min(512, TOK - 512 * bank)
                    for a in range(2):
                        mm = nc.tensor.matmul(ps[:, bank, 0:w], qst[:, hs, m, a, bass.ds(q0, P)],
                                              kst[:, hs, m, a, 512 * bank:512 * bank + w], start=(a == 0), stop=(a == 1))
                    if any(bank == banks[-1] for _, _, banks in MAX_PARTS):
                        mm.then_inc(scored, 1)

            def turn(n, v, pieces):
                for j in pieces:
                    t0, nt = PIECES[j]
                    if j == 0:
                        pe.wait_ge(mixed, 2 * n + 1)
                    if j == 2:
                        pe.wait_ge(mixed, 2 * n + 2)
                    pe.wait_ge(evac, 5 * n + (j if j else 1))
                    for t in range(nt):
                        tr = nc.tensor.transpose(ps[:, 5 + j % 2, t * P:(t + 1) * P],
                                                 pr[:, v, 0, (t0 + t) * P:(t0 + t + 1) * P], k.ident[:])
                    tr.then_inc(turned, 1)

            def values(w, slot, part):
                if part == 0:
                    pe.wait_ge(v_ready[0], w + 1)
                    pe.wait_ge(evac, 10 * w + 8)
                    pe.wait_ge(o_out, w + 1)
                if part == 1:
                    pe.wait_ge(evac, 10 * w + 11)
                if part == 2:
                    pe.wait_ge(v_ready[1], w + 1)
                for t in range(*VALUE_PARTS[part]):
                    mm = nc.tensor.matmul(ps[0:HD, 7, 0:GQ], vt[:, t, :], pt[:, slot, t, :], start=(t == 0), stop=(t == NT - 1))
                if part == 1:
                    mm.then_inc(half_summed, 1)
                if part == 3:
                    mm.then_inc(summed, 1)

            def turn_back():
                for b in range(GB):
                    tr = nc.tensor.transpose(ps[:, 5, 256 + b * P:256 + (b + 1) * P], ot[:, b * P:(b + 1) * P], k.ident[:])
                tr.then_inc(back, 1)

            def body(h, hs, g, w, at):
                if not at.tail:
                    pe.wait_ge(s_ld, 16 * STACK_LOADS * h + 16 * STACK_LOADS)
                for b in at.blocks:
                    n, even, gr = UB * w + b, b % 2 == 0, b // 2
                    slot = gr % 2
                    if not at.tail:
                        score(n, hs, g * (UB * P) + b * P, 0)
                    out = even and at.group(gr - 3)
                    if at.block(b - 2):
                        turn(n - 2, b % 2, (2, 3))
                        pe.wait_ge(evac, 5 * (n - 2) + 4)
                    elif out:
                        pe.wait_ge(evac, 5 * UB * w + 1)
                        pe.wait_ge(y_done, 2 * w + (gr - 3))
                    if out:
                        pe.wait_ge(o_out, 2 * w + (gr - 3 + 2))
                        turn_back()
                    if at.block(b - 2):
                        turn(n - 2, b % 2, (4,))
                    if at.group(gr - 2):
                        values(2 * w + (gr - 2), slot, 1 if even else 3)
                    if not at.tail:
                        score(n, hs, g * (UB * P) + b * P, 1)
                    if at.block(b - 1):
                        if even and at.group(gr - 3):
                            pe.wait_ge(y_done, 2 * w + (gr - 3 + 1))
                        turn(n - 1, (b - 1) % 2, (0, 1))
                    if even and at.group(gr - 2):
                        values(2 * w + (gr - 2), slot, 2)
                    if not even and at.group(gr - 1):
                        values(2 * w + (gr - 1), 1 - slot, 0)
            turns(pe, body)

        @block.scalar
        def _(act):
            act.wait_ge(cleared, 1)
            act.sem_inc(weighed, EX)
            act.sem_inc(evac, 1)
            link = Chain(act, act_chain)

            def weigh(n, v, m, old):
                act.wait_ge(maxed, 2 * n + (m + 1))
                for e, (lo, hi, banks) in enumerate(EXP_PARTS):
                    if m == 0 and e == EX - 1 and old:
                        act.wait_ge(turned, 5 * (n - 2) + 5)
                    nc.scalar.activation(pr[:, v, m, lo:hi], row[:, lo:hi], ACT.Exp, bias=nm[:, v, m:m + 1],
                                         accum_out=sums[:, v, m, e:e + 1]).then_inc(weighed, 1)

            def move(n, at, j):
                t0, nt = PIECES[j]
                act.wait_ge(turned, 5 * n + (j + 1))
                nc.scalar.copy(pt[:, at // 2, t0:t0 + nt, (at % 2) * P:(at % 2 + 1) * P],
                               ps[:, 5 + j % 2, 0:nt * P].rearrange("p (t q) -> p t q", q=P)).then_inc(evac, 1)

            def finish(w, slot, stored, r):
                act.wait_ge(y_st[slot], stored)
                for b in range(GB):
                    op = nc.scalar.activation(yt[:, slot, b, :], ps[:, 5, 256 + b * P:256 + b * P + HD], ACT.Copy,
                                              scale=recent[:, r + b:r + b + 1])
                op.then_inc(y_done, 1)

            def body(h, hs, g, w, at):
                link.turn(w * ACT_STEPS - (ACT_MISSED if at.lead else 0))
                for b in at.blocks:
                    n, v, gr = UB * w + b, b % 2, b // 2
                    old, last = at.block(b - 2), at.block(b - 1)
                    if old:
                        move(n - 2, (b - 2) % UB, 2)
                    if not at.tail:
                        weigh(n, v, 0, old)
                    if old:
                        move(n - 2, (b - 2) % UB, 3)
                        move(n - 2, (b - 2) % UB, 4)
                    if b % 2 == 0 and at.group(gr - 3):
                        if at.tail and not old:
                            act.wait_ge(back, 2 * w + (gr - 3 + 2))
                        if b == 0:
                            finish(2 * w - 3, 1, 16 * w - 16, UB - 1)
                        elif b == 2:
                            finish(2 * w - 2, 0, 16 * w, 1)
                        else:
                            finish(2 * w - 1, 1, 16 * w, UB - 1)
                    if b == 0 and at.lead:
                        if at.group(-3):
                            act.wait_ge(y_done, 2 * w - 2)
                        link(nc.scalar.copy(recent[:, 0:UB], recent[:, UB:]))
                    if last:
                        if b % 2 == 1 and at.group(b // 2 - 2):
                            act.wait_ge(summed, 2 * w + (b // 2 - 1))
                        move(n - 1, (b - 1) % UB, 0)
                    if not at.tail:
                        weigh(n, v, 1, old)
                    if last:
                        move(n - 1, (b - 1) % UB, 1)
                        link(nc.scalar.copy(recent[:, UB + b:UB + b + 1], rl[:, 1 - v, 0:1]))
            turns(act, body)

        @block.vector
        def _(dve):
            link = Chain(dve, chain)
            for counter in (o_out, back):
                dve.sem_inc(counter, 1)
            nc.vector.memset(ot[:], 0.0)
            nc.vector.memset(recent[:], 1.0).then_inc(cleared, 1)

            def most(n, v, m):
                for j, (lo, hi, banks) in enumerate(MAX_PARTS):
                    dve.wait_ge(scored, 2 * MX * n + (MX * m + j + 1))
                    op = nc.vector.reduce_max(mx[:, m, j:j + 1], row[:, lo:hi], AX.X, negate=True)
                link(op)
                nc.vector.tensor_scalar(nm[:, v, m:m + 1], mx[:, m, 0:1], mx[:, m, 1:2], mx[:, m, 2:3],
                                        ALU.min, ALU.min).then_inc(maxed, 1)

            def factors(n, v):
                dve.wait_ge(weighed, 2 * EX * n + 3 * EX)
                link(nc.vector.reduce_sum(ls[:, v, :], sums[:, v, :, :], AX.X))
                link(nc.vector.reciprocal(rl[:, v, :], ls[:, v, :]))
                link(nc.vector.scalar_tensor_tensor(out=cc[:, v, :], in0=ls[:, v, 0:1], scalar=nlam[:], in1=rl[:, v, 1:2],
                                                    op0=ALU.mult, op1=ALU.mult))

            def mix(v, lo, hi):
                nc.vector.scalar_tensor_tensor(out=pr[:, v, 0, lo:hi], in0=pr[:, v, 1, lo:hi], scalar=cc[:, v, :],
                                               in1=pr[:, v, 0, lo:hi], op0=ALU.mult, op1=ALU.add).then_inc(mixed, 1)

            def take_sums(w):
                dve.wait_ge(summed, w + 1)
                dve.wait_ge(back, w + 1)
                nc.vector.tensor_copy(ot[0:HD, :], ps[0:HD, 7, 0:GQ]).then_inc(o_out, 1)

            def body(h, hs, g, w, at):
                link.turn(w * STEPS - (MISSED if at.lead else 0))
                for b in at.blocks:
                    n, v, gr = UB * w + b, b % 2, b // 2
                    if not at.tail:
                        most(n, v, 0)
                    if at.block(b - 1):
                        factors(n - 1, 1 - v)
                        mix(1 - v, 0, 1024)
                    if b % 2 == 1 and at.group(gr - 2):
                        take_sums(2 * w + (gr - 2))
                    if not at.tail:
                        most(n, v, 1)
                    if at.block(b - 1):
                        mix(1 - v, 1024, TOK)
                assert at.tail or link.n == STEPS - (0 if at.lead else MISSED)
            turns(dve, body)


def differential_context(k, l, s, nlam):
    nc, io, d, ps = k.nc, k.io, k.d, k.ps
    QB = CTX // P
    with ExitStack() as st:
        sb = k.buffers(st)
        kst = sb("kst", [P, 2, 2, 2, CTX], BF16)
        qst = sb("qst", [P, 2, 2, 2, CTX], BF16)
        vt = sb("vt", [P, 2, QB, HD])
        pr = sb("pr", [P, QB, 2, CTX])
        pt = sb("pt", [P, QB, CTX])
        nm, sums, rl = (sb(n, [P, QB, 2]) for n in ("nm", "sums", "rl"))
        cc = sb("cc", [P, QB, 1])
        ot = sb("ot", [P, CTX])
        yt = sb("yt", [P, QB, B_HEADS, HD])
        block = st.enter_context(nc.Block())
        s_ld, y_st, cleared, scored, chain, weighed, turned, summed, back = (
            s[n] for n in ("xs_ld", "xy_st", "x_cleared", "x_scored", "x_chain", "x_weighed", "x_turned", "x_summed", "x_back"))
        LOADS = STACK_LOADS + 1
        STEPS = 8
        ctx = slice(SEQ, TOK)

        def heads(eng, body):
            with eng.Fori(0, B_HEADS // 2) as i:
                for u in range(2):
                    body(2 * i + u, u, i)

        @block.sync
        def _(sp):
            def load(h, u):
                for m in range(2):
                    stack_loads(sp, s_ld[u], d, lambda m, a: qst[:, u, m, a, :], lambda m, a: kst[:, u, m, a, :], h, m, ctx, ctx)
                sp.dma_start(vt[:, u, :, :], d["nat"][SEQ:TOK, bass.ds(h * HD + VB, HD)].rearrange("(c p) v -> p c v", p=P)
                             ).then_inc(s_ld[u], 16)
            for u in range(2):
                load(u, u)
            with sp.Fori(0, B_HEADS // 2 - 1) as i:
                for u in range(2):
                    sp.wait_ge(summed, 2 * i + (u + 1))
                    load(2 * i + (u + 2), u)
            sp.wait_ge(chain, STEPS * B_HEADS)
            sp.dma_start(d["y"][ctx, 256:640].rearrange("(b p) e -> p b e", p=P),
                         yt[:].rearrange("p b h e -> p b (h e)")).then_inc(y_st, 16)
            sp.wait_ge(y_st, 16)

        @block.tensor
        def _(pe):
            pe.wait_ge(cleared, 1)

            def body(h, u, i):
                pe.wait_ge(s_ld[u], 16 * LOADS * i + 16 * LOADS)
                for b in range(QB):
                    for m in range(2):
                        for a in range(2):
                            mm = nc.tensor.matmul(ps[:, b, m * CTX:(m + 1) * CTX], qst[:, u, m, a, b * P:(b + 1) * P],
                                                  kst[:, u, m, a, :], start=(a == 0), stop=(a == 1))
                mm.then_inc(scored, 1)
                pe.wait_ge(chain, STEPS * h + 5)
                for t in range(QB):
                    for b in range(QB):
                        tr = nc.tensor.transpose(ps[:, 2, (2 * t + b) * P:(2 * t + b + 1) * P],
                                                 pr[:, b, 0, t * P:(t + 1) * P], k.ident[:])
                tr.then_inc(turned, 1)
                pe.wait_ge(chain, STEPS * h + 6)
                for t in range(QB):
                    mm = nc.tensor.matmul(ps[0:HD, 3, 0:CTX], vt[:, u, t, :], pt[:, t, :], start=(t == 0), stop=(t == QB - 1))
                mm.then_inc(summed, 1)
                pe.wait_ge(chain, STEPS * h + 7)
                for b in range(QB):
                    tr = nc.tensor.transpose(ps[:, 4, b * P:(b + 1) * P], ot[:, b * P:(b + 1) * P], k.ident[:])
                tr.then_inc(back, 1)
            heads(pe, body)

        @block.scalar
        def _(act):
            def body(h, u, i):
                act.wait_ge(chain, STEPS * h + 1)
                for b in range(QB):
                    for m in range(2):
                        nc.scalar.activation(pr[:, b, m, :], ps[:, b, m * CTX:(m + 1) * CTX], ACT.Exp,
                                             bias=nm[:, b, m:m + 1],
                                             accum_out=sums[:, b, m:m + 1]).then_inc(weighed, 1)
            heads(act, body)

        @block.vector
        def _(dve):
            link = Chain(dve, chain)
            nc.vector.memset(ot[:], 0.0).then_inc(cleared, 1)

            def body(h, u, i):
                link.turn(STEPS * h)
                dve.wait_ge(scored, h + 1)
                link(nc.vector.reduce_max(nm[:], ps[:, 0:QB, :].rearrange("p b (m t) -> p b m t", m=2), AX.X, negate=True))
                dve.wait_ge(weighed, 4 * h + 4)
                link(nc.vector.reciprocal(rl[:], sums[:]))
                for b in range(QB):
                    op = nc.vector.scalar_tensor_tensor(out=cc[:, b, :], in0=sums[:, b, 0:1], scalar=nlam[:],
                                                        in1=rl[:, b, 1:2], op0=ALU.mult, op1=ALU.mult)
                link(op)
                for b in range(QB):
                    link(nc.vector.scalar_tensor_tensor(out=pr[:, b, 0, :], in0=pr[:, b, 1, :], scalar=cc[:, b, :],
                                                        in1=pr[:, b, 0, :], op0=ALU.mult, op1=ALU.add))
                dve.wait_ge(turned, h + 1)
                link(nc.vector.tensor_copy(pt[:].rearrange("p t q -> p (t q)"), ps[:, 2, :]))
                dve.wait_ge(summed, h + 1)
                link(nc.vector.tensor_copy(ot[0:HD, :], ps[0:HD, 3, 0:CTX]))
                dve.wait_ge(back, h + 1)
                link(nc.vector.tensor_tensor(yt[:, :, bass.ds(h, 1), :].rearrange("p b o e -> p b (o e)"),
                                             ps[:, 4, 0:CTX].rearrange("p (b t) -> p b t", b=QB)[:, :, 0:HD],
                                             rl[:, :, 0:1].to_broadcast([P, QB, HD]), ALU.mult))
                assert link.n == STEPS
            heads(dve, body)


def output_weights(k, stack):
    sb = k.buffers(stack)
    return {"wo": sb("wo", [P, KT, DM]), "gn": sb("gn", [P, B_HEADS + C_HEADS, HD]), "keep": sb("keep", [P, 1]),
            "gate": sb("gate", [P, 2, DM]), "lng": sb("lng", [P, DM]), "lnb": sb("lnb", [P, DM])}


def load_output_weights(k, l, sp, weights, w_ld):
    io, d = k.io, k.d
    wo, gn, keep, gate, lng, lnb = (weights[n] for n in ("wo", "gn", "keep", "gate", "lng", "lnb"))
    for h in range(B_HEADS):
        sp.dma_start(gn[:, h, :], io["diff_norm_g"][l, :].partition_broadcast(P)).then_inc(w_ld, 16)
    sp.dma_start(gn[:, B_HEADS:, :].rearrange("p h e -> p (h e)"), io["mlstm_norm_g"][l, :].partition_broadcast(P)).then_inc(w_ld, 16)
    sp.dma_start(keep[:], io["lam_keep"][l, 0:1].partition_broadcast(P)).then_inc(w_ld, 16)
    for r in range(2):
        sp.dma_start(gate[:, r, :], d["mod"][r, 2 * DM:].partition_broadcast(P)).then_inc(w_ld, 16)
    sp.dma_start(lng[:], io["ln_g"][l, :].partition_broadcast(P)).then_inc(w_ld, 16)
    sp.dma_start(lnb[:], io["ln_b"][l, :].partition_broadcast(P)).then_inc(w_ld, 16)
    sp.dma_start(wo[:], io["w_out"][l, :, :, :]).then_inc(w_ld, 16)


def output(k, l, s, weights, w_ld, with_ctx):
    nc, io, d, ps = k.nc, k.io, k.d, k.ps
    NH = B_HEADS + C_HEADS
    A = A_HEADS * HD
    W = 512
    with ExitStack() as st:
        sb = k.buffers(st)
        wo, gn, keep, gate, lng, lnb = (weights[n] for n in ("wo", "gn", "keep", "gate", "lng", "lnb"))
        xt, yt, gt = (sb(n, [P, 2, DM]) for n in ("xt", "yt", "gt"))
        sq = sb("sq", [P, 2, NH, HD])
        ss, sr, rr = (sb(n, [P, 2, NH]) for n in ("ss", "sr", "rr"))
        yT = sb("yT", [P, 2, KT, P])
        res = sb("res", [P, 2, DM])
        ot = sb("ot", [P, 2, DM])
        bn = sb("bn", [P, 2, 2, 6])
        mv, sd = sb("mv", [P, 2, 2]), sb("sd", [P, 2, 2])
        block = st.enter_context(nc.Block())
        ld, x_ld, o_st, squared, steps, roots, ready, turned, moved, prod, taken, centred, done = (
            s[n] for n in ("ld", "x_ld", "o_st", "squared", "steps", "roots", "ready", "turned", "moved",
                           "prod", "taken", "centred", "done"))
        N = NT if with_ctx else NTL
        PRE, POST = 4, 5

        def tiles(eng, first, body):
            first()
            with eng.Fori(0, NTL // 2 - 1) as i:
                for u in range(2):
                    body(2 * i + u, u, i, 0, True)
            for u in range(2):
                body(NTL - 2 + u, u, NTL // 2 - 1, 0, u == 0 or with_ctx)
            if with_ctx:
                for u in range(2):
                    body(NTL + u, u, NTL // 2, 1, u == 0)

        @block.sync
        def _(sp):
            def load_x(t, u):
                sp.dma_start(xt[:, u, :], d["x"][bass.ds(t * P, P), :]).then_inc(x_ld[u], 16)

            def load(t, u):
                rows = bass.ds(t * P, P)
                sp.dma_start(yt[:, u, :], d["y"][rows, :]).then_inc(ld[u], 16)
                for lo, hi, src in ((0, A, SA), (A, A + 384, SB), (A + 384, DM, SC)):
                    sp.dma_start(gt[:, u, lo:hi], d["nat"][rows, src:src + hi - lo]).then_inc(ld[u], 16)

            target = d["x"] if with_ctx else k.out

            def store(t, u):
                sp.wait_ge(done, t + 3)
                sp.dma_start(target[bass.ds(t * P, P), :], ot[:, u, :]).then_inc(o_st[u], 16)
            for u in range(2):
                sp.sem_inc(o_st[u], 16)
                load(u, u)
                load_x(u, u)
            def next_y(t, u):
                sp.wait_ge(turned, t)
                load(t, u)

            def next_x(t, u):
                sp.wait_ge(s["varied"], t - 1)
                load_x(t, u)
            next_y(2, 0)
            next_y(3, 1)
            next_x(2, 0)
            with sp.Fori(0, N // 2 - 2) as i:
                for u in range(2):
                    next_y(2 * i + (4 + u), u)
                    next_x(2 * i + (3 + u), 1 - u)
                    store(2 * i + u, u)
            next_x(N - 1, 1)
            for t in range(N - 4, N):
                store(t, t % 2)
            for u in range(2):
                sp.wait_ge(o_st[u], 16 + 16 * (N // 2))

        @block.tensor
        def _(pe):
            pe.sem_inc(turned, 1)

            def turn(t, u):
                pe.wait_ge(ready, t + 1)
                pe.wait_ge(moved, t + 1)
                for j in range(KT):
                    tr = nc.tensor.transpose(ps[:, j // 4, (j % 4) * P:(j % 4 + 1) * P], yt[:, u, j * P:(j + 1) * P], k.ident[:])
                tr.then_inc(turned, 1)

            def product(t, u, more):
                pe.wait_ge(moved, t + 2)
                pe.wait_ge(taken, t + 1)
                for n in range(DM // W):
                    for j in range(KT):
                        if more and (n, j) == (1, KT // 2):
                            turn(t + 1, 1 - u)
                        mm = nc.tensor.matmul(ps[:, 2 + 2 * u + n, :], yT[:, u, j, :], wo[:, j, n * W:(n + 1) * W],
                                              start=(j == 0), stop=(j == KT - 1))
                mm.then_inc(prod, 1)

            def first():
                turn(0, 0)
                pe.wait_ge(w_ld, 16 * (B_HEADS + 7))

            def body(t, u, i, r, more):
                product(t, u, more)
            tiles(pe, first, body)

        @block.gpsimd
        def _(pool):
            pool.sem_inc(done, 2)
            pool.sem_inc(s["scaled"], 2)

            def after(t, u, i):
                pool.wait_ge(centred, t + 1)
                pool.wait_ge(o_st[u], 16 * i + 16)
                nc.gpsimd.tensor_tensor(ot[:, u, :], res[:, u, :], lng[:], ALU.mult).then_inc(s["scaled"], 1)
                pool.wait_ge(s["scaled"], t + 3)
                nc.gpsimd.tensor_tensor(ot[:, u, :], ot[:, u, :], lnb[:], ALU.add).then_inc(done, 1)

            tiles(pool, lambda: None, lambda t, u, i, r, more: after(t, u, i))

        @block.scalar
        def _(act):
            act.sem_inc(moved, 1)

            def before(t, u, i):
                act.wait_ge(ld[u], 64 * i + 64)
                nc.scalar.square(sq[:, u, :, :], yt[:, u, A:].rearrange("p (h e) -> p h e", e=HD)).then_inc(squared, 1)
                act.wait_ge(s["summed"], t + 1)
                nc.scalar.sqrt(sr[:, u, :], ss[:, u, :]).then_inc(roots, 1)
                act.wait_ge(turned, t + 2)
                for n in range(2):
                    op = nc.scalar.copy(yT[:, u, 4 * n:4 * n + 4, :].rearrange("p k t -> p (k t)"), ps[:, n, :])
                op.then_inc(moved, 1)

            def after(t, u):
                act.wait_ge(s["varied"], t + 1)
                nc.scalar.sqrt(sd[:, u, 0:1], mv[:, u, 1:2]).then_inc(s["rooted"], 1)

            def body(t, u, i, r, more):
                if more:
                    before(t + 1, 1 - u, i + u)
                after(t, u)
            tiles(act, lambda: before(0, 0, 0), body)

        @block.vector
        def _(dve):
            dve.sem_inc(taken, 2)
            dve.wait_ge(w_ld, 16 * (B_HEADS + 7))
            gb = gn[:, 0:B_HEADS, :]
            nc.vector.tensor_scalar(gb, gb, keep[:], None, ALU.mult).then_inc(s["gn_ready"], 1)
            dve.wait_ge(s["gn_ready"], 1)
            link = Chain(dve, steps)

            def before(t, u, i):
                dve.wait_ge(squared, t + 1)
                link(nc.vector.reduce_sum(ss[:, u, :], sq[:, u, :, :], AX.X))
                nc.vector.tensor_scalar(ss[:, u, :], ss[:, u, :], 1.0 / HD, EPS, ALU.mult, ALU.add).then_inc(s["summed"], 1)
                dve.wait_ge(roots, t + 1)
                link(nc.vector.reciprocal(rr[:, u, :], sr[:, u, :]))
                y = yt[:, u, A:].rearrange("p (h e) -> p h e", e=HD)
                link(nc.vector.tensor_tensor(y, y, rr[:, u, :].unsqueeze(2).to_broadcast([P, NH, HD]), ALU.mult))
                link(nc.vector.tensor_tensor(y, y, gn[:], ALU.mult))
                nc.vector.tensor_tensor(yt[:, u, :], yt[:, u, :], gt[:, u, :], ALU.mult).then_inc(ready, 1)

            def after(t, u, i, r):
                dve.wait_ge(prod, t + 1)
                dve.wait_ge(x_ld[u], 16 * i + 16)
                dve.wait_ge(s["scaled"], t + 1)
                link(nc.vector.tensor_tensor(res[:, u, :], ps[:, 2 + 2 * u:4 + 2 * u, :].rearrange("p n w -> p (n w)"),
                                             gate[:, r, :], ALU.mult))
                dve.sem_inc(taken, 1)
                link(nc.vector.scalar_tensor_tensor(out=res[:, u, :], in0=xt[:, u, :], scalar=ALPHA, in1=res[:, u, :],
                                                    op0=ALU.mult, op1=ALU.add))
                for n in range(2):
                    op = nc.vector.bn_stats(bn[:, u, n, :], res[:, u, n * W:(n + 1) * W])
                link(op)
                nc.vector.memset(sd[:, u, 1:2], 0.0)
                link(nc.vector.bn_aggr(mv[:, u, :], bn[:, u, :, :].rearrange("p n s -> p (n s)")))
                nc.vector.tensor_scalar(mv[:, u, 1:2], mv[:, u, 1:2], EPS, None, ALU.add).then_inc(s["varied"], 1)
                dve.wait_ge(s["rooted"], t + 1)
                link(nc.vector.reciprocal(sd[:, u, 1:2], sd[:, u, 0:1]))
                nc.vector.tensor_scalar(res[:, u, :], res[:, u, :], mv[:, u, 0:1], sd[:, u, 1:2],
                                        ALU.subtract, ALU.mult).then_inc(centred, 1)

            def first():
                before(0, 0, 0)
                assert link.n == PRE

            def body(t, u, i, r, more):
                link.turn(PRE + (PRE + POST) * t if more else PRE * N + POST * (N - 1))
                if more:
                    before(t + 1, 1 - u, i + u)
                after(t, u, i, r)
                assert link.n == POST + (PRE if more else 0)
            tiles(dve, first, body)



def later_stages(k, l, with_ctx, stages):
    on = lambda name: stages is None or name in stages
    if on("b"):
        with ExitStack() as st:
            nlam = k.buffers(st)("nlam", [P, 1])
            s = k.semaphores(st, "diff", (
                "lam_ld", "lam_steps", "lam_exps", "s_ld", "cleared", "scored", "maxed",
                "chain", "act_chain", "weighed", "mixed", "turned", "evac", "half_summed", "summed", "o_out", "back",
                "y_done", "xy_st", "x_cleared", "x_scored", "x_chain", "x_weighed", "x_turned", "x_summed", "x_back"),
                {"v_ready": 2, "v_ld": 2, "y_st": 2, "xs_ld": 2})
            lambdas(k, l, s, nlam)
            differential(k, l, s, nlam)
            if with_ctx:
                differential_context(k, l, s, nlam)
    if on("c"):
        with ExitStack() as st:
            mlstm(k, l, k.semaphores(st, "mlstm", (
                "cleared", "g_ld", "v_ld", "gate_steps", "gate_exps", "row_st", "staged", "turned", "kept", "k_turned", "k_kept",
                "d_ld", "weighed", "prod", "stepped", "m_ld", "cleared2", "cleared3", "logits", "gated", "scored", "mixed",
                "intra", "inter", "inter_free", "den_steps", "y_done"), {"k_ld": 2, "c_ld": 2, "y_st": 2}), with_ctx)
    with ExitStack() as both:
        w_ld = k.semaphores(both, "out_weights", ("w_ld",))["w_ld"]
        weights = output_weights(k, both)
        if on("a"):
            with ExitStack() as st:
                window(k, l, k.semaphores(st, "window", (
                    "c_ld", "cleared", "scored", "maxed", "chain", "weighed", "turned", "ev_a", "ev_d", "summed", "o_out",
                    "back", "y_done"), {"ld": 2, "v_ld": 2, "y_st": 2}), with_ctx,
                    lambda sp: load_output_weights(k, l, sp, weights, w_ld))
        if on("o"):
            with ExitStack() as st:
                output(k, l, k.semaphores(st, "out", (
                    "squared", "steps", "roots", "ready", "turned", "moved", "prod", "taken", "centred",
                    "done", "scaled", "gn_ready", "summed", "varied", "rooted"), {"ld": 2, "x_ld": 2, "o_st": 2}),
                    weights, w_ld, with_ctx)


def more_constants():
    keep = np.ones((64, TOK), np.float32)
    keep[0:32, 0::P] = 0.0
    keep[32:64, P - 1::P] = 0.0
    t = np.arange(P)
    causal = np.stack([np.where(t[:, None] <= t[None], 0.0, NEG), np.where(t[:, None] >= t[None], 0.0, NEG)], 1)
    q, j = np.arange(P)[:, None], np.arange(3 * WIN)[None]
    near = np.abs(j - WIN - q) <= WIN
    window = np.stack([near & (j >= WIN), near, near & (j < 2 * WIN)], 1)
    lam = np.array([[0.8 - 0.6 * np.exp(-0.3 * n)] for n in range(DEPTH)])
    return {"lam_init": lam.astype(np.float32), "lam_keep": (1.0 - lam).astype(np.float32),
            "window": np.where(window, 0.0, NEG).astype(np.float32), "keep": keep, "causal": causal.astype(np.float32)}


def setup(k):
    nc, io, d = k.nc, k.io, k.d
    with ExitStack() as st:
        sb = k.buffers(st)
        zero = k.zero
        cols = sb("cond", [P, KT, 2])
        c_ld, i_ld, silu = k.semaphores(st, "setup", ("cond_ld", "ident_ld", "silu")).values()
        x_cp, z_st = k.copied["x_copied"], k.copied["pad_st"]
        block = st.enter_context(nc.Block())

        @block.sync
        def _(sp):
            sp.dma_start(k.ident[:], io["ident"]).then_inc(i_ld, 16)
            for r in range(2):
                sp.dma_start(cols[:, :, r], io["cond"][r, :].rearrange("(k p) -> p k", p=P),
                             allow_slow_non_contiguous=True).then_inc(c_ld, 16)
            sp.dma_start(d["x"][0:SEQ, :], io["x"]).then_inc(x_cp, 16)
            sp.dma_start(d["x"][SEQ:TOK, :], io["ctx"]).then_inc(x_cp, 16)
            sp.wait_ge(k.copied["cleared"], 1)
            for row in (0, CTX0 - WIN):
                sp.dma_start(d["va"][row:row + WIN, :], zero[:]).then_inc(z_st, 16)
                sp.dma_start(d["ka"][:, row:row + WIN], zero[:]).then_inc(z_st, 16)
            sp.wait_ge(i_ld, 16)

        @block.vector
        def _(dve):
            nc.vector.memset(zero[:], 0.0).then_inc(k.copied["cleared"], 1)

        @block.scalar
        def _(act):
            act.wait_ge(c_ld, 32)
            nc.scalar.activation(k.silu_c[:], cols[:], ACT.Silu).then_inc(silu, 1)
            act.wait_ge(silu, 1)


def layer(k, l, with_ctx, stages):
    d = k.d
    with ExitStack() as st:
        modulation(k, l, k.semaphores(st, "mod", ("b_ld", "done", "added", "stored", "cols_ld"), {"w_ld": 3}))
    with ExitStack() as wide:
        hT = k.buffers(wide)("hT", [P, KT, TOK])
        with ExitStack() as st:
            natural_project(k, l, hT, k.semaphores(
                st, "nat", ("turned", "h_ready", "kept", "prod", "evac", "v_free", "z_free", "n_ready",
                      "values_ready"),
                {"w_ld": NCH, "x_ld": 2, "n_st": 2}), with_ctx)
        latent_row = lambda t0: LAT0 + t0 if t0 < SEQ else CTX0
        ta = lambda i, u, b, t0, w, ob: [(d["qa"][u, :, t0:t0 + w], ob[:, 0, :])]
        tk = lambda i, u, b, t0, w, ob: [(d["ka"][:, latent_row(t0):latent_row(t0) + w], ob[:, 0, :])] if u == 0 else \
            [(d["gates"][:, t0:t0 + w], ob[:, 0, :])]
        tb = lambda i, u, b, t0, w, ob: [
            (d["qkb"][u, bass.ds(4 * i, 4), part, :, t0:t0 + w], ob[:, part, :]) for part in range(3)]
        tc = lambda i, u, b, t0, w, ob: [(d["qkc"][u, bass.ds(i * P, P), t0:t0 + w], ob[:, 0, :])]
        for kinds, first, pairs, out_of in ((("rope_a", "rope_a"), 0, 1, ta), (("rope_a", 1.0), 2, 1, tk),
                                            (("rope_b", "rope_b"), 4, 3, tb), ((HD ** -0.5, 1.0), 10, 3, tc)):
            with ExitStack() as st:
                transposed_project(k, l, hT, k.semaphores(
                    st, "tr", ("tab_ld", "prod", "evac", "rot", "rot_free", "done", "chain"),
                    {"w_ld": 2, "o_st": 2}), kinds, first, pairs, out_of)
    later_stages(k, l, with_ctx, stages)


def program(nc, io, out, d, stages):
    with ExitStack() as stack:
        k = Core(nc, stack, io, d)
        k.out = out
        k.ps = stack.enter_context(nc.psum_tensor("ps", [P, 8, 512], F32))
        k.ident = stack.enter_context(nc.sbuf_tensor("ident_sb", [P, P], F32))
        k.silu_c = stack.enter_context(nc.sbuf_tensor("silu_c", [P, KT, 2], F32))
        k.modc = stack.enter_context(nc.sbuf_tensor("modc", [P, 2, 2, KT], F32))
        k.zero = stack.enter_context(nc.sbuf_tensor("zero", [P, A_KV * HD], F32))
        k.copied = k.semaphores(stack, "setup", ("x_copied", "pad_st", "cleared"))
        setup(k)
        if DEPTH > 1:
            with nc.Fori(0, DEPTH - 1) as l:
                layer(k, l, True, stages)
        if stages is None or "2" in stages:
            layer(k, DEPTH - 1, False, stages)


def constants():
    def tables(dim):
        nf = dim // 4
        inv = (np.float32(10000.0) ** (-np.arange(nf, dtype=np.float32) / nf)).astype(np.float32)
        tok = np.arange(SEQ)
        ar = (tok // GRID_W).astype(np.float32)[:, None] * inv
        ac = (tok % GRID_W).astype(np.float32)[:, None] * inv
        ang = np.concatenate([ar, ar, ac, ac], -1).T
        both = np.stack([np.cos(ang.astype(np.float64)), np.sin(ang.astype(np.float64))], 1).astype(np.float32)
        return np.tile(both, (P // dim, 1, 1))

    def rotation(dim):
        m = np.zeros((P, P), np.float32)
        q = dim // 4
        for j in range(P):
            if (j % dim) // q % 2 == 0:
                m[j + q, j] = -1.0
            else:
                m[j - q, j] = 1.0
        return m
    c = {"rope": np.stack([tables(HD), tables(B_QK)]), "perm": np.stack([rotation(HD), rotation(B_QK)]),
         "ident": np.eye(P, dtype=np.float32)}
    c.update(more_constants())
    return c


def lay_out(inputs):
    f = {n: np.asarray(a) for n, a in inputs.items()}
    w = f["w_in"]
    at = np.cumsum([0, 256, 128, 128, 256, 384, 384, 384, 384, 384, 384, 384, 384, 384, 24])
    qa, ka, va, za, qb, kb, vb, zb, qm, km, vm, om, zm, gm = (w[:, :, at[n]:at[n + 1]] for n in range(14))
    nat = np.concatenate([va, za, vb, zb, vm, om, zm], 2).reshape(DEPTH, KT, P, NCH, CW).transpose(0, 3, 2, 1, 4)
    gate = np.zeros((DEPTH, DM, P), w.dtype)
    for n, kind in enumerate((0, 2, 1, 3)):
        gate[:, :, 32 * n:32 * n + C_HEADS] = gm[:, :, C_HEADS * kind:C_HEADS * (kind + 1)]
    third = lambda a, n: a[:, :, n * P:(n + 1) * P]
    tiles = [third(qa, 0), third(qa, 1), ka, gate]
    for q, kk in ((qb, kb), (qm, km)):
        for n in range(3):
            tiles += [third(q, n), third(kk, n)]
    tr = np.stack(tiles, 1).reshape(DEPTH, TILES, KT, P, P).transpose(0, 1, 3, 2, 4)
    a = {"x": f["x"][0], "ctx": f["ctx"][0], "cond": np.concatenate([f["c"], f["c_ctx"][None]], 0),
         "w_mod": f["w_mod"], "b_mod": f["b_mod"], "w_nat": nat, "w_tr": tr}
    a["w_out"] = f["w_out"].reshape(DEPTH, KT, P, DM).transpose(0, 2, 1, 3)
    for n in ("attn_sink", "diff_lambda", "diff_norm_g", "mlstm_norm_g", "ln_g", "ln_b"):
        a[n] = f[n]
    a["i_bias"], a["f_bias"] = f["mlstm_i_bias"], f["mlstm_f_bias"]
    a.update(constants())
    return {n: np.ascontiguousarray(v) for n, v in a.items()}


SCRATCH = {"x": ([TOK, DM], F32), "mod": ([2, 3 * DM], F32), "nat": ([TOK, NW], F32), "va": ([PADTOK, P], F32),
           "qa": ([2, P, TOK], F32), "ka": ([P, PADTOK], F32), "gates": ([P, TOK], F32),
           "qkb": ([2, 2 * B_HEADS, 3, B_QK, TOK], BF16), "qkc": ([2, 3 * P, TOK], F32),
           "u": ([12, TOK], F32), "decay": ([12, NT], F32), "y": ([TOK, DM], F32)}


def kernel(**inputs):
    import concourse.bacc as bacc
    from concourse.bass_utils import run_bass_kernel_spmd

    nc = bacc.Bacc("TRN2", target_bir_lowering=False, num_devices=1)
    arrays = lay_out(inputs)
    io = {n: nc.dram_tensor(f"in_{n}", a.shape, mybir.dt.from_np(a.dtype), kind="ExternalInput").ap() for n, a in arrays.items()}
    out = nc.dram_tensor("out_0", (SEQ, DM), F32, kind="ExternalOutput").ap()
    scratch = {n: nc.dram_tensor(f"work_{n}", s, t, kind="Internal").ap() for n, (s, t) in SCRATCH.items()}
    program(nc, io, out, scratch, None)
    result = run_bass_kernel_spmd(nc, [{f"in_{n}": a for n, a in arrays.items()}], core_ids=[0])
    return result.results[0]["out_0"].reshape(1, SEQ, DM)
```
